# Optimizing a Trainium2 kernel written in Bass

```python
import jax, jax.numpy as jnp
from jax import lax
import numpy as np

D_MODEL = 1024
BATCH = 1
SEQ = 256
DEPTH = 2

GRID_W = 64
CTX_LEN = 256
NA_HEADS = 8
NA_HEAD_DIM = 64
NA_KH = 8
NA_KW = 16
NA_W = NA_HEADS * NA_HEAD_DIM
MLA_HEADS = 8
MLA_NOPE = 64
MLA_ROPE = 32
MLA_V = 64
MLA_Q_LORA = 256
MLA_KV_LORA = 128
MLA_OUT_W = MLA_HEADS * MLA_V
ROPE_THETA = 10000.0
Q_BLOCK = 128
MIX_W = NA_W + MLA_OUT_W
IN_COLS = 3 * NA_W + MLA_Q_LORA + MLA_KV_LORA + MLA_ROPE
SPLITS = [NA_W, 2 * NA_W, 3 * NA_W, 3 * NA_W + MLA_Q_LORA, 3 * NA_W + MLA_Q_LORA + MLA_KV_LORA]
POOL_WINDOWS = (2, 4, 8, 16)
POOL_GROUPS = len(POOL_WINDOWS)
POOL_GROUP = D_MODEL // POOL_GROUPS
FFN_DIM = 2816
N_EXPERTS = 8
TOP_K = 2
EXPERT_DIM = 3584
N_ATTN_LAYERS = (DEPTH + 1) // 2
N_POOL_LAYERS = DEPTH // 2
DEEPNORM_ALPHA = (2 * DEPTH) ** 0.25
DEEPNORM_BETA = (8 * DEPTH) ** -0.25
LN_EPS = 1e-5
RMS_EPS = 1e-6


def layer_norm(x, g, b):
    xf = x.astype(jnp.float32)
    mu = jnp.mean(xf, -1, keepdims=True)
    var = jnp.mean(jnp.square(xf - mu), -1, keepdims=True)
    return ((xf - mu) * lax.rsqrt(var + LN_EPS)).astype(x.dtype) * g + b

def rms_norm(x, g):
    xf = x.astype(jnp.float32)
    return (xf * lax.rsqrt(jnp.mean(xf * xf, -1, keepdims=True) + RMS_EPS)).astype(x.dtype) * g

def modulate(h, shift, scale):
    return h * (1 + scale) + shift

def softmax_f32(s, like):
    return jax.nn.softmax(s.astype(jnp.float32), axis=-1).astype(like.dtype)

def _rotate(x, ang):
    half = x.shape[-1] // 2
    x1, x2 = x[..., :half], x[..., half:]
    cos = jnp.cos(ang).astype(x.dtype)
    sin = jnp.sin(ang).astype(x.dtype)
    return jnp.concatenate([x1 * cos - x2 * sin, x1 * sin + x2 * cos], -1)

def axial_rope(x, ang_row, ang_col):
    if x.ndim == 4:
        ang_row, ang_col = ang_row[:, None], ang_col[:, None]
    half = x.shape[-1] // 2
    return jnp.concatenate([_rotate(x[..., :half], ang_row), _rotate(x[..., half:], ang_col)], -1)

def grid_angles(n):
    t = jnp.arange(n, dtype=jnp.int32)
    row = (t // GRID_W).astype(jnp.float32)
    col = (t % GRID_W).astype(jnp.float32)
    n_freq = MLA_ROPE // 4
    inv = 1.0 / (ROPE_THETA ** (jnp.arange(n_freq, dtype=jnp.float32) / n_freq))
    return row[:, None] * inv, col[:, None] * inv

def neighbourhood_attention(q, k, v, kc, vc, rel_bias):
    b, s, h, dh = q.shape
    rows = s // GRID_W
    kh = min(NA_KH, rows)
    n_loc = kh * NA_KW
    scale = dh ** -0.5
    cols = jnp.arange(GRID_W)
    col_start = jnp.clip(cols - NA_KW // 2, 0, GRID_W - NA_KW)
    key_cols = col_start[:, None] + jnp.arange(NA_KW)
    dcol = key_cols - cols[:, None] + NA_KW - 1

    def row_fn(r):
        row_start = jnp.clip(r - kh // 2, 0, rows - kh)
        key_rows = row_start + jnp.arange(kh)
        idx = (key_rows[None, :, None] * GRID_W + key_cols[:, None, :]).reshape(GRID_W, n_loc)
        drow = key_rows - r + NA_KH - 1
        bias = rel_bias[:, drow[None, :, None], dcol[:, None, :]].reshape(h, GRID_W, n_loc)
        q_r = lax.dynamic_slice_in_dim(q, r * GRID_W, GRID_W, axis=1)
        k_g = jnp.take(k, idx, axis=1)
        v_g = jnp.take(v, idx, axis=1)
        s_loc = jnp.einsum('bqhd,bqkhd->bhqk', q_r, k_g) * scale + bias
        s_ctx = jnp.einsum('bqhd,bkhd->bhqk', q_r, kc) * scale
        p = softmax_f32(jnp.concatenate([s_loc, s_ctx], -1), v)
        return (jnp.einsum('bhqk,bqkhd->bqhd', p[..., :n_loc], v_g)
                + jnp.einsum('bhqk,bkhd->bqhd', p[..., n_loc:], vc))

    out = lax.map(row_fn, jnp.arange(rows))
    return jnp.moveaxis(out, 0, 1).reshape(b, s, h, dh)

def dense_attention(q, k, v, scale):
    s = jnp.einsum('bqhd,bkhd->bhqk', q, k) * scale
    return jnp.einsum('bhqk,bkhd->bqhd', softmax_f32(s, v), v)

def mla_attention(qn, qr, kn, kr, v, scale):
    b, n, h, _ = qn.shape
    nb = n // Q_BLOCK

    def blk(args):
        qn_b, qr_b = args
        s = (jnp.einsum('bqhd,bkhd->bhqk', qn_b, kn) + jnp.einsum('bqhr,bkr->bhqk', qr_b, kr)) * scale
        return jnp.einsum('bhqk,bkhd->bqhd', softmax_f32(s, v), v)

    qn_blocks = qn.reshape(b, nb, Q_BLOCK, h, qn.shape[-1]).swapaxes(0, 1)
    qr_blocks = qr.reshape(b, nb, Q_BLOCK, h, qr.shape[-1]).swapaxes(0, 1)
    out = lax.map(blk, (qn_blocks, qr_blocks))
    return out.swapaxes(0, 1).reshape(b, n, h, v.shape[-1])

def _project(hh, w_in, q_norm, w_q_up, kv_norm, w_kv_up):
    bsz, n, _ = hh.shape
    qa, ka, va, q_c, kv_c, k_rope = jnp.split(hh @ w_in, SPLITS, axis=-1)
    heads = lambda t: t.reshape(bsz, n, NA_HEADS, NA_HEAD_DIM)
    q_mla = (rms_norm(q_c, q_norm) @ w_q_up).reshape(bsz, n, MLA_HEADS, MLA_NOPE + MLA_ROPE)
    kv_mla = (rms_norm(kv_c, kv_norm) @ w_kv_up).reshape(bsz, n, MLA_HEADS, MLA_NOPE + MLA_V)
    return (heads(qa), heads(ka), heads(va), q_mla[..., :MLA_NOPE], q_mla[..., MLA_NOPE:],
            kv_mla[..., :MLA_NOPE], k_rope, kv_mla[..., MLA_NOPE:])

def attention_mixer(h_lat, h_ctx, w_in, rel_bias, q_norm, w_q_up, kv_norm, w_kv_up, w_out, with_ctx_out):
    b, s, _ = h_lat.shape
    qa, ka, va, qn, qr, kn, kr, vb = _project(h_lat, w_in, q_norm, w_q_up, kv_norm, w_kv_up)
    qa_c, ka_c, va_c, qn_c, qr_c, kn_c, kr_c, vb_c = _project(h_ctx, w_in, q_norm, w_q_up, kv_norm, w_kv_up)
    ang_r, ang_c = grid_angles(s)
    qr = axial_rope(qr, ang_r, ang_c)
    kr = axial_rope(kr, ang_r, ang_c)
    mla_scale = (MLA_NOPE + MLA_ROPE) ** -0.5
    o_a = neighbourhood_attention(qa, ka, va, ka_c, va_c, rel_bias)
    o_b = mla_attention(qn, qr, jnp.concatenate([kn_c, kn], 1), jnp.concatenate([kr_c, kr], 1),
                        jnp.concatenate([vb_c, vb], 1), mla_scale)
    y_lat = jnp.concatenate([o_a.reshape(b, s, NA_W), o_b.reshape(b, s, MLA_OUT_W)], -1) @ w_out
    if not with_ctx_out:
        return y_lat, None
    n_ctx = h_ctx.shape[1]
    o_a_c = dense_attention(qa_c, ka_c, va_c, NA_HEAD_DIM ** -0.5)
    o_b_c = mla_attention(qn_c, qr_c, kn_c, kr_c, vb_c, mla_scale)
    y_ctx = jnp.concatenate([o_a_c.reshape(b, n_ctx, NA_W), o_b_c.reshape(b, n_ctx, MLA_OUT_W)], -1) @ w_out
    return y_lat, y_ctx

def pool_mixer(h, w, scale):
    b, n, d = h.shape
    t = jnp.arange(n)
    half = jnp.array(POOL_WINDOWS, dtype=jnp.int32) // 2
    lo = jnp.clip(t[:, None] - half, 0, n)
    hi = jnp.clip(t[:, None] + half, 0, n)
    cnt = (hi - lo).astype(jnp.float32)
    hf = h.astype(jnp.float32).reshape(b, n, POOL_GROUPS, POOL_GROUP)
    cs = jnp.concatenate([jnp.zeros((b, 1, POOL_GROUPS, POOL_GROUP), jnp.float32), jnp.cumsum(hf, axis=1)], 1)
    grp = jnp.arange(POOL_GROUPS)
    win_sum = cs[:, hi, grp] - cs[:, lo, grp]
    mixed = (win_sum / cnt[..., None] - hf).astype(h.dtype)
    return jnp.einsum('bngc,gcd->bngd', mixed, w).reshape(b, n, d) * scale

def swiglu(h, wg, wu, wd):
    return (jax.nn.silu(h @ wg) * (h @ wu)) @ wd

def moe_swiglu(h, router, wg, wu, wd):
    logits = (h @ router).astype(jnp.float32)
    top_val, top_idx = lax.top_k(logits, TOP_K)
    top_w = jax.nn.softmax(top_val, axis=-1)
    gates = jnp.sum(jax.nn.one_hot(top_idx, N_EXPERTS, dtype=jnp.float32) * top_w[..., None], axis=-2).astype(h.dtype)
    out = jnp.zeros_like(h)
    for e in range(N_EXPERTS):
        out = out + gates[..., e:e + 1] * swiglu(h, wg[e], wu[e], wd[e])
    return out

def first_inputs(seed: int = 0) -> dict:
    key = jax.random.key(seed)
    ks = iter(jax.random.split(key, 40))

    def nrm(shape, scale):
        return jax.random.normal(next(ks), shape, jnp.float32) * scale

    D = D_MODEL
    beta = DEEPNORM_BETA
    return {
        'x': nrm((BATCH, SEQ, D), 1.0),
        'c': nrm((BATCH, D), 1.0),
        'ctx': nrm((BATCH, CTX_LEN, D), 1.0),
        'c_ctx': nrm((D,), 1.0),
        'mod_w': nrm((DEPTH, D, 6 * D), D ** -0.5),
        'mod_b': nrm((DEPTH, 6 * D), 0.02),
        'ln1_g': 1.0 + nrm((DEPTH, D), 0.02),
        'ln1_b': nrm((DEPTH, D), 0.02),
        'ln2_g': 1.0 + nrm((DEPTH, D), 0.02),
        'ln2_b': nrm((DEPTH, D), 0.02),
        'attn_w_in': nrm((N_ATTN_LAYERS, D, IN_COLS), D ** -0.5),
        'na_rel_bias': nrm((N_ATTN_LAYERS, NA_HEADS, 2 * NA_KH - 1, 2 * NA_KW - 1), 0.5),
        'mla_q_norm': 1.0 + nrm((N_ATTN_LAYERS, MLA_Q_LORA), 0.02),
        'mla_w_q_up': nrm((N_ATTN_LAYERS, MLA_Q_LORA, MLA_HEADS * (MLA_NOPE + MLA_ROPE)), MLA_Q_LORA ** -0.5),
        'mla_kv_norm': 1.0 + nrm((N_ATTN_LAYERS, MLA_KV_LORA), 0.02),
        'mla_w_kv_up': nrm((N_ATTN_LAYERS, MLA_KV_LORA, MLA_HEADS * (MLA_NOPE + MLA_V)), MLA_KV_LORA ** -0.5),
        'attn_w_out': nrm((N_ATTN_LAYERS, MIX_W, D), MIX_W ** -0.5 * beta),
        'ffn_w_gate': nrm((N_ATTN_LAYERS, D, FFN_DIM), D ** -0.5),
        'ffn_w_up': nrm((N_ATTN_LAYERS, D, FFN_DIM), D ** -0.5),
        'ffn_w_down': nrm((N_ATTN_LAYERS, FFN_DIM, D), FFN_DIM ** -0.5 * beta),
        'pool_w': nrm((N_POOL_LAYERS, POOL_GROUPS, POOL_GROUP, POOL_GROUP), POOL_GROUP ** -0.5 * beta),
        'pool_scale': 1.0 + nrm((N_POOL_LAYERS, D), 0.02),
        'moe_router': nrm((N_POOL_LAYERS, D, N_EXPERTS), D ** -0.5),
        'moe_w_gate': nrm((N_POOL_LAYERS, N_EXPERTS, D, EXPERT_DIM), D ** -0.5),
        'moe_w_up': nrm((N_POOL_LAYERS, N_EXPERTS, D, EXPERT_DIM), D ** -0.5),
        'moe_w_down': nrm((N_POOL_LAYERS, N_EXPERTS, EXPERT_DIM, D), EXPERT_DIM ** -0.5 * beta),
    }

def first_block(x, c, ctx, c_ctx, mod_w, mod_b, ln1_g, ln1_b, ln2_g, ln2_b, attn_w_in, na_rel_bias,
              mla_q_norm, mla_w_q_up, mla_kv_norm, mla_w_kv_up, attn_w_out, ffn_w_gate, ffn_w_up,
              ffn_w_down, pool_w, pool_scale, moe_router, moe_w_gate, moe_w_up, moe_w_down):
    for i in range(DEPTH):
        j = i // 2
        even = i % 2 == 0
        ctx_live = any(l % 2 == 0 for l in range(i + 1, DEPTH))
        m_lat = (jax.nn.silu(c) @ mod_w[i] + mod_b[i])[:, None, :]
        sh1, sc1, g1, sh2, sc2, g2 = jnp.split(m_lat, 6, axis=-1)
        m_ctx = jax.nn.silu(c_ctx) @ mod_w[i] + mod_b[i]
        csh1, csc1, cg1, csh2, csc2, cg2 = jnp.split(m_ctx, 6, axis=-1)

        h_lat = modulate(x, sh1, sc1)
        if even:
            h_ctx = modulate(ctx, csh1, csc1)
            y_lat, y_ctx = attention_mixer(h_lat, h_ctx, attn_w_in[j], na_rel_bias[j], mla_q_norm[j],
                                           mla_w_q_up[j], mla_kv_norm[j], mla_w_kv_up[j], attn_w_out[j],
                                           ctx_live)
        else:
            y_lat = pool_mixer(h_lat, pool_w[j], pool_scale[j])
            y_ctx = pool_mixer(modulate(ctx, csh1, csc1), pool_w[j], pool_scale[j]) if ctx_live else None
        x = layer_norm(DEEPNORM_ALPHA * x + g1 * y_lat, ln1_g[i], ln1_b[i])
        if ctx_live:
            ctx = layer_norm(DEEPNORM_ALPHA * ctx + cg1 * y_ctx, ln1_g[i], ln1_b[i])

        h = modulate(x, sh2, sc2)
        n_ctx = ctx.shape[1] if ctx_live else 0
        if ctx_live:
            h = jnp.concatenate([modulate(ctx, csh2, csc2), h], axis=1)
        if even:
            y = swiglu(h, ffn_w_gate[j], ffn_w_up[j], ffn_w_down[j])
        else:
            y = moe_swiglu(h, moe_router[j], moe_w_gate[j], moe_w_up[j], moe_w_down[j])
        x = layer_norm(DEEPNORM_ALPHA * x + g2 * y[:, n_ctx:], ln2_g[i], ln2_b[i])
        if ctx_live:
            ctx = layer_norm(DEEPNORM_ALPHA * ctx + cg2 * y[:, :n_ctx], ln2_g[i], ln2_b[i])
    return x


MIX_WIDTH = D_MODEL
N_MIXERS = 4
GROUP_WIDTH = MIX_WIDTH // N_MIXERS
N_GROUP_HEADS = 4
HEAD_DIM = GROUP_WIDTH // N_GROUP_HEADS
SHORT_CONV_WIDTH = 3
CHUNK = 128
IDX_HEADS = 4
IDX_DIM = 64
TOPK_MAX = 256
CONF_CONV_WIDTH = 31
FFN_HIDDEN = -(-8 * D_MODEL // (3 * 256)) * 256
NORM_EPS = 1e-6
NEG = -1e30
SPLIT_SIZES = (GROUP_WIDTH, GROUP_WIDTH, GROUP_WIDTH,
               GROUP_WIDTH, GROUP_WIDTH,
               GROUP_WIDTH, GROUP_WIDTH, GROUP_WIDTH,
               IDX_HEADS * IDX_DIM, IDX_DIM, IDX_HEADS,
               GROUP_WIDTH, GROUP_WIDTH)
IN_COLS_2 = sum(SPLIT_SIZES)


def rmsnorm(x, g):
    xf = x.astype(jnp.float32)
    y = xf * lax.rsqrt(jnp.mean(xf * xf, axis=-1, keepdims=True) + NORM_EPS)
    return (y * g.astype(jnp.float32)).astype(x.dtype)

def layernorm(x, g, b):
    xf = x.astype(jnp.float32)
    mu = jnp.mean(xf, axis=-1, keepdims=True)
    var = jnp.mean(jnp.square(xf - mu), axis=-1, keepdims=True)
    y = (xf - mu) * lax.rsqrt(var + LN_EPS)
    return (y * g.astype(jnp.float32) + b.astype(jnp.float32)).astype(x.dtype)

def causal_dwconv(x, w):
    width, chans = w.shape
    return lax.conv_general_dilated(
        x, w[:, None, :].astype(x.dtype), window_strides=(1,),
        padding=[(width - 1, 0)], dimension_numbers=('NWC', 'WIO', 'NWC'),
        feature_group_count=chans)

def rope_tables(seq, dim):
    inv_freq = ROPE_THETA ** (-jnp.arange(0, dim, 2, dtype=jnp.float32) / dim)
    ang = jnp.arange(seq, dtype=jnp.float32)[:, None] * inv_freq[None, :]
    return jnp.cos(ang), jnp.sin(ang)

def apply_rope(x, cos, sin):
    half = x.shape[-1] // 2
    c = cos[None, :, None, :].astype(x.dtype)
    s = sin[None, :, None, :].astype(x.dtype)
    x1, x2 = x[..., :half], x[..., half:]
    return jnp.concatenate([x1 * c - x2 * s, x2 * c + x1 * s], axis=-1)

def short_conv_mixer(b, c, h, w_conv):
    return b * causal_dwconv(c * h, w_conv)

def gmlp_mixer(u, v, ln_g, ln_b, w_s, b_s):
    bsz, seq, _ = v.shape
    vn = layernorm(v, ln_g, ln_b)
    vc = vn.reshape(bsz, seq // CHUNK, CHUNK, N_GROUP_HEADS, HEAD_DIM)
    mask = jnp.tril(jnp.ones((CHUNK, CHUNK), dtype=bool))
    ws = jnp.where(mask[None], w_s, 0).astype(v.dtype)
    mixed = jnp.einsum('hts,bnshd->bnthd', ws, vc)
    mixed = mixed + b_s.T[None, None, :, :, None].astype(v.dtype)
    return u * mixed.reshape(bsz, seq, GROUP_WIDTH)

def dsa_mixer(q, k, v, q_idx, k_idx, w_idx):
    bsz, seq, _ = q.shape
    topk = min(TOPK_MAX, seq // 4)
    cos_a, sin_a = rope_tables(seq, HEAD_DIM)
    cos_i, sin_i = rope_tables(seq, IDX_DIM)
    q = apply_rope(q.reshape(bsz, seq, N_GROUP_HEADS, HEAD_DIM), cos_a, sin_a)
    k = apply_rope(k.reshape(bsz, seq, N_GROUP_HEADS, HEAD_DIM), cos_a, sin_a)
    v = v.reshape(bsz, seq, N_GROUP_HEADS, HEAD_DIM)
    qi = apply_rope(q_idx.reshape(bsz, seq, IDX_HEADS, IDX_DIM), cos_i, sin_i).astype(jnp.float32)
    ki = apply_rope(k_idx[:, :, None, :], cos_i, sin_i)[:, :, 0, :].astype(jnp.float32)
    wi = w_idx.astype(jnp.float32) * (IDX_HEADS ** -0.5) * (IDX_DIM ** -0.5)
    scale = HEAD_DIM ** -0.5
    nblk = seq // Q_BLOCK

    def to_blocks(t):
        return jnp.swapaxes(t.reshape((bsz, nblk, Q_BLOCK) + t.shape[2:]), 0, 1)

    kpos = jnp.arange(seq)
    tpos = kpos.reshape(nblk, Q_BLOCK)

    def block(args):
        qb, qib, wib, tb = args
        rel = jax.nn.relu(jnp.einsum('bqjd,bsd->bqjs', qib, ki))
        score = jnp.einsum('bqjs,bqj->bqs', rel, wib)
        admissible = kpos[None, :] <= tb[:, None]
        score = jnp.where(admissible[None], score, NEG)
        _, idx = lax.top_k(score, topk)
        valid = idx <= tb[None, :, None]
        kg = jax.vmap(lambda kk, ii: kk[ii])(k, idx)
        vg = jax.vmap(lambda vv, ii: vv[ii])(v, idx)
        logits = jnp.einsum('bqhd,bqkhd->bqhk', qb, kg).astype(jnp.float32) * scale
        logits = jnp.where(valid[:, :, None, :], logits, NEG)
        p = jax.nn.softmax(logits, axis=-1).astype(v.dtype)
        return jnp.einsum('bqhk,bqkhd->bqhd', p, vg)

    out = lax.map(block, (to_blocks(q), to_blocks(qi), to_blocks(wi), tpos))
    return jnp.swapaxes(out, 0, 1).reshape(bsz, seq, GROUP_WIDTH)

def conformer_conv_mixer(a, gate, w_dw, b_dw, ln_g, ln_b):
    y = a * jax.nn.sigmoid(gate)
    y = causal_dwconv(y, w_dw) + b_dw.astype(y.dtype)
    y = layernorm(y, ln_g, ln_b)
    return jax.nn.silu(y)

def hybrid_layer(x, g_mix, w_in, w_conv_a, gmlp_ln_g, gmlp_ln_b, w_s, b_s,
                 w_conf, b_conf, conf_ln_g, conf_ln_b, w_out,
                 g_ffn, w_gate, w_up, w_down):
    h = rmsnorm(x, g_mix)
    z = h @ w_in
    cuts, acc = [], 0
    for sz in SPLIT_SIZES[:-1]:
        acc += sz
        cuts.append(acc)
    (a_b, a_c, a_h, g_u, g_v, q, k, v, q_idx, k_idx, w_idx, d_a, d_g) = jnp.split(z, cuts, axis=-1)
    y_a = short_conv_mixer(a_b, a_c, a_h, w_conv_a)
    y_b = gmlp_mixer(g_u, g_v, gmlp_ln_g, gmlp_ln_b, w_s, b_s)
    y_c = dsa_mixer(q, k, v, q_idx, k_idx, w_idx)
    y_d = conformer_conv_mixer(d_a, d_g, w_conf, b_conf, conf_ln_g, conf_ln_b)
    x = x + jnp.concatenate([y_a, y_b, y_c, y_d], axis=-1) @ w_out
    hf = rmsnorm(x, g_ffn)
    return x + (jax.nn.silu(hf @ w_gate) * (hf @ w_up)) @ w_down

def second_inputs(seed: int = 0) -> dict:
    key = jax.random.key(seed)
    ks = jax.random.split(key, 20)
    f32 = jnp.float32
    G, H = GROUP_WIDTH, N_GROUP_HEADS

    def nrm(k, shape, scale):
        return jax.random.normal(k, shape, f32) * scale

    def gain(k, shape):
        return 1.0 + 0.05 * jax.random.normal(k, shape, f32)

    return {
        "x": jax.random.normal(ks[0], (BATCH, SEQ, D_MODEL), f32),
        "g_mix": gain(ks[1], (DEPTH, D_MODEL)),
        "w_in": nrm(ks[2], (DEPTH, D_MODEL, IN_COLS_2), D_MODEL ** -0.5),
        "w_conv_a": nrm(ks[3], (DEPTH, SHORT_CONV_WIDTH, G), SHORT_CONV_WIDTH ** -0.5),
        "gmlp_ln_g": gain(ks[4], (DEPTH, G)),
        "gmlp_ln_b": nrm(ks[5], (DEPTH, G), 0.02),
        "w_s": nrm(ks[6], (DEPTH, H, CHUNK, CHUNK), 0.5 * CHUNK ** -0.5),
        "b_s": 1.0 + nrm(ks[7], (DEPTH, H, CHUNK), 0.1),
        "w_conf": nrm(ks[8], (DEPTH, CONF_CONV_WIDTH, G), CONF_CONV_WIDTH ** -0.5),
        "b_conf": nrm(ks[9], (DEPTH, G), 0.02),
        "conf_ln_g": gain(ks[10], (DEPTH, G)),
        "conf_ln_b": nrm(ks[11], (DEPTH, G), 0.02),
        "w_out": nrm(ks[12], (DEPTH, MIX_WIDTH, D_MODEL), 0.5 * MIX_WIDTH ** -0.5),
        "g_ffn": gain(ks[13], (DEPTH, D_MODEL)),
        "w_gate": nrm(ks[14], (DEPTH, D_MODEL, FFN_HIDDEN), D_MODEL ** -0.5),
        "w_up": nrm(ks[15], (DEPTH, D_MODEL, FFN_HIDDEN), D_MODEL ** -0.5),
        "w_down": nrm(ks[16], (DEPTH, FFN_HIDDEN, D_MODEL), 0.5 * FFN_HIDDEN ** -0.5),
        "g_final": gain(ks[17], (D_MODEL,)),
    }

def second_block(x, g_mix, w_in, w_conv_a, gmlp_ln_g, gmlp_ln_b, w_s, b_s,
              w_conf, b_conf, conf_ln_g, conf_ln_b, w_out,
              g_ffn, w_gate, w_up, w_down, g_final):
    for l in range(DEPTH):
        x = hybrid_layer(x, g_mix[l], w_in[l], w_conv_a[l], gmlp_ln_g[l], gmlp_ln_b[l],
                         w_s[l], b_s[l], w_conf[l], b_conf[l], conf_ln_g[l], conf_ln_b[l],
                         w_out[l], g_ffn[l], w_gate[l], w_up[l], w_down[l])
    return rmsnorm(x, g_final)


def setup_inputs(seed=0):
    out = dict(first_inputs(seed))
    for name, value in second_inputs(seed + 1).items():
        if name != "x":
            out[name + "_2"] = value
    return out


def reference(
    x, c, ctx, c_ctx, mod_w, mod_b, ln1_g, ln1_b, ln2_g, ln2_b, attn_w_in, na_rel_bias,
    mla_q_norm, mla_w_q_up, mla_kv_norm, mla_w_kv_up, attn_w_out, ffn_w_gate, ffn_w_up,
    ffn_w_down, pool_w, pool_scale, moe_router, moe_w_gate, moe_w_up, moe_w_down, g_mix_2,
    w_in_2, w_conv_a_2, gmlp_ln_g_2, gmlp_ln_b_2, w_s_2, b_s_2, w_conf_2, b_conf_2, conf_ln_g_2,
    conf_ln_b_2, w_out_2, g_ffn_2, w_gate_2, w_up_2, w_down_2, g_final_2,
):
    x = first_block(
        x, c, ctx, c_ctx, mod_w, mod_b, ln1_g, ln1_b, ln2_g, ln2_b, attn_w_in, na_rel_bias,
        mla_q_norm, mla_w_q_up, mla_kv_norm, mla_w_kv_up, attn_w_out, ffn_w_gate, ffn_w_up,
        ffn_w_down, pool_w, pool_scale, moe_router, moe_w_gate, moe_w_up, moe_w_down,
    )
    return second_block(
        x, g_mix_2, w_in_2, w_conv_a_2, gmlp_ln_g_2, gmlp_ln_b_2, w_s_2, b_s_2, w_conf_2,
        b_conf_2, conf_ln_g_2, conf_ln_b_2, w_out_2, g_ffn_2, w_gate_2, w_up_2, w_down_2,
        g_final_2,
    )


_drawn_inputs = setup_inputs


def setup_inputs(seed=0):
    import zlib

    import numpy as np

    out = dict(_drawn_inputs(seed))
    spreads = {}
    factors = {'na_rel_bias': 3.651,
     'mla_q_norm': 8.0,
     'mla_kv_norm': 8.0,
     'pool_scale': 8.0,
     'gmlp_ln_g_2': 8.0,
     'gmlp_ln_b_2': 35.621,
     'b_conf_2': 6.472,
     'conf_ln_g_2': 4.306,
     'conf_ln_b_2': 8.0,
     'g_ffn_2': 2.805}
    for name, (base, spread) in spreads.items():
        noise = np.random.default_rng([zlib.crc32(name.encode()), seed]).standard_normal(out[name].shape)
        drawn = base * np.exp(spread * noise) if base else spread * noise
        out[name] = __import__('jax').numpy.asarray(drawn.astype(out[name].dtype))
    for name, factor in factors.items():
        out[name] = (out[name] * factor).astype(out[name].dtype)
    return out
```

```python
from contextlib import ExitStack

import concourse.bass as bass
import numpy as np
from concourse import mybir
from concourse.alu_op_type import AluOpType as ALU

P = 128
D = 1024
KT = D // P
SEQ = 256
TT = SEQ // P
HEADS = 8
HD = 64
ROPE_D = 32
MQ = HD + ROPE_D
CW = 4096
RING = 7
NC_COLS = 1952
FT = 22
EXPERTS = 8
EFT = 28
SLOTS = 128
PASSES_MAX = SEQ // SLOTS
ALPHA = 4.0 ** 0.25
LN_EPS = 1e-5
RMS_EPS = 1e-6
NEG = -1e30
TAPS_A, TAPS_C = 3, 31
HALO = 8
MLA_SCALE = float(MQ) ** -0.5
NA_SCALE = float(HD) ** -0.5

F32 = mybir.dt.float32
I32 = mybir.dt.int32
ACT = mybir.ActivationFunctionType
AX_X = mybir.AxisListType.X



def ffn_order(n_gu):
    order, down = [], 0
    for i in range(n_gu):
        order.append(("gu", i))
        if i >= 2 and i % 2 == 0:
            order.append(("d", down))
            down += 1
    while 4 * down < 2 * n_gu:
        order.append(("d", down))
        down += 1
    return order


FFN_ORDER = ffn_order(FT // 2)
MOE_ORDER = ffn_order(EFT // 2)
FIRST_ORDER = ([("mod", 0, i) for i in range(4)] + [("proj", n) for n in ("c", "ka", "qa", "va")]
               + [("mod", 0, i) for i in range(4, 12)] + [("mod", 1, i) for i in range(2)]
               + [("up",)] + [("mod", 1, i) for i in range(2, 12)]
               + [("out", 0), ("out", 1)] + [("ffn",) + c for c in FFN_ORDER] + [("pool",)])
LAYER_ORDER = ([("mix", n) for n in ("qi", "dd", "qk", "vg", "ch", "bu")]
               + [("out", 0), ("out", 1)] + [("ffn",) + c for c in FFN_ORDER])
N_FIRST, N_EXPERT, N_LAYER = len(FIRST_ORDER), len(MOE_ORDER), len(LAYER_ORDER)
assert N_FIRST % RING == 0 and N_EXPERT % RING == 0
N_CHUNKS = N_FIRST + EXPERTS * N_EXPERT + 2 * N_LAYER

COLS = {}
_n = 0
for _name, _w in (("modb0", 48), ("modb1", 48), ("c", 16), ("qn", 2), ("kvn", 1), ("pscale", 8), ("half", 1)):
    COLS[_name] = (_n, _w)
    _n += _w
N_COLS = 128
CONST = {}
_n = 0
for _name, _w in (("ident", 128), ("ones", 128), ("before", 128), ("tri", 128), ("iota", 128),
                  ("causal", 512), ("mcos", 64), ("msin", 32), ("dcos", 64), ("dsin", 64), ("rev", 8),
                  ("neghalf", 8)):
    CONST[_name] = (_n, _w)
    _n += _w
N_CONST = _n
QI_W = 324
PAR = {}
_n = 0
for _name, _w in (("gmix", 8), ("gffn", 8), ("wca", 6), ("wcf", 62), ("bcf", 2), ("clg", 2), ("clb", 2),
                  ("gg", 256), ("gb", 256), ("bs", 256)):
    PAR[_name] = (_n, _w)
    _n += _w
N_PAR = _n
WS_AT = KT * QI_W
PAR_AT = WS_AT + 4 * P
INV_AT = 2048 + 64


class Progress:

    def __init__(self, sem, book):
        self.sem, self.book, self.n, self.named = sem, book, 0, set()

    def did(self, *names):
        self.n += 1
        for name in names:
            assert name not in self.named, name
            self.named.add(name)
            self.book[name] = self.n
        if not self.book.get("complete"):
            self.book["per turn"] = self.n
        return 1

    @property
    def per(self):
        return self.book.get("per turn", 1)

    def at(self, name, turn=None):
        assert name in self.book or not self.book.get("complete"), name
        k = self.book.get(name, 1)
        return k if turn is None else turn * self.per + (self.per + k)

    def was(self, name, turn):
        assert name in self.book or not self.book.get("complete"), name
        return turn * self.per + self.book.get(name, 1)

    def last(self, turn=None):
        return self.n if turn is None else turn * self.per + (self.per + self.n)


def build(nc, ins, out, books):
    chunks_d, x_d, ctx_d, cols_d, const_d, bias_d, rows_d, gfin_d = ins
    with ExitStack() as ctx:
        def sem(name):
            return ctx.enter_context(nc.semaphore(name))

        ring = ctx.enter_context(nc.sbuf_tensor("ring", [P, RING * CW], F32))
        bank = [ctx.enter_context(nc.psum_tensor(f"bank{i}", [P, 512], F32)) for i in range(8)]
        x = ctx.enter_context(nc.sbuf_tensor("x", [P, TT, D], F32))
        cols = ctx.enter_context(nc.sbuf_tensor("cols", [P, N_COLS], F32))
        const = ctx.enter_context(nc.sbuf_tensor("const", [P, N_CONST], F32))
        mod = ctx.enter_context(nc.sbuf_tensor("mod", [P, 2, 48, 2], F32))
        stat = ctx.enter_context(nc.sbuf_tensor("stat", [P, 128], F32))
        soft = ctx.enter_context(nc.sbuf_tensor("soft", [P, 3, 32], F32))
        n_passes = ctx.enter_context(nc.sbuf_tensor("n_passes", [P, 1], I32))
        R = ctx.enter_context(nc.sbuf_tensor("rows", [P, 4096], F32))
        W = ctx.enter_context(nc.sbuf_tensor("work", [P, 16232], F32))

        def view(region, at, *dims):
            n = int(np.prod(dims))
            v = region[:, at:at + n]
            if len(dims) == 2:
                v = v.rearrange("p (a b) -> p a b", a=dims[0])
            elif len(dims) == 3:
                v = v.rearrange("p (a b c) -> p a b c", a=dims[0], b=dims[1])
            elif len(dims) == 4:
                v = v.rearrange("p (a b c d) -> p a b c d", a=dims[0], b=dims[1], c=dims[2])
            return v

        def col(name, i=0):
            return cols[:, COLS[name][0] + i:COLS[name][0] + i + 1]

        def con(name, *dims):
            return view(const, CONST[name][0], *(dims or (CONST[name][1],)))

        ident, ones = con("ident"), con("ones")
        nmax, rsum, rinv = soft[:, 0, :], soft[:, 1, :], soft[:, 2, :]

        ln_g, ln_b = R[:, 0:D], R[:, D:2 * D]
        gate_row = [R[:, 2 * D:3 * D], R[:, 3 * D:4 * D]]
        hT4 = view(R, 0, KT, 2 * SEQ)
        qmT = view(R, 0, HEADS, SEQ)
        vm = view(R, 2048, 4, HEADS * HD)
        bias = view(W, 0, TT, HEADS, SEQ)
        kmT = view(W, 0, HEADS, 2 * SEQ)
        ctx_tok = view(W, 4096, TT, D)
        o_tok = ctx_tok
        c_tok = view(W, 6144, 4, 416)
        probsT = view(W, 6144, 2, 512)
        qaT = view(W, 7808, 4, SEQ)
        kaT = view(W, 8832, 4, 2 * SEQ)
        va = view(W, 10880, 4, 512)
        qm_tok = view(W, 7808, TT, HEADS * MQ)
        oT = view(W, 9344, KT, SEQ)
        rope_a = view(W, 14976, 256)
        rope_b = view(W, 15232, 256)
        qcT = view(W, 12928, 2, SEQ)
        kvcT = view(W, 13440, 512)
        krT = view(W, 13952, 512)
        probs = view(W, 14464, 3, 512)
        hT = view(W, 0, KT, SEQ)
        hid = view(W, 2048, FT, SEQ)
        silu = view(W, 7680, 2, 512)
        tmp = view(W, 8704, TT, D)
        hp = view(W, 2048, KT, SEQ + 2 * HALO)
        win = [view(W, 4224, 2, SEQ + 2 * HALO), view(W, 4768, 2, SEQ + 2 * HALO)]
        mixT = view(W, 5312, KT, SEQ)
        xgT = view(W, 0, KT, SLOTS)
        hidE = view(W, 2048, EFT, SLOTS)
        pick = view(W, 5632, TT, SLOTS)
        pickg = view(W, 5888, TT, SLOTS)
        spread = view(W, 6144, SEQ)
        outE = view(W, 6400, D)
        siluE = view(W, 7680, 2, 256)
        place = view(W, 8192, TT, EXPERTS)
        gates = view(W, 8208, TT, EXPERTS)
        route = view(W, 8224, 12, 16)
        now = view(W, 8416, 2, TT)
        acc = view(W, 10752, TT, D)
        catT = view(W, 2048, KT, SEQ)
        qi_tok = view(W, 4096, TT, QI_W)
        qir = view(W, 4744, TT, 384)
        chp = view(W, 4096, 2, SEQ + TAPS_A - 1)
        rt_a, rt_b = view(W, 5512, 512), view(W, 6024, 512)
        junk = view(W, 5512, D)
        qk_tok = view(W, 6536, TT, 512)
        vg_tok = view(W, 7560, TT, 512)
        bu = view(W, 8704, 2, 512)
        yp = view(W, 9728, 2, SEQ + TAPS_C - 1)
        par = view(W, 10752, N_PAR)
        qkr = view(W, 11616, TT, 512)
        qiT = view(W, 12640, 2, SEQ)
        kiT = view(W, 13152, SEQ)
        qT = view(W, 13408, 2, SEQ)
        kT = view(W, 13920, 2, SEQ)
        probs2 = view(W, 14432, 3, SEQ)
        sig = view(W, 14432, 2, SEQ)
        probsT2 = view(W, 15200, 2, SEQ)
        ac = view(W, 15200, 2, SEQ)
        o_c = view(W, 15712, TT, SEQ)
        rel = view(R, 0, TT, 4, SEQ)
        conv = view(R, 0, 2, SEQ)
        ynorm = view(R, 512, TT, SEQ)
        mixed = view(R, 1024, 2, SEQ)
        left = view(R, 2048, TT, SEQ)
        mask = view(R, 2560, TT, SEQ)
        wsm = view(R, 3072, 4, P)
        vn = view(R, 3584, TT, SEQ)
        gfin = R[:, 0:D]
        ms = view(W, 5512, 3, SEQ)
        diag = [W[:, 12928 + P * i:12928 + P * (i + 1)] for i in range(2)]

        def pr(name, i=0, w=1):
            return par[:, PAR[name][0] + i:PAR[name][0] + i + w]

        in_loaded = sem("in_loaded")
        bias_loaded = sem("bias_loaded")
        rows_loaded = sem("rows_loaded")
        gfin_loaded = sem("gfin_loaded")
        stored = sem("stored")
        wait_carrier = sem("wait_carrier")
        landed_a = [sem(f"landed_first_{i}") for i in range(RING)]
        landed_b = [sem(f"landed_expert_{i}") for i in range(RING)]
        landed_c = [sem(f"landed_layer_{i}") for i in range(RING)]

        def progress(name):
            return Progress(sem(name), books.setdefault(name, {}))

        ten, vec, sca, pol = (progress(f"{e}_first") for e in ("tensor", "vector", "scalar", "pool"))
        ten_b, vec_b, sca_b = (progress(f"{e}_experts") for e in ("tensor", "vector", "scalar"))
        ten_c, vec_c, sca_c, pol_c = (progress(f"{e}_layers") for e in ("tensor", "vector", "scalar", "pool"))
        vec_f, sca_f, pol_f, ten_f = (progress(f"{e}_final") for e in ("vector", "scalar", "pool", "tensor"))

        def slot(n):
            return ring[:, (n % RING) * CW:(n % RING + 1) * CW]

        FIRST_AT = {c: n for n, c in enumerate(FIRST_ORDER)}
        EXPERT_AT = {c: n for n, c in enumerate(MOE_ORDER)}
        LAYER_AT = {c: n for n, c in enumerate(LAYER_ORDER)}

        def layer_landed(n, turn):
            per_layer = len(range(n % RING, N_LAYER, RING))
            return turn * (16 * per_layer) + 16 * (n // RING + 1)

        GROUPS = ([("h", k) for k in range(KT)] + [("c", t) for t in range(4)] + [("ka", i) for i in range(4)]
                  + [("qa", i) for i in range(2)] + [("va", t) for t in range(4)])
        UP_GROUPS = ([("qup", t, half) for t in range(TT) for half in range(2)] + [("v", t) for t in range(4)]
                     + [("kn", h) for h in range(HEADS)] + [("qmT", i) for i in range(4)])

        def by_scalar(n):
            return n % 2 == 1

        def probs_got_by(u):
            return sca if u % 2 else vec

        block = ctx.enter_context(nc.Block())

        @block.sync
        def _(sp):
            for n in range(N_FIRST):
                if n >= RING:
                    sp.wait_ge(ten.sem, ten.at(f"used {n - RING}"))
                sp.dma_start(slot(n), chunks_d[n]).then_inc(landed_a[n % RING], 16)

            for n in range(RING):
                sp.wait_ge(ten.sem, ten.at(f"used {N_FIRST - RING + n}"))
                sp.dma_start(slot(n), chunks_d[N_FIRST + n]).then_inc(landed_b[n], 16)
            sp.wait_ge(vec.sem, vec.at("passes"))
            passes = sp.value_load(n_passes[0:1, 0:1], min_val=1, max_val=PASSES_MAX)

            def load(n, first, turn):
                sp.wait_ge(ten_b.sem, ten_b.at(f"used {n - RING}", turn))
                sp.dma_start(slot(n), chunks_d[bass.ds(first + n, 1)].rearrange("a p n -> (a p) n"))\
                    .then_inc(landed_b[n % RING], 16)

            with sp.Fori(0, passes) as p:
                with sp.Fori(0, EXPERTS - 1) as e:
                    for n in range(RING, N_EXPERT + RING):
                        load(n, e * N_EXPERT + N_FIRST, p * EXPERTS + e)
                for n in range(RING, N_EXPERT):
                    load(n, N_FIRST + (EXPERTS - 1) * N_EXPERT, p * EXPERTS + (EXPERTS - 1))
                behind = nc.s_assert_within(
                    (p - passes + 1) * (EXPERTS * N_EXPERT) + (N_FIRST + (EXPERTS - 1) * N_EXPERT),
                    N_FIRST - N_EXPERT, N_FIRST + (EXPERTS - 1) * N_EXPERT,
                    skip_runtime_bounds_check_because="p is below the number of passes, which is at most two")
                for n in range(N_EXPERT, N_EXPERT + RING):
                    load(n, behind, p * EXPERTS + (EXPERTS - 1))

            for layer in range(2):
                for n in range(0 if layer else RING, N_LAYER):
                    if n >= RING:
                        sp.wait_ge(ten_c.sem, ten_c.at(f"used {n - RING}", layer))
                    else:
                        sp.wait_ge(ten_c.sem, ten_c.at(f"used {max(range(n, N_LAYER, RING))}", layer - 1))
                    sp.dma_start(slot(n), chunks_d[N_FIRST + EXPERTS * N_EXPERT + layer * N_LAYER + n])\
                        .then_inc(landed_c[n % RING], 16)
            for t in range(TT):
                sp.wait_ge(vec_f.sem, vec_f.at(f"out {t}"))
                sp.dma_start(out[t * P:(t + 1) * P, :], tmp[:, t, :]).then_inc(stored, 16)
            sp.wait_ge(stored, 16 * TT)

        @block.gpsimd
        def _(pool):
            pool.dma_start(bias, bias_d).then_inc(bias_loaded, 16)

            def rsqrt(n, dst, src, w):
                pool.wait_ge(vec.sem, vec.at(f"power {n} wanted"))
                nc.gpsimd.tensor_tensor(dst, src, con("neghalf")[:, 0:w], ALU.pow).then_inc(pol.sem, pol.did(f"power {n}"))

            pool.wait_ge(in_loaded, 64)
            rsqrt("c", stat[:, 8:14], stat[:, 0:6], 6)
            pool.wait_ge(vec.sem, vec.at("krT"))
            pool.wait_ge(ten.sem, ten.at("scores 15"))
            nc.gpsimd.tensor_copy(kmT[HD:MQ, :, :], krT[HD:MQ, :].unsqueeze(1).broadcast_to([ROPE_D, HEADS, 2 * SEQ]))\
                .then_inc(pol.sem, pol.did("kmT rope"))
            for n in range(4):
                if n == 0:
                    pool.wait_ge(ten.sem, ten.at("attended"))
                else:
                    pool.wait_ge(vec.sem, vec.at(f"norm {n - 1} 1"))
                pool.dma_start(R[:, 0:2 * D], rows_d[n]).then_inc(rows_loaded, 16)
                for t in range(TT):
                    if n < 3:
                        rsqrt(f"norm {n} {t}", stat[:, 40 + t:41 + t], stat[:, 32 + t:33 + t], 1)
                    else:
                        pool.wait_ge(vec_f.sem, vec_f.at(f"power wanted {t}"))
                        nc.gpsimd.tensor_tensor(stat[:, 40 + t:41 + t], stat[:, 32 + t:33 + t], con("neghalf")[:, 0:1],
                                                ALU.pow).then_inc(pol_f.sem, pol_f.did(f"power norm {t}"))
            pool.sem_inc(pol_c.sem, pol_c.per)
            with pool.Fori(0, 2) as l:
                for n, w in (("mix", 2), ("v", 2), ("conf", 2), ("ffn", 2)):
                    pool.wait_ge(vec_c.sem, vec_c.at(f"power {n} wanted", l))
                    at = {"mix": 0, "v": 2, "conf": 4, "ffn": 6}[n]
                    nc.gpsimd.tensor_tensor(stat[:, 40 + at:42 + at], stat[:, 32 + at:34 + at],
                                            con("neghalf")[:, 0:2], ALU.pow).then_inc(pol_c.sem, pol_c.did(f"power {n}"))
            pool.wait_ge(vec_c.sem, vec_c.at("x 1", 1))
            pool.dma_start(gfin, gfin_d).then_inc(gfin_loaded, 16)
            pool.wait_ge(vec_f.sem, vec_f.at("power wanted final"))
            nc.gpsimd.tensor_tensor(stat[:, 40:42], stat[:, 32:34], con("neghalf")[:, 0:2], ALU.pow)\
                .then_inc(pol_f.sem, pol_f.did("power final"))

        @block.tensor
        def _(pe):
            mm, tr = nc.tensor.matmul, nc.tensor.transpose
            csilu = view(stat, 48, KT, 2)

            def landed(chunk):
                n = FIRST_AT[chunk]
                pe.wait_ge(landed_a[n % RING], 16 * (n // RING + 1))
                return slot(n)

            def used(chunk):
                return f"used {FIRST_AT[chunk]}"

            def rows(w):
                return w.rearrange("p (k n) -> p k n", k=KT)

            def wait_all(*whos):
                for who, name in whos:
                    pe.wait_ge(who.sem, who.at(name))

            def mod_chunk(which, i):
                w = rows(landed(("mod", which, i)))
                for j in range(4):
                    at = which * 96 + (4 * i + j) * 2
                    for k in range(KT):
                        last = mm(bank[7][:, at:at + 2], w[:, k, j * P:(j + 1) * P], csilu[:, k, :],
                                  start=k == 0, stop=k == KT - 1)
                last.then_inc(ten.sem, ten.did(used(("mod", which, i))))

            pe.wait_ge(in_loaded, 64)
            pe.wait_ge(sca.sem, sca.at("silu c"))
            for i in range(4):
                mod_chunk(0, i)

            def bank_free(groups, n):
                if n >= 7:
                    who = sca if by_scalar(n - 7) else vec
                    pe.wait_ge(who.sem, who.at(f"got {groups[n - 7]}"))
                return bank[n % 7]

            n = 0
            pe.wait_ge(vec.sem, vec.at("mod 0 first"))
            for k in range(KT):
                b = bank_free(GROUPS, n)
                for t in range(4):
                    src = ctx_tok[:, t, :] if t < 2 else x[:, t - 2, :]
                    last = tr(b[:, t * P:(t + 1) * P], src[:, k * P:(k + 1) * P], ident)
                last.then_inc(ten.sem, ten.did(f"full {GROUPS[n]}"))
                n += 1
            for k in range(KT):
                who = sca if by_scalar(k) else vec
                pe.wait_ge(who.sem, who.at(f"got {('h', k)}"))
            w = rows(landed(("proj", "c")))
            for t in range(4):
                b = bank_free(GROUPS, n)
                c0 = 256 if t < 2 else 0
                for k in range(KT):
                    last = mm(b[:, c0:416], hT4[:, k, t * P:(t + 1) * P], w[:, k, c0:416], start=k == 0, stop=k == KT - 1)
                last.then_inc(ten.sem, ten.did(f"full {GROUPS[n]}", *[used(("proj", "c"))] * (t == 3)))
                n += 1
            w = rows(landed(("proj", "ka")))
            for i in range(4):
                b = bank_free(GROUPS, n)
                for k in range(KT):
                    last = mm(b[:, :], w[:, k, i * P:(i + 1) * P], hT4[:, k, :], start=k == 0, stop=k == KT - 1)
                last.then_inc(ten.sem, ten.did(f"full {GROUPS[n]}", *[used(("proj", "ka"))] * (i == 3)))
                n += 1
            w = rows(landed(("proj", "qa")))
            for i in range(2):
                b = bank_free(GROUPS, n)
                for j in range(2):
                    for k in range(KT):
                        last = mm(b[:, j * SEQ:(j + 1) * SEQ], w[:, k, (2 * i + j) * P:(2 * i + j + 1) * P],
                                  hT4[:, k, SEQ:2 * SEQ], start=k == 0, stop=k == KT - 1)
                last.then_inc(ten.sem, ten.did(f"full {GROUPS[n]}", *[used(("proj", "qa"))] * (i == 1)))
                n += 1
            w = rows(landed(("proj", "va")))
            for t in range(4):
                b = bank_free(GROUPS, n)
                for k in range(KT):
                    last = mm(b[:, :], hT4[:, k, t * P:(t + 1) * P], w[:, k, :], start=k == 0, stop=k == KT - 1)
                last.then_inc(ten.sem, ten.did(f"full {GROUPS[n]}", *[used(("proj", "va"))] * (t == 3)))
                n += 1

            wait_all((vec, "codes normed"), (vec, f"got {('va', 2)}"), (sca, f"got {('va', 3)}"))
            for t in range(TT):
                for j in range(2):
                    last = tr(bank[0][:, j * SEQ + t * P:j * SEQ + (t + 1) * P], c_tok[:, 2 + t, j * P:(j + 1) * P], ident)
            for t in range(4):
                last = tr(bank[1][:, t * P:(t + 1) * P], c_tok[:, t, 256:384], ident)
            for t in range(4):
                last = tr(bank[2][0:MQ, t * P:(t + 1) * P], c_tok[:, t, 416 - MQ:416], ident)
            last.then_inc(ten.sem, ten.did("codes transposed"))
            wait_all((vec, "krT"))
            pe.wait_ge(bias_loaded, 16)

            def scores(u):
                h, t = (u % 16) // 2, u % 2
                b = bank[u % 3]
                if u % 16 >= 3:
                    pe.wait_ge(sca.sem, sca.at(f"exp {u - 3}"))
                if u < 16:
                    s = slice(HD * (h % 2), HD * (h % 2) + HD)
                    mm(b[:, :], qaT[s, h // 2, t * P:(t + 1) * P], kaT[s, h // 2, :], start=True, stop=False)
                    last = mm(b[:, SEQ:], ident, bias[:, t, h, :], start=False, stop=True)
                else:
                    last = mm(b[:, :], qmT[0:MQ, h, t * P:(t + 1) * P], kmT[0:MQ, h, :], start=True, stop=True)
                last.then_inc(ten.sem, ten.did(f"scores {u}"))

            def transposed(u):
                pe.wait_ge(sca.sem, sca.at(f"exp {u}"))
                if u % 16 >= 2:
                    wait_all((probs_got_by(u - 2), f"probsT {u - 2}"))
                for k in range(4):
                    last = tr(bank[3 + u % 2][:, k * P:(k + 1) * P], probs[:, u % 3, k * P:(k + 1) * P], ident)
                last.then_inc(ten.sem, ten.did(f"probs transposed {u}"))

            def attend(u):
                h = (u % 16) // 2
                v = va if u < 16 else vm
                wait_all((probs_got_by(u), f"probsT {u}"))
                if u % 16 >= 2:
                    wait_all((vec, f"o {u - 2}"))
                for k in range(4):
                    last = mm(bank[5 + u % 2][:, 0:HD], probsT[:, u % 2, k * P:(k + 1) * P], v[:, k, h * HD:(h + 1) * HD],
                              start=k == 0, stop=k == 3)
                last.then_inc(ten.sem, ten.did(f"attended {u}", *["attended"] * (u == 31)))

            def units(first, mods):
                scores(first)
                scores(first + 1)
                transposed(first)
                for u in range(first, first + 16):
                    if u + 2 < first + 16:
                        scores(u + 2)
                    if u + 1 < first + 16:
                        transposed(u + 1)
                    if mods:
                        mod_chunk(*mods.pop(0))
                    attend(u)

            units(0, [(0, i) for i in range(4, 12)] + [(1, 0), (1, 1)])

            wait_all((vec, "o 15"), (vec, "krT"), (pol, "kmT rope"))
            w = landed(("up",))
            wv = w[:, 1536:2560].rearrange("p (h t d) -> p h t d", h=HEADS, t=2)
            for n, g in enumerate(UP_GROUPS):
                b = bank_free(UP_GROUPS, n)
                if g[0] == "qup":
                    t, half = g[1:]
                    for k in range(2):
                        last = mm(b[:, 0:384], qcT[:, k, t * P:(t + 1) * P], w[:, k * 768 + half * 384:k * 768 + half * 384 + 384],
                                  start=k == 0, stop=k == 1)
                elif g[0] == "v":
                    last = mm(b[:, :], kvcT[:, g[1] * P:(g[1] + 1) * P], wv[:, :, 1, :], start=True, stop=True)
                elif g[0] == "kn":
                    last = mm(b[0:HD, :], wv[:, g[1], 0, :], kvcT, start=True, stop=True)
                else:
                    if g[1] == 0:
                        wait_all((vec, "q rope"))
                    for j in range(2):
                        for t in range(TT):
                            h = 2 * g[1] + j
                            last = tr(b[0:MQ, j * SEQ + t * P:j * SEQ + (t + 1) * P], qm_tok[:, t, h * MQ:(h + 1) * MQ], ident)
                last.then_inc(ten.sem, ten.did(f"full {g}", *[used(("up",))] * (g == ("kn", 7))))
            for g in UP_GROUPS[-7:]:
                n = UP_GROUPS.index(g)
                wait_all((sca if by_scalar(n) else vec, f"got {g}"))
            units(16, [(1, i) for i in range(2, 12)])

            wait_all((vec, "o 31"), (vec, "mod all"))
            for b in range(4):
                for j in range(2):
                    for t in range(TT):
                        k = 2 * b + j
                        last = tr(bank[b][:, j * SEQ + t * P:j * SEQ + (t + 1) * P], o_tok[:, t, k * P:(k + 1) * P], ident)
                last.then_inc(ten.sem, ten.did(f"o transposed {b}"))
            wait_all((vec, "oT 2"), (sca, "oT 3"))
            for half in range(2):
                w = rows(landed(("out", half)))
                for t in range(TT):
                    for k in range(KT):
                        last = mm(bank[4 + 2 * t + half][:, :], oT[:, k, t * P:(t + 1) * P], w[:, k, :],
                                  start=k == 0, stop=k == KT - 1)
                last.then_inc(ten.sem, ten.did(used(("out", half)), *["y 0"] * (half == 1)))

            def gate_rows(n):
                for k in range(KT):
                    wait_all((vec, f"diag {n} {k}"))
                    last = mm(bank[k // 4][:, (k % 4) * P:(k % 4 + 1) * P], ones, diag[k % 2], start=True, stop=True)
                    last.then_inc(ten.sem, ten.did(f"gate {n} {k}"))

            def transpose_x(n):
                wait_all((vec, f"norm {n} 1"))
                for b in range(4):
                    for j in range(2):
                        for t in range(TT):
                            k = 2 * b + j
                            last = tr(bank[b][:, j * SEQ + t * P:j * SEQ + (t + 1) * P], x[:, t, k * P:(k + 1) * P], ident)
                    last.then_inc(ten.sem, ten.did(f"x {n} transposed {b}"))

            gate_rows(0)
            wait_all((sca, "gate row 0"))
            gate_rows(1)
            wait_all((sca, "gate row 1"))
            transpose_x(0)
            wait_all((sca, "hT 0 3"), (vec, "hT 0 2"))
            for c in FFN_ORDER:
                w = landed(("ffn",) + c)
                if c[0] == "gu":
                    i = c[1]
                    if i >= 2:
                        wait_all((vec, f"hid {i - 2}"))
                    w4 = w.rearrange("p (k s n) -> p k s n", k=KT, s=2)
                    for s in range(2):
                        for j in range(2):
                            for k in range(KT):
                                last = mm(bank[2 * (i % 2) + s][:, j * SEQ:(j + 1) * SEQ], w4[:, k, s, j * P:(j + 1) * P],
                                          hT[:, k, :], start=k == 0, stop=k == KT - 1)
                    last.then_inc(ten.sem, ten.did(f"gu {i}", used(("ffn",) + c)))
                else:
                    fs = range(4 * c[1], min(4 * c[1] + 4, FT))
                    wait_all((vec, f"hid {fs[-1] // 2}"))
                    for f in fs:
                        for t in range(TT):
                            for half in range(2):
                                at = (f % 4) * D + half * 512
                                last = mm(bank[4 + 2 * t + half][:, :], hid[:, f, t * P:(t + 1) * P], w[:, at:at + 512],
                                          start=f == 0, stop=f == FT - 1)
                    last.then_inc(ten.sem, ten.did(used(("ffn",) + c), *["y 1"] * (fs[-1] == FT - 1)))

            gate_rows(2)
            wait_all((sca, "gate row 2"))
            transpose_x(1)
            w = landed(("pool",))
            for g in range(4):
                wait_all((vec, f"mixT {g}"))
                for t in range(TT):
                    for k in range(2):
                        last = mm(bank[4 + 2 * t + g // 2][:, (g % 2) * 256:(g % 2) * 256 + 256],
                                  mixT[:, 2 * g + k, t * P:(t + 1) * P], w[:, (2 * g + k) * 256:(2 * g + k + 1) * 256],
                                  start=k == 0, stop=k == 1)
            last.then_inc(ten.sem, ten.did("y 2"))
            gate_rows(3)
            wait_all((sca, "gate row 3"))
            transpose_x(2)
            wait_all((sca, "hT 2 3"), (vec, "hT 2 2"))
            for t in range(TT):
                for k in range(KT):
                    last = mm(bank[4][:, t * 8:t * 8 + 8], hT[:, k, t * P:(t + 1) * P], w[:, 2048 + 8 * k:2048 + 8 * k + 8],
                              start=k == 0, stop=k == KT - 1)
            last.then_inc(ten.sem, ten.did("logits", used(("pool",))))
            wait_all((vec, "selected"))
            before = con("before")
            sel = [route[:, 11, 8 * t:8 * t + 8] for t in range(TT)]
            mm(bank[5][:, 0:8], before, sel[0], start=True, stop=True)
            mm(bank[5][:, 8:16], ones, sel[0], start=True, stop=False)
            mm(bank[5][:, 8:16], before, sel[1], start=False, stop=True)
            mm(bank[5][:, 16:24], ones, sel[0], start=True, stop=False)
            mm(bank[5][:, 16:24], ones, sel[1], start=False, stop=True).then_inc(ten.sem, ten.did("places"))

            wait_all((vec, "passes"))
            passes = pe.value_load(n_passes[0:1, 0:1], min_val=1, max_val=PASSES_MAX)
            pe.sem_inc(ten_b.sem, ten_b.per)

            def scatter(j):
                for t in range(TT):
                    for half in range(2):
                        if t == 1:
                            pe.wait_ge(vec_b.sem, vec_b.at(f"added {half}", j))
                        mm(bank[6 + half][:, :], spread[:, t * P:(t + 1) * P], outE[:, half * 512:half * 512 + 512],
                           start=True, stop=True).then_inc(ten_b.sem, ten_b.did(f"scattered {2 * t + half}"))

            with pe.Fori(0, passes) as p:
                with pe.Fori(0, EXPERTS) as e:
                    j = p * EXPERTS + e
                    pe.wait_ge(vec_b.sem, vec_b.at("picked", j))
                    pe.wait_ge(vec_b.sem, vec_b.was("xgT", j))
                    pe.wait_ge(sca_b.sem, sca_b.was("xgT", j))
                    for b in range(2):
                        for i in range(4):
                            k = 4 * b + i
                            for t in range(TT):
                                last = mm(bank[b][:, i * P:(i + 1) * P], x[:, t, k * P:(k + 1) * P], pick[:, t, :],
                                          start=t == 0, stop=t == TT - 1)
                        last.then_inc(ten_b.sem, ten_b.did(f"gathered {b}"))
                    pe.wait_ge(vec_b.sem, vec_b.was("outE", j))
                    pe.wait_ge(sca_b.sem, sca_b.was("outE", j))
                    pe.wait_ge(vec_b.sem, vec_b.was("added 3", j))
                    scatter(j)
                    pe.wait_ge(vec_b.sem, vec_b.at("pickg", j))
                    pe.wait_ge(vec_b.sem, vec_b.was("hid 13", j))
                    for t in range(TT):
                        last = tr(bank[3][:, t * P:(t + 1) * P], pickg[:, t, :], ident)
                    last.then_inc(ten_b.sem, ten_b.did("spread"))
                    pe.wait_ge(sca_b.sem, sca_b.at("xgT", j))
                    pe.wait_ge(vec_b.sem, vec_b.at("xgT", j))
                    for c in MOE_ORDER:
                        n = EXPERT_AT[c]
                        pe.wait_ge(landed_b[n % RING], j * (16 * N_EXPERT // RING) + 16 * (n // RING + 1))
                        w = slot(n)
                        if c[0] == "gu":
                            i = c[1]
                            b = bank[2 + i % 2]
                            if i >= 2:
                                pe.wait_ge(vec_b.sem, vec_b.at(f"hid {i - 2}", j))
                            elif i == 1:
                                pe.wait_ge(sca_b.sem, sca_b.at("spread", j))
                            w4 = w.rearrange("p (k s n) -> p k s n", k=KT, s=2)
                            for s in range(2):
                                for f in range(2):
                                    for k in range(KT):
                                        at = (2 * s + f) * SLOTS
                                        last = mm(b[:, at:at + SLOTS], w4[:, k, s, f * P:(f + 1) * P], xgT[:, k, :],
                                                  start=k == 0, stop=k == KT - 1)
                            last.then_inc(ten_b.sem, ten_b.did(f"gu {i}", f"used {n}"))
                        else:
                            fs = range(4 * c[1], 4 * c[1] + 4)
                            pe.wait_ge(vec_b.sem, vec_b.at(f"hid {fs[-1] // 2}", j))
                            for f in fs:
                                for half in range(2):
                                    at = (f % 4) * D + half * 512
                                    last = mm(bank[4 + half][:, :], hidE[:, f, :], w[:, at:at + 512],
                                              start=f == 0, stop=f == EFT - 1)
                            last.then_inc(ten_b.sem, ten_b.did(f"used {n}", *["y"] * (fs[-1] == EFT - 1)))
            turns = passes * EXPERTS
            pe.wait_ge(vec_b.sem, vec_b.was("outE", turns))
            pe.wait_ge(sca_b.sem, sca_b.was("outE", turns))
            pe.wait_ge(vec_b.sem, vec_b.was("added 3", turns))
            for t in range(TT):
                for half in range(2):
                    b = bank[(6, 7, 0, 1)[2 * t + half]]
                    last = mm(b[:, :], spread[:, t * P:(t + 1) * P], outE[:, half * 512:half * 512 + 512], start=True, stop=True)
            last.then_inc(ten_f.sem, ten_f.did("scattered"))

            for i in range(RING):
                pe.wait_ge(landed_b[i], passes * (16 * EXPERTS * N_EXPERT // RING) + 16)
                pe.sem_inc(landed_c[i], 16)
            pe.wait_ge(vec_f.sem, vec_f.at("x"))
            pe.sem_inc(ten_c.sem, ten_c.per)
            with pe.Fori(0, 2) as l:

                def chunk(c):
                    n = LAYER_AT[c]
                    pe.wait_ge(landed_c[n % RING], layer_landed(n, l))
                    return slot(n)

                def done(*names):
                    return ten_c.did(*names)

                def used_c(c):
                    return f"used {LAYER_AT[c]}"

                def wait(who, name):
                    pe.wait_ge(who.sem, who.at(name, l))

                def transpose_scaled(name):
                    wait(sca_c, f"{name} scaled")
                    for b in range(4):
                        for j in range(2):
                            for t in range(TT):
                                k = 2 * b + j
                                last = tr(bank[b][:, j * SEQ + t * P:j * SEQ + (t + 1) * P], tmp[:, t, k * P:(k + 1) * P], ident)
                        last.then_inc(ten_c.sem, done(f"{name} transposed {b}"))

                def by_tokens(c, name, first, width):
                    w = chunk(("mix", c))
                    w = w[:, 0:KT * width].rearrange("p (k n) -> p k n", k=KT)
                    for t in range(TT):
                        for k in range(KT):
                            last = mm(bank[first + t][:, 0:width], hT[:, k, t * P:(t + 1) * P], w[:, k, :],
                                      start=k == 0, stop=k == KT - 1)
                        last.then_inc(ten_c.sem, done(f"{name} {t}", *[used_c(("mix", c))] * (t == 1)))

                def by_features(c, name, first):
                    w = rows(chunk(("mix", c)))
                    for i in range(2):
                        for s in range(2):
                            for k in range(KT):
                                last = mm(bank[first + i][:, s * SEQ:(s + 1) * SEQ], w[:, k, s * 256 + i * P:s * 256 + (i + 1) * P],
                                          hT[:, k, :], start=k == 0, stop=k == KT - 1)
                        last.then_inc(ten_c.sem, done(f"{name} {i}", *[used_c(("mix", c))] * (i == 1)))

                pe.wait_ge(vec_c.sem, vec_c.was("x 1", l))
                transpose_scaled("mix")
                wait(vec_c, "mix hT 2")
                wait(sca_c, "mix hT 3")
                by_tokens("qi", "qi", 4, QI_W)
                by_features("dd", "dd", 6)
                wait(vec_c, "qi rope")
                for t in range(TT):
                    for i in range(2):
                        tr(bank[0][:, i * SEQ + t * P:i * SEQ + (t + 1) * P], qir[:, t, i * P:(i + 1) * P], ident)
                for t in range(TT):
                    last = tr(bank[1][:, t * P:(t + 1) * P], qir[:, t, 2 * P:3 * P], ident)
                last.then_inc(ten_c.sem, done("qi transposed"))
                wait(sca_c, "qi got 1")
                by_tokens("qk", "qk", 4, 512)
                wait(sca_c, "qiT")
                for t in range(TT):
                    for i in range(4):
                        s = slice(HD * (i % 2), HD * (i % 2) + HD)
                        last = mm(bank[2 + (i % 2) - 2 * t][:, (i // 2) * SEQ:(i // 2 + 1) * SEQ],
                                  qiT[s, i // 2, t * P:(t + 1) * P], kiT[s, :], start=True, stop=True)
                    last.then_inc(ten_c.sem, done(f"index scores {t}"))
                wait(sca_c, "sig 1")
                wait(vec_c, "yp 1")
                by_tokens("vg", "vg", 6, 512)
                wait(sca_c, "rel 0")
                by_features("ch", "ch", 2)
                wait(vec_c, "qk got 1")
                by_features("bu", "bu", 4)
                wait(vec_c, "qk rope")
                wait(sca_c, "rel 1")
                for i in range(2):
                    for t in range(TT):
                        tr(bank[0][:, i * SEQ + t * P:i * SEQ + (t + 1) * P], qkr[:, t, i * P:(i + 1) * P], ident)
                        last = tr(bank[1][:, i * SEQ + t * P:i * SEQ + (t + 1) * P], qkr[:, t, 256 + i * P:256 + (i + 1) * P], ident)
                last.then_inc(ten_c.sem, done("qk transposed"))
                wait(vec_c, "vn")
                wait(sca_c, "vg got 1")
                for h in range(4):
                    for t in range(TT):
                        s = slice(HD * (h % 2), HD * (h % 2) + HD)
                        last = mm(bank[6 + h // 2][s, t * P:(t + 1) * P], vn[:, t, h * HD:(h + 1) * HD], wsm[:, h, :],
                                  start=True, stop=True)
                last.then_inc(ten_c.sem, done("gated"))
                wait(vec_c, "conv 1")
                wait(vec_c, "ch got 1")
                for t in range(TT):
                    for i in range(2):
                        last = tr(bank[2][:, t * SEQ + i * P:t * SEQ + (i + 1) * P], conv[:, i, t * P:(t + 1) * P], ident)
                last.then_inc(ten_c.sem, done("conv transposed"))
                wait(vec_c, "ynorm 1")
                for t in range(TT):
                    for i in range(2):
                        last = tr(bank[3][:, i * SEQ + t * P:i * SEQ + (t + 1) * P], ynorm[:, t, i * P:(i + 1) * P], ident)
                last.then_inc(ten_c.sem, done("ynorm transposed"))

                wait(vec_c, "kT")
                wait(sca_c, "qT")
                wait(vec_c, "y_b 1")
                wait(sca_c, "bu got 1")

                def scores_c(u):
                    h, t = u // 2, u % 2
                    if u >= 3:
                        wait(vec_c, f"masked {u - 3}")
                    s = slice(HD * (h % 2), HD * (h % 2) + HD)
                    mm(bank[u % 3][:, 0:SEQ], qT[s, h // 2, t * P:(t + 1) * P], kT[s, h // 2, :], start=True, stop=True)\
                        .then_inc(ten_c.sem, done(f"scores {u}"))

                def transposed_c(u):
                    wait(sca_c, f"exp {u}")
                    if u >= 2:
                        wait(sca_c, f"probsT {u - 2}")
                    for k in range(TT):
                        last = tr(bank[4 + u % 2][:, k * P:(k + 1) * P], probs2[:, u % 3, k * P:(k + 1) * P], ident)
                    last.then_inc(ten_c.sem, done(f"probs transposed {u}"))

                def attend_c(u):
                    h = u // 2
                    wait(sca_c, f"probsT {u}")
                    if u >= 2:
                        wait(vec_c, f"o {u - 2}")
                    for k in range(TT):
                        last = mm(bank[6 + u % 2][:, 0:HD], probsT2[:, u % 2, k * P:(k + 1) * P],
                                  vg_tok[:, k, h * HD:(h + 1) * HD], start=k == 0, stop=k == 1)
                    last.then_inc(ten_c.sem, done(f"attended {u}"))

                scores_c(0)
                scores_c(1)
                transposed_c(0)
                for u in range(8):
                    if u + 2 < 8:
                        scores_c(u + 2)
                    if u + 1 < 8:
                        transposed_c(u + 1)
                    attend_c(u)
                wait(vec_c, "o 7")
                for i in range(2):
                    for t in range(TT):
                        last = tr(bank[0][:, i * SEQ + t * P:i * SEQ + (t + 1) * P], o_c[:, t, i * P:(i + 1) * P], ident)
                last.then_inc(ten_c.sem, done("o transposed"))
                wait(sca_c, "y_d 1")
                wait(vec_c, "y_c")
                for half in range(2):
                    w = rows(chunk(("out", half)))
                    for t in range(TT):
                        for k in range(KT):
                            last = mm(bank[4 + 2 * t + half][:, :], catT[:, k, t * P:(t + 1) * P], w[:, k, :],
                                      start=k == 0, stop=k == KT - 1)
                    last.then_inc(ten_c.sem, done(used_c(("out", half)), *["y 0"] * (half == 1)))
                transpose_scaled("ffn")
                wait(vec_c, "ffn hT 2")
                wait(sca_c, "ffn hT 3")
                for c in FFN_ORDER:
                    w = chunk(("ffn",) + c)
                    if c[0] == "gu":
                        i = c[1]
                        if i >= 2:
                            wait(vec_c, f"hid {i - 2}")
                        w4 = w.rearrange("p (k s n) -> p k s n", k=KT, s=2)
                        for s in range(2):
                            for j in range(2):
                                for k in range(KT):
                                    last = mm(bank[2 * (i % 2) + s][:, j * SEQ:(j + 1) * SEQ], w4[:, k, s, j * P:(j + 1) * P],
                                              hT[:, k, :], start=k == 0, stop=k == KT - 1)
                        last.then_inc(ten_c.sem, done(f"gu {i}", used_c(("ffn",) + c)))
                    else:
                        fs = range(4 * c[1], min(4 * c[1] + 4, FT))
                        wait(vec_c, f"hid {fs[-1] // 2}")
                        for f in fs:
                            for t in range(TT):
                                for half in range(2):
                                    at = (f % 4) * D + half * 512
                                    last = mm(bank[4 + 2 * t + half][:, :], hid[:, f, t * P:(t + 1) * P], w[:, at:at + 512],
                                              start=f == 0, stop=f == FT - 1)
                        last.then_inc(ten_c.sem, done(used_c(("ffn",) + c), *["y 1"] * (fs[-1] == FT - 1)))
        def gate_col(n, k):
            layer, part = n // 2, n % 2
            return mod[:, layer, 16 + 24 * part + k, 0:1]

        @block.vector
        def _(dve):
            v = nc.vector

            def hold():
                dve.wait_ge(vec.sem, vec.last())

            def after(*whos):
                for who, name in whos:
                    dve.wait_ge(who.sem, who.at(name))

            def sign(ins, *names):
                ins.then_inc(vec.sem, vec.did(*names))

            dve.wait_ge(in_loaded, 64)
            after((ten, "used 3"))
            modb = [cols[:, COLS[f"modb{i}"][0]:COLS[f"modb{i}"][0] + 48] for i in range(2)]

            def mod_out(layer, j0, j1, plus_one, *names):
                n = j1 - j0
                src = bank[7][:, layer * 96 + 2 * j0:layer * 96 + 2 * j1].rearrange("p (j c) -> p j c", c=2)
                v.tensor_tensor(mod[:, layer, j0:j1, :], src, modb[layer][:, j0:j1].unsqueeze(2).broadcast_to([P, n, 2]), ALU.add)\
                    .then_inc(vec.sem, vec.did())
                hold()
                for i, j in enumerate(plus_one):
                    v.tensor_scalar(mod[:, layer, j:j + 8, :], mod[:, layer, j:j + 8, :], 1.0, None, ALU.add)\
                        .then_inc(vec.sem, vec.did(*names * (i == len(plus_one) - 1)))

            mod_out(0, 0, 16, [8], "mod 0 first")
            hold()

            def got(groups, n):
                after((ten, f"full {groups[n]}"))
                return bank[n % 7], f"got {groups[n]}"

            for n, g in enumerate(GROUPS):
                if by_scalar(n):
                    continue
                b, name = got(GROUPS, n)
                if g[0] == "h":
                    k = g[1]
                    for c in range(2):
                        v.tensor_scalar(hT4[:, k, (1 - c) * SEQ:(2 - c) * SEQ], b[:, (1 - c) * SEQ:(2 - c) * SEQ],
                                        mod[:, 0, 8 + k, c:c + 1], mod[:, 0, k, c:c + 1], ALU.mult, ALU.add)\
                            .then_inc(vec.sem, vec.did(*[name] * c))
                elif g[0] == "c":
                    t, c0 = g[1], 256 if g[1] < 2 else 0
                    v.tensor_copy(c_tok[:, t, c0:], b[:, c0:416]).then_inc(vec.sem, vec.did(name))
                elif g[0] == "ka":
                    v.tensor_copy(kaT[:, g[1], :], b[:, :]).then_inc(vec.sem, vec.did(name))
                elif g[0] == "qa":
                    v.tensor_scalar(qaT[:, 2 * g[1]:2 * g[1] + 2, :], b[:, :].rearrange("p (j n) -> p j n", j=2),
                                    NA_SCALE, None, ALU.mult).then_inc(vec.sem, vec.did(name))
                else:
                    v.tensor_copy(va[:, g[1], :], b[:, :]).then_inc(vec.sem, vec.did(name))

            after((sca, f"got {('c', 1)}"), (sca, f"got {('c', 3)}"))
            hold()
            parts = [(2, 0, 256), (3, 0, 256)] + [(t, 256, 384) for t in range(4)]
            for i, (t, a, b) in enumerate(parts):
                v.tensor_tensor_reduce(out=probs[:, 0, 0:b - a], in0=c_tok[:, t, a:b], in1=c_tok[:, t, a:b], scale=1.0,
                                       scalar=0.0, op0=ALU.mult, op1=ALU.add, accum_out=stat[:, 16 + i:17 + i])\
                    .then_inc(vec.sem, vec.did())
                hold()
            v.tensor_scalar(stat[:, 0:2], stat[:, 16:18], 1.0 / 256, RMS_EPS, ALU.mult, ALU.add).then_inc(vec.sem, vec.did())
            v.tensor_scalar(stat[:, 2:6], stat[:, 18:22], 1.0 / 128, RMS_EPS, ALU.mult, ALU.add)\
                .then_inc(vec.sem, vec.did("power c wanted"))
            kr = c_tok[:, 2:4, 384:416]
            kr5 = kr.rearrange("p t (a s f) -> p t a s f", a=2, s=2)
            ra = rope_a[:, 0:64].rearrange("p (t n) -> p t n", t=2)
            ra5 = ra.rearrange("p t (a s f) -> p t a s f", a=2, s=2)
            rb = [rope_b[:, 32 * i:32 * i + 32].rearrange("p (t a f) -> p t a f", t=2, a=2) for i in range(2)]
            msin = con("msin", 2, 2, 8)
            mcos = con("mcos", 2, 32)
            v.tensor_tensor(ra, kr, mcos, ALU.mult).then_inc(vec.sem, vec.did())
            v.tensor_tensor(rb[0], kr5[:, :, :, 1, :], msin, ALU.mult).then_inc(vec.sem, vec.did())
            v.tensor_tensor(rb[1], kr5[:, :, :, 0, :], msin, ALU.mult).then_inc(vec.sem, vec.did())
            hold()
            v.tensor_tensor(kr5[:, :, :, 0, :], ra5[:, :, :, 0, :], rb[0], ALU.subtract).then_inc(vec.sem, vec.did())
            v.tensor_tensor(kr5[:, :, :, 1, :], ra5[:, :, :, 1, :], rb[1], ALU.add).then_inc(vec.sem, vec.did())
            after((pol, "power c"))
            for i, (t, a, b) in enumerate(parts):
                v.tensor_scalar(c_tok[:, t, a:b], c_tok[:, t, a:b], stat[:, 8 + i:9 + i], None, ALU.mult)\
                    .then_inc(vec.sem, vec.did(*["codes normed"] * (i == 5)))
            after((ten, "codes transposed"))
            for j in range(2):
                v.tensor_scalar(qcT[:, j, :], bank[0][:, j * SEQ:(j + 1) * SEQ], col("qn", j), None, ALU.mult)\
                    .then_inc(vec.sem, vec.did())
            v.tensor_scalar(kvcT, bank[1][:, :], col("kvn"), None, ALU.mult).then_inc(vec.sem, vec.did())
            v.tensor_copy(krT[HD:MQ, :], bank[2][HD:MQ, :]).then_inc(vec.sem, vec.did("krT"))

            def peak(u):
                after((ten, f"scores {u}"))
                v.tensor_reduce(nmax[:, u:u + 1], bank[u % 3][:, :], axis=AX_X, op=ALU.max, negate=True)\
                    .then_inc(vec.sem, vec.did(f"nmax {u}"))

            def probs_out(u):
                if u % 2 == 0:
                    after((ten, f"probs transposed {u}"))
                    if u >= 2:
                        after((ten, f"attended {u - 2}"))
                    v.tensor_copy(probsT[:, u % 2, :], bank[3 + u % 2][:, :]).then_inc(vec.sem, vec.did(f"probsT {u}"))

            def o_out(u):
                h, t = (u % 16) // 2, u % 2
                after((sca, f"exp {u}"))
                v.reciprocal(rinv[:, u:u + 1], rsum[:, u:u + 1]).then_inc(vec.sem, vec.did())
                after((ten, f"attended {u}"))
                hold()
                at = h * HD + (u // 16) * 512
                v.tensor_scalar(o_tok[:, t, at:at + HD], bank[5 + u % 2][:, 0:HD], rinv[:, u:u + 1], None, ALU.mult)\
                    .then_inc(vec.sem, vec.did(f"o {u}"))

            def units(first):
                peak(first)
                peak(first + 1)
                probs_out(first)
                for u in range(first, first + 16):
                    if u + 2 < first + 16:
                        peak(u + 2)
                    if u + 1 < first + 16:
                        probs_out(u + 1)
                    o_out(u)

            units(0)
            for n, g in enumerate(UP_GROUPS):
                if not by_scalar(n):
                    b, name = got(UP_GROUPS, n)
                    if g[0] == "qup":
                        v.tensor_scalar(qm_tok[:, g[1], g[2] * 384:g[2] * 384 + 384], b[:, 0:384], MLA_SCALE, None, ALU.mult)\
                            .then_inc(vec.sem, vec.did(name))
                    elif g[0] == "v":
                        v.tensor_copy(vm[:, g[1], :], b[:, :]).then_inc(vec.sem, vec.did(name))
                    elif g[0] == "kn":
                        v.tensor_copy(kmT[0:HD, g[1], :], b[0:HD, :]).then_inc(vec.sem, vec.did(name))
                    else:
                        v.tensor_copy(qmT[0:MQ, 2 * g[1]:2 * g[1] + 2, :], b[0:MQ, :].rearrange("p (j n) -> p j n", j=2))\
                            .then_inc(vec.sem, vec.did(name))
                if g == ("qup", 1, 1):
                    after((sca, f"got {('qup', 0, 1)}"), (sca, f"got {('qup', 1, 1)}"))
                    for t in range(TT):
                        q = qm_tok[:, t, :].rearrange("p (h c) -> p h c", h=HEADS)[:, :, HD:MQ]
                        q5 = q.rearrange("p h (a s f) -> p h a s f", a=2, s=2)
                        ra = rope_a.rearrange("p (h n) -> p h n", h=HEADS)
                        ra5 = ra.rearrange("p h (a s f) -> p h a s f", a=2, s=2)
                        rb = [rope_b[:, 128 * i:128 * i + 128].rearrange("p (h a f) -> p h a f", h=HEADS, a=2) for i in range(2)]
                        hold()
                        v.tensor_tensor(ra, q, mcos[:, t, :].unsqueeze(1).broadcast_to([P, HEADS, ROPE_D]), ALU.mult)\
                            .then_inc(vec.sem, vec.did())
                        s = msin[:, t, :, :].unsqueeze(1).broadcast_to([P, HEADS, 2, 8])
                        v.tensor_tensor(rb[0], q5[:, :, :, 1, :], s, ALU.mult).then_inc(vec.sem, vec.did())
                        v.tensor_tensor(rb[1], q5[:, :, :, 0, :], s, ALU.mult).then_inc(vec.sem, vec.did())
                        hold()
                        v.tensor_tensor(q5[:, :, :, 0, :], ra5[:, :, :, 0, :], rb[0], ALU.subtract).then_inc(vec.sem, vec.did())
                        v.tensor_tensor(q5[:, :, :, 1, :], ra5[:, :, :, 1, :], rb[1], ALU.add)\
                            .then_inc(vec.sem, vec.did(*["q rope"] * (t == 1)))
            units(16)
            after((ten, f"used {FIRST_AT[('mod', 1, 11)]}"))
            mod_out(0, 16, 48, [32])
            mod_out(1, 0, 48, [8, 32], "mod all")
            for b in range(0, 4, 2):
                after((ten, f"o transposed {b}"))
                v.tensor_copy(oT[:, 2 * b:2 * b + 2, :], bank[b][:, :].rearrange("p (j n) -> p j n", j=2))\
                    .then_inc(vec.sem, vec.did(f"oT {b}"))

            def diagonals(n):
                for k in range(KT):
                    if k >= 2:
                        after((ten, f"gate {n} {k - 2}"))
                    elif n:
                        after((ten, f"gate {n - 1} {k + 6}"))
                    extra = (col("pscale", k), ALU.mult) if n == 2 else (None,)
                    v.tensor_scalar(diag[k % 2], ident, gate_col(n, k), extra[0], ALU.mult, *extra[1:])\
                        .then_inc(vec.sem, vec.did(f"diag {n} {k}"))

            def layer_norm(n, y, seq, powered, rows, last_names):
                def own():
                    dve.wait_ge(seq.sem, seq.last())

                for t in range(TT):
                    for half in range(2):
                        c = slice(half * 512, half * 512 + 512)
                        v.tensor_tensor(tmp[:, t, c], y(t, half), gate_row[n % 2][:, c], ALU.mult).then_inc(seq.sem, seq.did())
                own()
                for t in range(TT):
                    v.scalar_tensor_tensor(x[:, t, :], x[:, t, :], ALPHA, tmp[:, t, :], ALU.mult, ALU.add)\
                        .then_inc(seq.sem, seq.did())
                own()
                bn = view(stat, 64, TT, 2, 6)
                mv = view(stat, 88, TT, 2)
                for t in range(TT):
                    for half in range(2):
                        v.bn_stats(bn[:, t, half, :], x[:, t, half * 512:half * 512 + 512]).then_inc(seq.sem, seq.did())
                own()
                for t in range(TT):
                    v.bn_aggr(mv[:, t, :], bn[:, t, :, :].rearrange("p a b -> p (a b)")).then_inc(seq.sem, seq.did())
                own()
                for t in range(TT):
                    v.tensor_scalar(stat[:, 32 + t:33 + t], mv[:, t, 1:2], LN_EPS, None, ALU.add)\
                        .then_inc(seq.sem, seq.did(powered[0].format(t=t)))
                for t in range(TT):
                    who = powered[2]
                    dve.wait_ge(who.sem, who.at(powered[1].format(t=t)))
                    v.tensor_scalar(x[:, t, :], x[:, t, :], mv[:, t, 0:1], stat[:, 40 + t:41 + t], ALU.subtract, ALU.mult)\
                        .then_inc(seq.sem, seq.did())
                dve.wait_ge(rows_loaded, 16 * rows)
                own()
                for t in range(TT):
                    v.tensor_tensor(x[:, t, :], x[:, t, :], ln_g, ALU.mult).then_inc(seq.sem, seq.did())
                own()
                for t in range(TT):
                    v.tensor_tensor(x[:, t, :], x[:, t, :], ln_b, ALU.add).then_inc(seq.sem, seq.did(last_names[t]))
                own()

            def first_norm(n):
                after((ten, f"y {n}"), (sca, f"gate row {n}"))
                layer_norm(n, lambda t, half: bank[4 + 2 * t + half][:, :], vec,
                           (f"power norm {n} {{t}} wanted", f"power norm {n} {{t}}", pol), n + 1,
                           [f"norm {n} {t}" for t in range(TT)])

            hold()
            diagonals(0)
            diagonals(1)
            first_norm(0)
            for b in range(0, 4, 2):
                after((ten, f"x 0 transposed {b}"))
                for j in range(2):
                    k = 2 * b + j
                    v.tensor_scalar(hT[:, k, :], bank[b][:, j * SEQ:(j + 1) * SEQ], mod[:, 0, 32 + k, 0:1],
                                    mod[:, 0, 24 + k, 0:1], ALU.mult, ALU.add)\
                        .then_inc(vec.sem, vec.did(*[f"hT 0 {b}"] * j))
            for i in range(FT // 2):
                after((sca, f"silu {i}"))
                v.tensor_tensor(hid[:, 2 * i:2 * i + 2, :], silu[:, i % 2, :].rearrange("p (j n) -> p j n", j=2),
                                bank[2 * (i % 2) + 1][:, :].rearrange("p (j n) -> p j n", j=2), ALU.mult)\
                    .then_inc(vec.sem, vec.did(f"hid {i}"))
            diagonals(2)
            first_norm(1)

            v.memset(hp[:, :, 0:HALO], 0.0).then_inc(vec.sem, vec.did())
            v.memset(hp[:, :, HALO + SEQ:], 0.0).then_inc(vec.sem, vec.did())
            for b in range(0, 4, 2):
                after((ten, f"x 1 transposed {b}"))
                for j in range(2):
                    k = 2 * b + j
                    v.tensor_scalar(hp[:, k, HALO:HALO + SEQ], bank[b][:, j * SEQ:(j + 1) * SEQ], mod[:, 1, 8 + k, 0:1],
                                    mod[:, 1, k, 0:1], ALU.mult, ALU.add)\
                        .then_inc(vec.sem, vec.did(*[f"hT 1 {b}"] * j))
            n_pool = FIRST_AT[("pool",)]
            dve.wait_ge(landed_a[n_pool % RING], 16 * (n_pool // RING + 1))
            inv = slot(n_pool)[:, INV_AT:INV_AT + 1024].rearrange("p (g n) -> p g n", g=4)
            L = SEQ + 2 * HALO
            for g in range(4):
                if g % 2:
                    after((sca, f"hT 1 {g}"))
                hold()
                h = hp[:, 2 * g:2 * g + 2, :]
                v.tensor_tensor(win[0][:, :, 1:L], h[:, :, 0:L - 1], h[:, :, 1:L], ALU.add).then_inc(vec.sem, vec.did())
                a, edge, reach = 0, 1, 1
                for step in range(g):
                    hold()
                    lo, hi = edge + reach, L - (edge + reach - 1)
                    v.tensor_tensor(win[1 - a][:, :, lo:hi], win[a][:, :, lo - reach:hi - reach],
                                    win[a][:, :, lo + reach:hi + reach], ALU.add).then_inc(vec.sem, vec.did())
                    a, edge, reach = 1 - a, lo, 2 * reach
                hold()
                mid = slice(HALO, HALO + SEQ)
                v.tensor_tensor(win[a][:, :, mid], win[a][:, :, mid], inv[:, g, :].unsqueeze(1).broadcast_to([P, 2, SEQ]),
                                ALU.mult).then_inc(vec.sem, vec.did())
                hold()
                v.tensor_tensor(mixT[:, 2 * g:2 * g + 2, :], win[a][:, :, mid], h[:, :, mid], ALU.subtract)\
                    .then_inc(vec.sem, vec.did(f"mixT {g}"))
            diagonals(3)
            first_norm(2)
            for b in range(0, 4, 2):
                after((ten, f"x 2 transposed {b}"))
                for j in range(2):
                    k = 2 * b + j
                    v.tensor_scalar(hT[:, k, :], bank[b][:, j * SEQ:(j + 1) * SEQ], mod[:, 1, 32 + k, 0:1],
                                    mod[:, 1, 24 + k, 0:1], ALU.mult, ALU.add)\
                        .then_inc(vec.sem, vec.did(*[f"hT 2 {b}"] * j))

            def r(i):
                return route[:, i, :].rearrange("p (t e) -> p t e", t=TT)

            def over(m):
                return m.unsqueeze(2).broadcast_to([P, TT, EXPERTS])

            rev = con("rev").unsqueeze(1).broadcast_to([P, TT, EXPERTS])
            m = [stat[:, 96 + 2 * i:98 + 2 * i] for i in range(8)]

            def step(ins, *names):
                ins.then_inc(vec.sem, vec.did(*names))
                hold()

            after((ten, "logits"))
            step(v.tensor_copy(route[:, 0, :], bank[4][:, 0:16]))
            src = 0
            for i in range(2):
                step(v.tensor_reduce(m[i], r(src), axis=AX_X, op=ALU.max))
                step(v.tensor_tensor(r(1), r(src), over(m[i]), ALU.is_equal))
                step(v.tensor_tensor(r(1), r(1), rev, ALU.mult))
                step(v.tensor_reduce(m[2], r(1), axis=AX_X, op=ALU.max))
                step(v.tensor_tensor(r(2 + i), rev, over(m[2]), ALU.is_equal))
                if i == 0:
                    step(v.scalar_tensor_tensor(route[:, 4, :], route[:, 2, :], -3e38, route[:, 0, :], ALU.mult, ALU.add))
                    src = 4
            step(v.tensor_tensor(m[3], m[1], m[0], ALU.subtract), "gate exponents")
            after((sca, "gate exponentials"))
            step(v.tensor_scalar(m[5], m[4], 1.0, None, ALU.add))
            step(v.reciprocal(m[6], m[5]))
            step(v.tensor_tensor(m[7], m[4], m[6], ALU.mult))
            step(v.tensor_tensor(r(5), r(2), over(m[6]), ALU.mult))
            step(v.tensor_tensor(r(6), r(3), over(m[7]), ALU.mult))
            step(v.tensor_tensor(gates, r(5), r(6), ALU.add))
            step(v.tensor_tensor(r(11), r(2), r(3), ALU.add), "selected")
            v.memset(acc, 0.0).then_inc(vec.sem, vec.did())
            v.memset(outE, 0.0).then_inc(vec.sem, vec.did())
            v.memset(spread, 0.0).then_inc(vec.sem, vec.did())
            step(v.tensor_scalar(r(7), r(11), -1e6, 1e6, ALU.mult, ALU.add))
            after((ten, "places"))
            step(v.tensor_tensor(place, bank[5][:, 0:16].rearrange("p (t e) -> p t e", t=TT), r(7), ALU.add))
            step(v.tensor_reduce(m[0][:, 0:1], bank[5][:, 16:24], axis=AX_X, op=ALU.max))
            step(v.tensor_scalar(n_passes[:, :], m[0][:, 0:1], float(SLOTS), 1.0, ALU.is_gt, ALU.add), "passes")

            passes = dve.value_load(n_passes[0:1, 0:1], min_val=1, max_val=PASSES_MAX)
            dve.sem_inc(vec_b.sem, vec_b.per)
            with dve.Fori(0, passes) as p:
                with dve.Fori(0, EXPERTS) as e:
                    j = p * EXPERTS + e

                    def own():
                        dve.wait_ge(vec_b.sem, vec_b.last(j))

                    v.tensor_copy(now[:, 0, :].unsqueeze(2), place[:, :, bass.ds(e, 1)]).then_inc(vec_b.sem, vec_b.did())
                    v.tensor_copy(now[:, 1, :].unsqueeze(2), gates[:, :, bass.ds(e, 1)]).then_inc(vec_b.sem, vec_b.did())
                    own()
                    v.tensor_scalar(place[:, :, bass.ds(e, 1)], place[:, :, bass.ds(e, 1)], -float(SLOTS), None, ALU.add)\
                        .then_inc(vec_b.sem, vec_b.did())
                    dve.wait_ge(ten_b.sem, ten_b.was("gathered 1", j))
                    for t in range(TT):
                        v.tensor_scalar(pick[:, t, :], con("iota"), now[:, 0, t:t + 1], None, ALU.is_equal)\
                            .then_inc(vec_b.sem, vec_b.did(*["picked"] * t))
                    dve.wait_ge(ten_b.sem, ten_b.was("spread", j))
                    for t in range(TT):
                        v.tensor_scalar(pickg[:, t, :], con("iota"), now[:, 0, t:t + 1], now[:, 1, t:t + 1],
                                        ALU.is_equal, ALU.mult).then_inc(vec_b.sem, vec_b.did(*["pickg"] * t))
                    dve.wait_ge(ten_b.sem, ten_b.at("gathered 1", j))
                    for k in range(4, KT):
                        v.tensor_scalar(xgT[:, k, :], bank[1][:, (k - 4) * P:(k - 3) * P], mod[:, 1, 32 + k, 0:1],
                                        mod[:, 1, 24 + k, 0:1], ALU.mult, ALU.add)\
                            .then_inc(vec_b.sem, vec_b.did(*["xgT"] * (k == KT - 1)))
                    for i in range(4):
                        dve.wait_ge(ten_b.sem, ten_b.at(f"scattered {i}", j))
                        a = acc[:, i // 2, (i % 2) * 512:(i % 2) * 512 + 512]
                        v.tensor_tensor(a, a, bank[6 + i % 2][:, :], ALU.add).then_inc(vec_b.sem, vec_b.did(f"added {i}"))
                    for i in range(EFT // 2):
                        dve.wait_ge(sca_b.sem, sca_b.at(f"silu {i}", j))
                        v.tensor_tensor(hidE[:, 2 * i:2 * i + 2, :], siluE[:, i % 2, :].rearrange("p (j n) -> p j n", j=2),
                                        bank[2 + i % 2][:, 256:512].rearrange("p (j n) -> p j n", j=2), ALU.mult)\
                            .then_inc(vec_b.sem, vec_b.did(f"hid {i}"))
                    dve.wait_ge(ten_b.sem, ten_b.at("y", j))
                    v.tensor_copy(outE[:, 512:D], bank[5][:, :]).then_inc(vec_b.sem, vec_b.did("outE"))

            dve.wait_ge(vec_b.sem, vec_b.was("outE", passes * EXPERTS))
            dve.wait_ge(ten_f.sem, ten_f.at("scattered"))
            for i in range(4):
                a = acc[:, i // 2, (i % 2) * 512:(i % 2) * 512 + 512]
                v.tensor_tensor(a, a, bank[(6, 7, 0, 1)[i]][:, :], ALU.add).then_inc(vec_f.sem, vec_f.did())
            dve.wait_ge(vec_f.sem, vec_f.last())
            layer_norm(3, lambda t, half: acc[:, t, half * 512:half * 512 + 512], vec_f,
                       ("power wanted {t}", "power norm {t}", pol_f), 4, ["x 3 0", "x"])

            dve.sem_inc(vec_c.sem, vec_c.per)
            with dve.Fori(0, 2) as l:

                def own():
                    dve.wait_ge(vec_c.sem, vec_c.last(l))

                def wait(who, name):
                    dve.wait_ge(who.sem, who.at(name, l))

                def alone():
                    dve.sem_inc(wait_carrier, 1)

                def did(*names):
                    return vec_c.did(*names)

                S = vec_c.sem
                dve.wait_ge(landed_c[0], layer_landed(0, l))
                dve.wait_ge(sca_c.sem, sca_c.was("ffn hT 3", l))
                dve.wait_ge(ten_c.sem, ten_c.was("gated", l))
                first = slot(0)
                v.tensor_copy(par, first[:, PAR_AT:PAR_AT + N_PAR]).then_inc(S, did("par"))
                v.tensor_tensor(wsm, first[:, WS_AT:WS_AT + 4 * P].rearrange("p (h t) -> p h t", h=4),
                                con("tri").unsqueeze(1).broadcast_to([P, 4, P]), ALU.mult).then_inc(S, did())

                def power(name, at, src, scale, eps):
                    if scale is None:
                        v.tensor_scalar(stat[:, 32 + at:34 + at], src, eps, None, ALU.add).then_inc(S, did(f"power {name} wanted"))
                    else:
                        v.tensor_scalar(stat[:, 32 + at:34 + at], src, scale, eps, ALU.mult, ALU.add)\
                            .then_inc(S, did(f"power {name} wanted"))

                def scaled_out(name, gain):
                    for b in range(0, 4, 2):
                        wait(ten_c, f"{name} transposed {b}")
                        for j in range(2):
                            v.tensor_scalar(hT[:, 2 * b + j, :], bank[b][:, j * SEQ:(j + 1) * SEQ], pr(gain, 2 * b + j), None,
                                            ALU.mult).then_inc(S, did(*[f"{name} hT {b}"] * j))

                wait(sca_c, "mix squares")
                power("mix", 0, stat[:, 16:18], 1.0 / D, RMS_EPS)
                own()
                scaled_out("mix", "gmix")

                def rotate(dst, src, t, heads):
                    s4 = src.rearrange("p (h s f) -> p h s f", h=heads, s=2)
                    d4 = dst.rearrange("p (h s f) -> p h s f", h=heads, s=2)
                    a4 = rt_a[:, 0:heads * HD].rearrange("p (h s f) -> p h s f", h=heads, s=2)
                    a3 = rt_a[:, 0:heads * HD].rearrange("p (g f) -> p g f", f=32)
                    b = [rt_b[:, 256 * i:256 * i + 32 * heads].rearrange("p (h f) -> p h f", h=heads) for i in range(2)]
                    cos, sin = con("dcos", 2, 32)[:, t, :], con("dsin", 2, 32)[:, t, :]
                    v.tensor_tensor(a3, src.rearrange("p (g f) -> p g f", f=32),
                                    cos.unsqueeze(1).broadcast_to([P, 2 * heads, 32]), ALU.mult).then_inc(S, did())
                    for i in range(2):
                        v.tensor_tensor(b[i], s4[:, :, 1 - i, :], sin.unsqueeze(1).broadcast_to([P, heads, 32]), ALU.mult)\
                            .then_inc(S, did())
                    own()
                    v.tensor_tensor(d4[:, :, 0, :], a4[:, :, 0, :], b[0], ALU.subtract).then_inc(S, did())
                    v.tensor_tensor(d4[:, :, 1, :], a4[:, :, 1, :], b[1], ALU.add).then_inc(S, did())
                    own()

                wi = view(stat, 20, TT, 4)
                for t in range(TT):
                    wait(sca_c, f"qi got {t}")
                    v.tensor_scalar(wi[:, t, :], qi_tok[:, t, 320:324], 0.5 * NA_SCALE, None, ALU.mult).then_inc(S, did())
                    rotate(qir[:, t, 0:320], qi_tok[:, t, 0:320], t, 5)
                    v.tensor_copy(qir[:, t, 320:384], qir[:, t, 256:320]).then_inc(S, did(*["qi rope"] * t))
                v.memset(yp[:, :, 0:TAPS_C - 1], 0.0).then_inc(S, did())
                for i in range(2):
                    wait(sca_c, f"sig {i}")
                    v.tensor_tensor(yp[:, i, TAPS_C - 1:], bank[6 + i][:, 0:SEQ], sig[:, i, :], ALU.mult)\
                        .then_inc(S, did(f"yp {i}"))
                for t in range(TT):
                    wait(ten_c, f"qk {t}")
                    v.tensor_copy(qk_tok[:, t, :], bank[4 + t][:, :]).then_inc(S, did(f"qk got {t}"))
                top = stat[:, 104:112]
                for t in range(TT):
                    wait(sca_c, f"rel {t}")
                    s = left[:, t, :]
                    v.tensor_scalar(s, rel[:, t, 0, :], wi[:, t, 0:1], None, ALU.mult).then_inc(S, did())
                    for i in range(1, 4):
                        own()
                        v.scalar_tensor_tensor(s, rel[:, t, i, :], wi[:, t, i:i + 1], s, ALU.mult, ALU.add).then_inc(S, did())
                    own()
                    v.tensor_tensor(s, s, con("causal", 2, SEQ)[:, t, :], ALU.add).then_inc(S, did())
                    for _ in range(SEQ // 4 // 8):
                        own()
                        alone()
                        v.max(top, s).then_inc(S, did())
                        own()
                        alone()
                        v.match_replace(out=s, in_to_replace=top, in_values=s, imm_value=-3e38).then_inc(S, did())
                    own()
                    v.tensor_scalar(mask[:, t, :], s, -2e38, NEG, ALU.is_gt, ALU.mult).then_inc(S, did())
                    own()
                    v.tensor_tensor(mask[:, t, :], mask[:, t, :], con("causal", 2, SEQ)[:, t, :], ALU.add).then_inc(S, did())
                own()
                for t in range(TT):
                    rotate(qkr[:, t, :], qk_tok[:, t, :], t, 8)
                v.memset(chp[:, :, 0:TAPS_A - 1], 0.0).then_inc(S, did("qk rope"))
                for i in range(2):
                    wait(sca_c, f"ac {i}")
                    v.tensor_tensor(chp[:, i, TAPS_A - 1:], ac[:, i, :], bank[2 + i][:, SEQ:2 * SEQ], ALU.mult)\
                        .then_inc(S, did(f"ch got {i}"))
                wait(sca_c, "vg got 1")
                bn, mv = view(stat, 64, TT, 6), view(stat, 88, TT, 2)
                for t in range(TT):
                    v.bn_stats(bn[:, t, :], vg_tok[:, t, 256:512]).then_inc(S, did())
                own()
                alone()
                for t in range(TT):
                    v.bn_aggr(mv[:, t, :], bn[:, t, :]).then_inc(S, did())
                own()
                power("v", 2, mv[:, :, 1], None, LN_EPS)
                ya = rt_a.rearrange("p (i n) -> p i n", i=2)
                for tap in range(TAPS_A):
                    own()
                    for i in range(2):
                        w = pr("wca", 3 * i + tap)
                        if tap == 0:
                            v.tensor_scalar(ya[:, i, :], chp[:, i, 0:SEQ], w, None, ALU.mult).then_inc(S, did())
                        else:
                            v.scalar_tensor_tensor(ya[:, i, :], chp[:, i, tap:tap + SEQ], w, ya[:, i, :], ALU.mult, ALU.add)\
                                .then_inc(S, did())
                wait(pol_c, "power v")
                for t in range(TT):
                    v.tensor_scalar(vn[:, t, :], vg_tok[:, t, 256:512], mv[:, t, 0:1], stat[:, 42 + t:43 + t],
                                    ALU.subtract, ALU.mult).then_inc(S, did())
                own()
                for name, op in (("gg", ALU.mult), ("gb", ALU.add)):
                    v.tensor_tensor(vn, vn, pr(name, 0, 256).unsqueeze(1).broadcast_to([P, TT, 256]), op)\
                        .then_inc(S, did(*["vn"] * (name == "gb")))
                    own()
                wait(ten_c, "qk transposed")
                v.tensor_copy(kT, bank[1][:, :].rearrange("p (i n) -> p i n", i=2)).then_inc(S, did("kT"))
                for i in range(2):
                    wait(sca_c, f"bu got {i}")
                    v.tensor_tensor(catT[:, i, :], ya[:, i, :], bu[:, i, 0:SEQ], ALU.mult).then_inc(S, did())
                for tap in range(TAPS_C):
                    own()
                    for i in range(2):
                        w = pr("wcf", TAPS_C * i + tap)
                        if tap == 0:
                            v.tensor_scalar(conv[:, i, :], yp[:, i, 0:SEQ], w, pr("bcf", i), ALU.mult, ALU.add).then_inc(S, did())
                        else:
                            v.scalar_tensor_tensor(conv[:, i, :], yp[:, i, tap:tap + SEQ], w, conv[:, i, :], ALU.mult, ALU.add)\
                                .then_inc(S, did(*[f"conv {i}"] * (tap == TAPS_C - 1)))
                wait(ten_c, "gated")
                for i in range(2):
                    v.tensor_tensor(mixed[:, i, :].rearrange("p (t n) -> p t n", t=TT),
                                    bank[6 + i][:, 0:SEQ].rearrange("p (t n) -> p t n", t=TT),
                                    pr("bs", P * i, P).unsqueeze(1).broadcast_to([P, TT, P]), ALU.add).then_inc(S, did())
                own()
                for i in range(2):
                    v.tensor_tensor(catT[:, 2 + i, :], mixed[:, i, :], bu[:, i, SEQ:2 * SEQ], ALU.mult).then_inc(S, did(f"y_b {i}"))
                wait(ten_c, "conv transposed")
                for t in range(TT):
                    v.bn_stats(bn[:, t, :], bank[2][:, t * SEQ:(t + 1) * SEQ]).then_inc(S, did())
                own()
                alone()
                for t in range(TT):
                    v.bn_aggr(mv[:, t, :], bn[:, t, :]).then_inc(S, did())
                own()
                power("conf", 4, mv[:, :, 1], None, LN_EPS)
                wait(pol_c, "power conf")
                for t in range(TT):
                    v.tensor_scalar(ynorm[:, t, :], bank[2][:, t * SEQ:(t + 1) * SEQ], mv[:, t, 0:1], stat[:, 44 + t:45 + t],
                                    ALU.subtract, ALU.mult).then_inc(S, did(f"ynorm {t}"))

                def peak_c(u):
                    wait(ten_c, f"scores {u}")
                    if u >= 3:
                        wait(sca_c, f"exp {u - 3}")
                    alone()
                    v.tensor_tensor_reduce(out=ms[:, u % 3, :], in0=bank[u % 3][:, 0:SEQ], in1=mask[:, u % 2, :], scale=1.0,
                                           scalar=-3e38, op0=ALU.add, op1=ALU.max, accum_out=rinv[:, 8 + u:9 + u])\
                        .then_inc(S, did(f"masked {u}"))
                    own()
                    v.tensor_scalar(nmax[:, u:u + 1], rinv[:, 8 + u:9 + u], -1.0, None, ALU.mult).then_inc(S, did(f"nmax {u}"))

                def o_c_out(u):
                    wait(sca_c, f"exp {u}")
                    v.reciprocal(rinv[:, u:u + 1], rsum[:, u:u + 1]).then_inc(S, did())
                    wait(ten_c, f"attended {u}")
                    own()
                    v.tensor_scalar(o_c[:, u % 2, (u // 2) * HD:(u // 2 + 1) * HD], bank[6 + u % 2][:, 0:HD], rinv[:, u:u + 1],
                                    None, ALU.mult).then_inc(S, did(f"o {u}"))

                own()
                peak_c(0)
                peak_c(1)
                for u in range(8):
                    if u + 2 < 8:
                        peak_c(u + 2)
                    o_c_out(u)
                wait(ten_c, "o transposed")
                v.tensor_copy(catT[:, 4:6, :], bank[0][:, :].rearrange("p (i n) -> p i n", i=2)).then_inc(S, did("y_c"))

                def residual(name):
                    wait(ten_c, name.replace("x", "y"))
                    for t in range(TT):
                        for half in range(2):
                            a = x[:, t, half * 512:half * 512 + 512]
                            v.tensor_tensor(a, a, bank[4 + 2 * t + half][:, :], ALU.add)\
                                .then_inc(S, did(*[name] * (t == 1 and half == 1)))

                residual("x 0")
                wait(sca_c, "ffn squares")
                power("ffn", 6, stat[:, 18:20], 1.0 / D, RMS_EPS)
                scaled_out("ffn", "gffn")
                for i in range(FT // 2):
                    wait(sca_c, f"silu {i}")
                    v.tensor_tensor(hid[:, 2 * i:2 * i + 2, :], silu[:, i % 2, :].rearrange("p (j n) -> p j n", j=2),
                                    bank[2 * (i % 2) + 1][:, :].rearrange("p (j n) -> p j n", j=2), ALU.mult)\
                        .then_inc(S, did(f"hid {i}"))
                residual("x 1")

            dve.wait_ge(vec_c.sem, vec_c.at("x 1", 1))
            dve.wait_ge(sca_f.sem, sca_f.at("squares"))
            v.tensor_scalar(stat[:, 32:34], stat[:, 16:18], 1.0 / D, RMS_EPS, ALU.mult, ALU.add)\
                .then_inc(vec_f.sem, vec_f.did("power wanted final"))
            dve.wait_ge(pol_f.sem, pol_f.at("power final"))
            dve.wait_ge(gfin_loaded, 16)
            for t in range(TT):
                v.scalar_tensor_tensor(tmp[:, t, :], x[:, t, :], stat[:, 40 + t:41 + t], gfin, ALU.mult, ALU.mult)\
                    .then_inc(vec_f.sem, vec_f.did(f"out {t}"))

        @block.scalar
        def _(act):
            a = nc.scalar
            for dst, src in ((cols[:, :], cols_d), (const[:, :], const_d), (ctx_tok, ctx_d), (x[:, :, :], x_d)):
                act.dma_start(dst, src).then_inc(in_loaded, 16)

            def after(*whos):
                for who, name in whos:
                    act.wait_ge(who.sem, who.at(name))

            act.wait_ge(in_loaded, 64)
            a.activation(stat[:, 48:64], cols[:, COLS["c"][0]:COLS["c"][0] + 16], ACT.Silu).then_inc(sca.sem, sca.did("silu c"))
            after((vec, "mod 0 first"))

            def copy(dst, src, **kw):
                return a.activation(dst, src, ACT.Copy, **kw)

            for n, g in enumerate(GROUPS):
                if not by_scalar(n):
                    continue
                after((ten, f"full {g}"))
                b, name = bank[n % 7], f"got {g}"
                if g[0] == "h":
                    k = g[1]
                    for c in range(2):
                        a.activation(hT4[:, k, (1 - c) * SEQ:(2 - c) * SEQ], b[:, (1 - c) * SEQ:(2 - c) * SEQ], ACT.Identity,
                                     scale=mod[:, 0, 8 + k, c:c + 1], bias=mod[:, 0, k, c:c + 1])\
                            .then_inc(sca.sem, sca.did(*[name] * c))
                elif g[0] == "c":
                    t, c0 = g[1], 256 if g[1] < 2 else 0
                    copy(c_tok[:, t, c0:], b[:, c0:416]).then_inc(sca.sem, sca.did(name))
                elif g[0] == "ka":
                    copy(kaT[:, g[1], :], b[:, :]).then_inc(sca.sem, sca.did(name))
                elif g[0] == "qa":
                    copy(qaT[:, 2 * g[1]:2 * g[1] + 2, :], b[:, :].rearrange("p (j n) -> p j n", j=2), scale=NA_SCALE)\
                        .then_inc(sca.sem, sca.did(name))
                else:
                    copy(va[:, g[1], :], b[:, :]).then_inc(sca.sem, sca.did(name))

            def exp(u):
                after((vec, f"nmax {u}"))
                if u >= 3:
                    after((ten, f"probs transposed {u - 3}"))
                a.activation(probs[:, u % 3, :], bank[u % 3][:, :], ACT.Exp, bias=nmax[:, u:u + 1],
                             accum_out=rsum[:, u:u + 1]).then_inc(sca.sem, sca.did(f"exp {u}"))

            def probs_out(u):
                if u % 2:
                    after((ten, f"probs transposed {u}"))
                    if u >= 2:
                        after((ten, f"attended {u - 2}"))
                    copy(probsT[:, u % 2, :], bank[3 + u % 2][:, :]).then_inc(sca.sem, sca.did(f"probsT {u}"))

            def units(first):
                exp(first)
                exp(first + 1)
                for u in range(first, first + 16):
                    if u + 2 < first + 16:
                        exp(u + 2)
                    if u + 1 < first + 16:
                        probs_out(u + 1)

            units(0)
            for n, g in enumerate(UP_GROUPS):
                if not by_scalar(n):
                    continue
                after((ten, f"full {g}"))
                b, name = bank[n % 7], f"got {g}"
                if g[0] == "qup":
                    copy(qm_tok[:, g[1], g[2] * 384:g[2] * 384 + 384], b[:, 0:384], scale=MLA_SCALE).then_inc(sca.sem, sca.did(name))
                elif g[0] == "v":
                    copy(vm[:, g[1], :], b[:, :]).then_inc(sca.sem, sca.did(name))
                elif g[0] == "kn":
                    copy(kmT[0:HD, g[1], :], b[0:HD, :]).then_inc(sca.sem, sca.did(name))
                else:
                    copy(qmT[0:MQ, 2 * g[1]:2 * g[1] + 2, :], b[0:MQ, :].rearrange("p (j n) -> p j n", j=2))\
                        .then_inc(sca.sem, sca.did(name))
            units(16)
            for b in range(1, 4, 2):
                after((ten, f"o transposed {b}"))
                copy(oT[:, 2 * b:2 * b + 2, :], bank[b][:, :].rearrange("p (j n) -> p j n", j=2)).then_inc(sca.sem, sca.did(f"oT {b}"))

            def gate_row_out(n):
                for half in range(2):
                    after((ten, f"gate {n} {4 * half + 3}"))
                    copy(gate_row[n % 2][:, half * 512:half * 512 + 512], bank[half][:, :])\
                        .then_inc(sca.sem, sca.did(*[f"gate row {n}"] * half))

            def modulated_out(n, dst, layer, part):
                for b in range(1, 4, 2):
                    after((ten, f"x {n} transposed {b}"))
                    for j in range(2):
                        k = 2 * b + j
                        a.activation(dst(k), bank[b][:, j * SEQ:(j + 1) * SEQ], ACT.Identity,
                                     scale=mod[:, layer, 24 * part + 8 + k, 0:1], bias=mod[:, layer, 24 * part + k, 0:1])\
                            .then_inc(sca.sem, sca.did(*[f"hT {n} {b}"] * j))

            gate_row_out(0)
            gate_row_out(1)
            modulated_out(0, lambda k: hT[:, k, :], 0, 1)
            for i in range(FT // 2):
                after((ten, f"gu {i}"))
                if i >= 2:
                    after((vec, f"hid {i - 2}"))
                a.activation(silu[:, i % 2, :], bank[2 * (i % 2)][:, :], ACT.Silu).then_inc(sca.sem, sca.did(f"silu {i}"))
            gate_row_out(2)
            modulated_out(1, lambda k: hp[:, k, HALO:HALO + SEQ], 1, 0)
            gate_row_out(3)
            modulated_out(2, lambda k: hT[:, k, :], 1, 1)
            after((vec, "gate exponents"))
            a.activation(stat[:, 104:106], stat[:, 102:104], ACT.Exp).then_inc(sca.sem, sca.did("gate exponentials"))

            after((vec, "passes"))
            passes = act.value_load(n_passes[0:1, 0:1], min_val=1, max_val=PASSES_MAX)
            act.sem_inc(sca_b.sem, sca_b.per)
            with act.Fori(0, passes) as p:
                with act.Fori(0, EXPERTS) as e:
                    j = p * EXPERTS + e
                    act.wait_ge(ten_b.sem, ten_b.at("gathered 0", j))
                    for k in range(4):
                        a.activation(xgT[:, k, :], bank[0][:, k * P:(k + 1) * P], ACT.Identity, scale=mod[:, 1, 32 + k, 0:1],
                                     bias=mod[:, 1, 24 + k, 0:1]).then_inc(sca_b.sem, sca_b.did(*["xgT"] * (k == 3)))
                    act.wait_ge(ten_b.sem, ten_b.at("spread", j))
                    copy(spread, bank[3][:, 0:SEQ]).then_inc(sca_b.sem, sca_b.did("spread"))
                    for i in range(EFT // 2):
                        act.wait_ge(ten_b.sem, ten_b.at(f"gu {i}", j))
                        if i >= 2:
                            act.wait_ge(vec_b.sem, vec_b.at(f"hid {i - 2}", j))
                        else:
                            act.wait_ge(vec_b.sem, vec_b.was(f"hid {EFT // 2 - 2 + i}", j))
                        a.activation(siluE[:, i % 2, :], bank[2 + i % 2][:, 0:256], ACT.Silu)\
                            .then_inc(sca_b.sem, sca_b.did(f"silu {i}"))
                    act.wait_ge(ten_b.sem, ten_b.at("y", j))
                    copy(outE[:, 0:512], bank[4][:, :]).then_inc(sca_b.sem, sca_b.did("outE"))

            act.sem_inc(sca_c.sem, sca_c.per)
            act.wait_ge(vec_f.sem, vec_f.at("x"))
            with act.Fori(0, 2) as l:
                S = sca_c.sem

                def wait(who, name):
                    act.wait_ge(who.sem, who.at(name, l))

                def did(*names):
                    return sca_c.did(*names)

                def scale_x(name, at, power):
                    for t in range(TT):
                        a.activation(junk, x[:, t, :], ACT.Square, accum_out=stat[:, at + t:at + t + 1])\
                            .then_inc(S, did(*[f"{name} squares"] * t))
                        act.wait_ge(S, sca_c.last(l))
                    wait(pol_c, f"power {name}")
                    for t in range(TT):
                        a.activation(tmp[:, t, :], x[:, t, :], ACT.Copy, scale=stat[:, power + t:power + t + 1])\
                            .then_inc(S, did(*[f"{name} scaled"] * t))

                def scaled_out(name, gain):
                    for b in range(1, 4, 2):
                        wait(ten_c, f"{name} transposed {b}")
                        for j in range(2):
                            a.activation(hT[:, 2 * b + j, :], bank[b][:, j * SEQ:(j + 1) * SEQ], ACT.Copy,
                                         scale=pr(gain, 2 * b + j)).then_inc(S, did(*[f"{name} hT {b}"] * j))

                act.wait_ge(vec_c.sem, vec_c.was("x 1", l))
                scale_x("mix", 16, 40)
                wait(vec_c, "par")
                scaled_out("mix", "gmix")
                for t in range(TT):
                    wait(ten_c, f"qi {t}")
                    copy(qi_tok[:, t, :], bank[4 + t][:, 0:QI_W]).then_inc(S, did(f"qi got {t}"))
                for i in range(2):
                    wait(ten_c, f"dd {i}")
                    a.activation(sig[:, i, :], bank[6 + i][:, SEQ:2 * SEQ], ACT.Sigmoid).then_inc(S, did(f"sig {i}"))
                wait(ten_c, "qi transposed")
                copy(qiT, bank[0][:, :].rearrange("p (i n) -> p i n", i=2)).then_inc(S, did())
                copy(kiT, bank[1][:, 0:SEQ]).then_inc(S, did("qiT"))
                for t in range(TT):
                    wait(ten_c, f"index scores {t}")
                    for i in range(2):
                        a.activation(rel[:, t, i:4:2, :], bank[2 + i - 2 * t][:, :].rearrange("p (i n) -> p i n", i=2), ACT.Relu)\
                            .then_inc(S, did(*[f"rel {t}"] * i))
                for t in range(TT):
                    wait(ten_c, f"vg {t}")
                    copy(vg_tok[:, t, :], bank[6 + t][:, :]).then_inc(S, did(f"vg got {t}"))
                for i in range(2):
                    wait(ten_c, f"ch {i}")
                    copy(ac[:, i, :], bank[2 + i][:, 0:SEQ]).then_inc(S, did(f"ac {i}"))
                for i in range(2):
                    wait(ten_c, f"bu {i}")
                    copy(bu[:, i, :], bank[4 + i][:, :]).then_inc(S, did(f"bu got {i}"))
                wait(ten_c, "qk transposed")
                copy(qT, bank[0][:, :].rearrange("p (i n) -> p i n", i=2), scale=NA_SCALE).then_inc(S, did("qT"))
                wait(ten_c, "ynorm transposed")
                for i in range(2):
                    a.activation(catT[:, 6 + i, :], bank[3][:, i * SEQ:(i + 1) * SEQ], ACT.Silu, scale=pr("clg", i),
                                 bias=pr("clb", i)).then_inc(S, did(f"y_d {i}"))

                def exp_c(u):
                    wait(vec_c, f"nmax {u}")
                    if u >= 3:
                        wait(ten_c, f"probs transposed {u - 3}")
                    a.activation(probs2[:, u % 3, :], ms[:, u % 3, :], ACT.Exp, bias=nmax[:, u:u + 1],
                                 accum_out=rsum[:, u:u + 1]).then_inc(S, did(f"exp {u}"))

                def probs_out_c(u):
                    wait(ten_c, f"probs transposed {u}")
                    if u >= 2:
                        wait(ten_c, f"attended {u - 2}")
                    copy(probsT2[:, u % 2, :], bank[4 + u % 2][:, 0:SEQ]).then_inc(S, did(f"probsT {u}"))

                exp_c(0)
                exp_c(1)
                probs_out_c(0)
                for u in range(8):
                    if u + 2 < 8:
                        exp_c(u + 2)
                    if u + 1 < 8:
                        probs_out_c(u + 1)
                wait(vec_c, "x 0")
                scale_x("ffn", 18, 46)
                scaled_out("ffn", "gffn")
                for i in range(FT // 2):
                    wait(ten_c, f"gu {i}")
                    if i >= 2:
                        wait(vec_c, f"hid {i - 2}")
                    a.activation(silu[:, i % 2, :], bank[2 * (i % 2)][:, :], ACT.Silu).then_inc(S, did(f"silu {i}"))
            act.wait_ge(vec_c.sem, vec_c.at("x 1", 1))
            for t in range(TT):
                a.activation(junk, x[:, t, :], ACT.Square, accum_out=stat[:, 16 + t:17 + t])\
                    .then_inc(sca_f.sem, sca_f.did(*["squares"] * t))
                act.wait_ge(sca_f.sem, sca_f.last())


def host_constants():
    f = np.float32
    c = np.zeros((P, N_CONST), f)

    def put(name, a):
        at, w = CONST[name]
        c[:, at:at + w] = np.asarray(a, f).reshape(P, w)

    i = np.arange(P)
    put("ident", np.eye(P))
    put("ones", np.ones((P, P)))
    put("before", i[:, None] < i[None, :])
    put("tri", i[:, None] <= i[None, :])
    put("iota", np.broadcast_to(i, (P, P)))
    tok = (np.arange(TT)[None, :] * P + i[:, None])
    put("causal", np.where(np.arange(SEQ)[None, None, :] <= tok[:, :, None], 0.0, NEG))
    inv = (1.0 / (np.float32(10000.0) ** (np.arange(8, dtype=f) / f(8)))).astype(f)
    ang = np.stack([(tok // 64).astype(f)[:, :, None] * inv, (tok % 64).astype(f)[:, :, None] * inv], 2).astype(f)
    put("mcos", np.stack([np.cos(ang)] * 2, 3))
    put("msin", np.sin(ang))
    inv = (np.float32(10000.0) ** (-np.arange(0, HD, 2, dtype=f) / f(HD))).astype(f)
    ang = (tok.astype(f)[:, :, None] * inv).astype(f)
    put("dcos", np.cos(ang))
    put("dsin", np.sin(ang))
    put("rev", np.broadcast_to(np.arange(8, 0, -1), (P, 8)))
    put("neghalf", np.full((P, 8), -0.5))
    t = np.arange(SEQ)
    counts = np.stack([np.clip(t + w // 2, 0, SEQ) - np.clip(t - w // 2, 0, SEQ) for w in (2, 4, 8, 16)])
    return c, (1.0 / counts.astype(f)).astype(f)


def by_rows(w):
    return w.reshape(-1, P, w.shape[1]).transpose(1, 0, 2)


def column(a):
    return np.asarray(a).reshape(-1, P).T


def ffn_chunks(order, wg, wu, wd):
    g, u, d = by_rows(wg), by_rows(wu), by_rows(wd)
    for kind, i in order:
        if kind == "gu":
            yield np.stack([g[:, :, 256 * i:256 * i + 256], u[:, :, 256 * i:256 * i + 256]], 2)
        else:
            yield d[:, 4 * i:4 * i + 4]


def host_layout(a, inv_counts):
    chunks = np.zeros((N_CHUNKS, P, CW), np.float32)
    count = [0]

    def push(*parts):
        at = 0
        for part in parts:
            part = np.asarray(part).reshape(P, -1)
            chunks[count[0], :, at:at + part.shape[1]] = part
            at += part.shape[1]
        count[0] += 1

    w_in = by_rows(a["attn_w_in"][0])
    w_out = by_rows(a["attn_w_out"][0])
    proj = {"qa": slice(0, 512), "ka": slice(512, 1024), "va": slice(1024, 1536), "c": slice(1536, NC_COLS)}
    ffn = ffn_chunks(FFN_ORDER, a["ffn_w_gate"][0], a["ffn_w_up"][0], a["ffn_w_down"][0])
    for c in FIRST_ORDER:
        if c[0] == "mod":
            push(by_rows(a["mod_w"][c[1]][:, 512 * c[2]:512 * c[2] + 512]))
        elif c[0] == "proj":
            w = w_in[:, :, proj[c[1]]]
            push(np.pad(w, ((0, 0), (0, 0), (0, 512 - w.shape[2]))))
        elif c[0] == "up":
            push(by_rows(a["mla_w_q_up"][0]), a["mla_w_kv_up"][0])
        elif c[0] == "out":
            push(w_out[:, :, 512 * c[1]:512 * c[1] + 512])
        elif c[0] == "ffn":
            push(next(ffn))
        else:
            push(a["pool_w"][0].reshape(4, 2, P, 256).transpose(2, 0, 1, 3), by_rows(a["moe_router"][0]),
                 np.broadcast_to(inv_counts.reshape(1, -1), (P, 4 * SEQ)))
    for e in range(EXPERTS):
        for part in ffn_chunks(MOE_ORDER, a["moe_w_gate"][0, e], a["moe_w_up"][0, e], a["moe_w_down"][0, e]):
            push(part)
    for l in range(2):
        w = by_rows(a["w_in_2"][l])
        w_out = by_rows(a["w_out_2"][l])
        ffn = ffn_chunks(FFN_ORDER, a["w_gate_2"][l], a["w_up_2"][l], a["w_down_2"][l])
        spread = lambda v: np.broadcast_to(np.asarray(v).reshape(1, -1), (P, 256))
        taps = lambda v: np.asarray(v).T.reshape(2, P, -1).transpose(1, 0, 2)
        b_s = np.repeat(a["b_s_2"][l].reshape(2, 2, 1, P), HD, axis=2).reshape(2, P, P).transpose(1, 0, 2)
        mix = {
            "qi": (w[:, :, 2048:2048 + QI_W], a["w_s_2"][l].transpose(2, 0, 1), column(a["g_mix_2"][l]), column(a["g_ffn_2"][l]),
                   taps(a["w_conv_a_2"][l]), taps(a["w_conf_2"][l]), column(a["b_conf_2"][l]), column(a["conf_ln_g_2"][l]),
                   column(a["conf_ln_b_2"][l]), spread(a["gmlp_ln_g_2"][l]), spread(a["gmlp_ln_b_2"][l]), b_s),
            "dd": (w[:, :, 2372:2884],),
            "qk": (w[:, :, 1280:1792],),
            "vg": (np.concatenate([w[:, :, 1792:2048], w[:, :, 1024:1280]], 2),),
            "ch": (w[:, :, 256:768],),
            "bu": (np.concatenate([w[:, :, 0:256], w[:, :, 768:1024]], 2),),
        }
        for c in LAYER_ORDER:
            if c[0] == "mix":
                push(*mix[c[1]])
            elif c[0] == "out":
                push(w_out[:, :, 512 * c[1]:512 * c[1] + 512])
            else:
                push(next(ffn))
    assert count[0] == N_CHUNKS

    cols = np.zeros((P, N_COLS), np.float32)

    def put(name, v):
        at, w = COLS[name]
        cols[:, at:at + w] = np.asarray(v).reshape(P, w)

    put("modb0", column(a["mod_b"][0]))
    put("modb1", column(a["mod_b"][1]))
    put("c", np.stack([column(a["c"][0]), column(a["c_ctx"])], 2))
    put("qn", column(a["mla_q_norm"][0]))
    put("kvn", column(a["mla_kv_norm"][0]))
    put("pscale", column(a["pool_scale"][0]))

    rb = a["na_rel_bias"][0]
    pos = np.arange(SEQ)
    row, colm = pos // 64, pos % 64
    start = np.clip(colm - 8, 0, 64 - 16)
    near = (colm[None, :] >= start[:, None]) & (colm[None, :] < start[:, None] + 16)
    drow = row[None, :] - row[:, None] + 7
    dcol = np.where(near, colm[None, :] - colm[:, None] + 15, 0)
    bias = np.where(near[None], rb[:, drow, dcol], np.float32(NEG)).astype(np.float32)
    bias = bias.reshape(HEADS, TT, P, SEQ).transpose(2, 1, 0, 3)
    rows = np.stack([np.concatenate([a[f"ln{i % 2 + 1}_g"][i // 2], a[f"ln{i % 2 + 1}_b"][i // 2]]) for i in range(4)])
    rows = np.broadcast_to(rows[:, None, :], (4, P, 2 * D))
    gfin = np.broadcast_to(a["g_final_2"][None, :], (P, D))
    tokens = lambda v: v.reshape(TT, P, D).transpose(1, 0, 2)
    return chunks, tokens(a["x"][0]), tokens(a["ctx"][0]), cols, bias, rows, gfin


def kernel(**inputs):
    from concourse import bacc
    from concourse.bass_utils import run_bass_kernel_spmd

    arrays = {name: np.asarray(value) for name, value in inputs.items()}
    const, inv_counts = host_constants()
    chunks, x, ctx, cols, bias, rows, gfin = host_layout(arrays, inv_counts)
    sent = {"chunks": chunks, "x_in": x, "ctx_in": ctx, "cols_in": cols, "const_in": const, "bias_in": bias,
            "rows_in": rows, "gfin_in": gfin}
    sent = {name: np.ascontiguousarray(value) for name, value in sent.items()}

    def program(books):
        nc = bacc.Bacc("TRN2", target_bir_lowering=False, num_devices=1)
        ins = [nc.dram_tensor(name, value.shape, F32, kind="ExternalInput").ap() for name, value in sent.items()]
        out = nc.dram_tensor("out", (SEQ, D), F32, kind="ExternalOutput").ap()
        build(nc, ins, out, books)
        return nc

    books = {}
    program(books)
    for book in books.values():
        book["complete"] = True
    nc = program(books)
    result = run_bass_kernel_spmd(nc, [sent], core_ids=[0])
    return result.results[0]["out"].reshape(1, SEQ, D)
```

```python
from contextlib import ExitStack

import concourse.bass as bass
import numpy as np
from concourse import mybir
from concourse.alu_op_type import AluOpType as ALU

P = 128
D = 1024
KT = D // P
SEQ = 256
TT = SEQ // P
HEADS = 8
HD = 64
ROPE_D = 32
MQ = HD + ROPE_D
CW = 4096
RING = 7
NC_COLS = 1952
FT = 22
EXPERTS = 8
EFT = 28
SLOTS = 128
QW = CW // 4
Q_FFN, Q_MOE = 3, 4
KEPT = 8
PASSES_MAX = SEQ // SLOTS
ALPHA = 4.0 ** 0.25
LN_EPS = 1e-5
RMS_EPS = 1e-6
NEG = -1e30
TAPS_A, TAPS_C = 3, 31
TAPS_EARLY = 18
WINDOWS = (2, 4, 8, 16)
MLA_SCALE = float(MQ) ** -0.5
NA_SCALE = float(HD) ** -0.5

F32 = mybir.dt.float32
F32R = mybir.dt.float32r
I32 = mybir.dt.int32
ACT = mybir.ActivationFunctionType
AX_X = mybir.AxisListType.X



def ffn_order(n_gu):
    order, down = [], 0
    for i in range(n_gu):
        order.append(("gu", i))
        if i >= 2 and i % 2 == 0:
            order.append(("d", down))
            down += 1
    while 4 * down < 2 * n_gu:
        order.append(("d", down))
        down += 1
    return order


def quarters(c, tiles):
    return 4 if c[0] == "gu" else min(4, tiles - 4 * c[1])


FFN_ORDER = ffn_order(FT // 2)
MOE_ORDER = ffn_order(EFT // 2)
MODS = [("mod", 0, i) for i in range(4, 12)] + [("mod", 1, i) for i in range(12)]
PROJ_MODS, NA_MODS = 9, 6
FIRST_ORDER = ([("mod", 0, i) for i in range(4)]
               + [("proj", "c"), ("proj", "ka")] + MODS[0:2] + [("proj", "qa")] + MODS[2:4] + [("proj", "va")]
               + MODS[4:PROJ_MODS + NA_MODS] + [("up",)] + MODS[PROJ_MODS + NA_MODS:]
               + [("out", 0), ("out", 1)] + [("ffn",) + c for c in FFN_ORDER] + [("pool",)])
LAYER_ORDER = ([("mix", n) for n in ("qi", "dd", "qk", "vg", "ch", "bu")]
               + [("out", 0), ("out", 1)] + [("ffn",) + c for c in FFN_ORDER])
N_FIRST, N_EXPERT, N_LAYER = len(FIRST_ORDER), len(MOE_ORDER), len(LAYER_ORDER)
assert N_FIRST % RING == 0 and N_EXPERT % RING == 0
N_CHUNKS = N_FIRST + EXPERTS * N_EXPERT + 2 * N_LAYER



def held(c):
    if c == ("up",):
        return 2560
    if c[0] == "ffn" and c[1] == "d":
        return QW * quarters(c[1:], FT)
    return CW


COLS = {}
_n = 0
for _name, _w in (("modb0", 48), ("modb1", 48), ("c", 16), ("qn", 2), ("kvn", 1), ("pscale", 8), ("lng", 32), ("lnb", 32),
                  ("router", 64)):
    COLS[_name] = (_n, _w)
    _n += _w
N_COLS = _n
CONST = {}
_n = 0
for _name, _w in (("ident", 128), ("ones", 128), ("before", 128), ("tri", 128), ("iota", 128),
                  ("causal", 512), ("mcos", 64), ("msin", 32), ("dcos", 64), ("dsin", 64), ("rev", 8),
                  ("neghalf", 8)):
    CONST[_name] = (_n, _w)
    _n += _w
N_CONST = _n
QI_W = 324
PAR = {}
_n = 0
for _name, _w in (("gmix", 8), ("gffn", 8), ("wca", 6), ("wcf", 62), ("bcf", 2), ("clg", 2), ("clb", 2),
                  ("gg", 256), ("gb", 256), ("bs", 256)):
    PAR[_name] = (_n, _w)
    _n += _w
N_PAR = _n
WS_AT = KT * QI_W
PAR_AT = WS_AT + 4 * P
MEANS_AT = 2048


class Progress:

    def __init__(self, sem, book):
        self.sem, self.book, self.n, self.named = sem, book, 0, set()

    def did(self, *names):
        self.n += 1
        for name in names:
            assert name not in self.named, name
            self.named.add(name)
            self.book[name] = self.n
        if not self.book.get("complete"):
            self.book["per turn"] = self.n
        return 1

    @property
    def per(self):
        return self.book.get("per turn", 1)

    def at(self, name, turn=None):
        assert name in self.book or not self.book.get("complete"), name
        k = self.book.get(name, 1)
        return k if turn is None else turn * self.per + (self.per + k)

    def was(self, name, turn):
        assert name in self.book or not self.book.get("complete"), name
        return turn * self.per + self.book.get(name, 1)

    def last(self, turn=None):
        return self.n if turn is None else turn * self.per + (self.per + self.n)

    def last_but(self, k, turn):
        return turn * self.per + (self.per + self.n - k)


def build(nc, ins, out, books):
    chunks_d, x_d, ctx_d, cols_d, const_d, bias_d, rows_d, gfin_d = ins
    with ExitStack() as ctx:
        def sem(name):
            return ctx.enter_context(nc.semaphore(name))

        ring = ctx.enter_context(nc.sbuf_tensor("ring", [P, RING * CW], F32))
        bank = [ctx.enter_context(nc.psum_tensor(f"bank{i}", [P, 512], F32)) for i in range(8)]
        x = ctx.enter_context(nc.sbuf_tensor("x", [P, TT, D], F32))
        cols = ctx.enter_context(nc.sbuf_tensor("cols", [P, N_COLS], F32))
        const = ctx.enter_context(nc.sbuf_tensor("const", [P, N_CONST], F32))
        mod = ctx.enter_context(nc.sbuf_tensor("mod", [P, 2, 48, 2], F32))
        fold = ctx.enter_context(nc.sbuf_tensor("fold", [P, 3, 2, KT], F32))
        stat = ctx.enter_context(nc.sbuf_tensor("stat", [P, 128], F32))
        soft = ctx.enter_context(nc.sbuf_tensor("soft", [P, 3, 32], F32))
        n_passes = ctx.enter_context(nc.sbuf_tensor("n_passes", [P, 1], I32))
        at_rows = -(-nc.sbuf_base // 32) * 32
        R = ctx.enter_context(nc.sbuf_tensor("rows", [P, 4096], F32))
        at_work = -(-nc.sbuf_base // 32) * 32
        W = ctx.enter_context(nc.sbuf_tensor("work", [P, 16232], F32))
        R_parts = nc.alloc_sbuf_tensor_at("rows_parts", [P, 4096], F32R, offset=at_rows)
        W_parts = nc.alloc_sbuf_tensor_at("work_parts", [P, 16232], F32R, offset=at_work)

        def view(region, at, *dims):
            n = int(np.prod(dims))
            v = region[:, at:at + n]
            if len(dims) == 2:
                v = v.rearrange("p (a b) -> p a b", a=dims[0])
            elif len(dims) == 3:
                v = v.rearrange("p (a b c) -> p a b c", a=dims[0], b=dims[1])
            elif len(dims) == 4:
                v = v.rearrange("p (a b c d) -> p a b c d", a=dims[0], b=dims[1], c=dims[2])
            return v

        def col(name, i=0):
            return cols[:, COLS[name][0] + i:COLS[name][0] + i + 1]

        def con(name, *dims):
            return view(const, CONST[name][0], *(dims or (CONST[name][1],)))

        ident, ones = con("ident"), con("ones")
        nmax, rsum, rinv = soft[:, 0, :], soft[:, 1, :], soft[:, 2, :]

        ln_g, ln_b = R[:, 0:D], R[:, D:2 * D]
        gate_row = [R[:, 2 * D:3 * D], R[:, 3 * D:4 * D]]
        hT4 = view(R, 0, KT, 2 * SEQ)
        qmT = view(R, 0, HEADS, SEQ)
        vm = view(R, 2048, 4, HEADS * HD)
        bias = view(W, 0, TT, HEADS, SEQ)
        kmT = view(W, 0, HEADS, 2 * SEQ)
        ctx_tok = view(W, 4096, TT, D)
        o_tok = ctx_tok
        c_tok = view(W, 6144, 4, 416)
        probsT = view(W, 6144, 2, 512)
        qaT = view(W, 7808, 4, SEQ)
        kaT = view(W, 8832, 4, 2 * SEQ)
        va = view(W, 10880, 4, 512)
        qm_tok = view(W, 7808, TT, HEADS * MQ)
        oT = view(W, 9344, KT, SEQ)
        rope_a = view(W, 14976, 256)
        rope_b = view(W, 15232, 256)
        qcT = view(W, 12928, 2, SEQ)
        kvcT = view(W, 13440, 512)
        krT = view(W, 13952, 512)
        probs = view(W, 14464, 3, 512)
        mod_rows = W[0:2, 12928:12928 + 4 * 512]
        hT = view(W, 0, KT, SEQ)
        hT_hi, hT_lo = view(W_parts, 0, KT, SEQ), view(W_parts, 2048, KT, SEQ)
        hid_hi, hid_lo = view(W_parts, 4096, KEPT, SEQ), view(W_parts, 6144, KEPT, SEQ)
        silu = view(W, 8192, 2, 512)
        tmp = view(W, 4096, TT, D)
        hm = view(W, 6144, KT, SEQ)
        q_hi = [W_parts[:, a:a + QW] for a in (11264, 13312, 9216)] + [R_parts[:, 0:QW]]
        q_lo = [W_parts[:, a + QW:a + 2 * QW] for a in (11264, 13312, 9216)] + [R_parts[:, QW:2 * QW]]
        mixT = view(W, 6144, KT, SEQ)
        xg_hi, xg_lo = view(W_parts, 0, KT, SLOTS), view(W_parts, 1024, KT, SLOTS)
        hidE_hi, hidE_lo = view(W_parts, 2048, KEPT, SLOTS), view(W_parts, 3072, KEPT, SLOTS)
        siluE = view(W, 4096, 2, 256)
        hid_tok = view(W, 4608, 2, 256)
        pick = view(W, 5120, TT, SLOTS)
        pickg = view(W, 5376, TT, SLOTS)
        spread = view(W, 5632, SEQ)
        outE = view(W, 5888, D)
        xm = view(W, 5888, KT, SLOTS)
        acc = view(W, 7168, TT, D)
        place = view(W, 15616, TT, EXPERTS + 1)
        gates = view(W, 15648, TT, EXPERTS + 1)
        route = view(W, 15680, 12, 16)
        now = view(W, 15872, 2, TT)
        catT = view(W, 2048, KT, SEQ)
        qi_tok = view(W, 4096, TT, QI_W)
        qir = view(W, 4744, TT, 384)
        chp = view(W, 4096, 2, SEQ + TAPS_A - 1)
        rt_a, rt_b = view(W, 5512, 512), view(W, 6024, 512)
        junk = view(W, 6144, D)
        qk_tok = view(W, 6536, TT, 512)
        vg_tok = view(W, 7560, TT, 512)
        bu = view(W, 8704, 2, 512)
        yp = view(W, 9728, 2, SEQ + TAPS_C - 1)
        par = view(W, 10752, N_PAR)
        qkr = view(W, 11616, TT, 512)
        qiT = view(W, 12640, 2, SEQ)
        kiT = view(W, 13152, SEQ)
        qT = view(W, 13408, 2, SEQ)
        kT = view(W, 13920, 2, SEQ)
        probs2 = view(W, 14432, 3, SEQ)
        sig = view(W, 14432, 2, SEQ)
        probsT2 = view(W, 15200, 2, SEQ)
        ac = view(W, 15200, 2, SEQ)
        o_c = view(W, 15712, TT, SEQ)
        ah = view(W, 15712, 2, SEQ)
        rel = view(R, 0, TT, 4, SEQ)
        conv = catT[:, 6:8, :]
        ynorm = view(R, 512, TT, SEQ)
        mixed = view(R, 1024, 2, SEQ)
        left = view(R, 2048, TT, SEQ)
        mask = view(R, 2560, TT, SEQ)
        wsm = view(R, 3072, 4, P)
        vn = view(R, 3584, TT, SEQ)
        gfin = R[:, 0:D]
        ms = view(W, 5512, 3, SEQ)
        diag = [W[:, 15360 + P * i:15360 + P * (i + 1)] for i in range(4)]

        def pr(name, i=0, w=1):
            return par[:, PAR[name][0] + i:PAR[name][0] + i + w]

        columns_loaded = sem("columns_loaded")
        constants_loaded = sem("constants_loaded")
        tokens_loaded = sem("tokens_loaded")
        bias_loaded = sem("bias_loaded")
        rows_loaded = sem("rows_loaded")
        gfin_loaded = sem("gfin_loaded")
        stored = sem("stored")
        wait_carrier = sem("wait_carrier")
        landed_a = [sem(f"landed_first_{i}") for i in range(RING)]
        landed_b = [sem(f"landed_expert_{i}") for i in range(RING)]
        landed_c = [sem(f"landed_layer_{i}") for i in range(RING)]

        def progress(name):
            return Progress(sem(name), books.setdefault(name, {}))

        ten, vec, sca, pol = (progress(f"{e}_first") for e in ("tensor", "vector", "scalar", "pool"))
        ten_b, vec_b, sca_b = (progress(f"{e}_experts") for e in ("tensor", "vector", "scalar"))
        ten_c, vec_c, sca_c, pol_c = (progress(f"{e}_layers") for e in ("tensor", "vector", "scalar", "pool"))
        vec_f, sca_f, pol_f, ten_f = (progress(f"{e}_final") for e in ("vector", "scalar", "pool", "tensor"))

        def slot(n):
            return ring[:, (n % RING) * CW:(n % RING + 1) * CW]

        FIRST_AT = {c: n for n, c in enumerate(FIRST_ORDER)}
        EXPERT_AT = {c: n for n, c in enumerate(MOE_ORDER)}
        LAYER_AT = {c: n for n, c in enumerate(LAYER_ORDER)}

        def layer_landed(n, turn):
            per_layer = len(range(n % RING, N_LAYER, RING))
            return turn * (16 * per_layer) + 16 * (n // RING + 1)

        GROUPS = ([("h", k) for k in range(KT)] + [("c", t) for t in range(4)] + [("ka", i) for i in range(4)]
                  + [("qa", i) for i in range(2)] + [("va", t) for t in range(4)])
        UP_GROUPS = ([("qup", t, half) for t in range(TT) for half in range(2)] + [("v", t) for t in range(4)]
                     + [("kn", h) for h in range(HEADS)] + [("qmT", i) for i in range(4)])

        def by_scalar(n):
            return n % 2 == 1

        def matmul3(out, lhs, rhs, start, stop):
            (a_hi, a_lo), (b_hi, b_lo) = lhs, rhs
            nc.tensor.matmul(out, a_hi, b_hi, start=start, stop=False)
            nc.tensor.matmul(out, a_hi, b_lo, start=False, stop=False)
            return nc.tensor.matmul(out, a_lo, b_hi, start=False, stop=stop)

        def first_released(n):
            return (vec, f"split {n}") if FIRST_ORDER[n][0] == "ffn" else (ten, f"used {n}")

        def layer_released(n):
            return (vec_c, f"split {n}") if LAYER_ORDER[n][0] == "ffn" else (ten_c, f"used {n}")

        block = ctx.enter_context(nc.Block())

        @block.sync
        def _(sp):
            for n in range(N_FIRST):
                if n >= RING:
                    who, name = first_released(n - RING)
                    sp.wait_ge(who.sem, who.at(name))
                w = held(FIRST_ORDER[n])
                sp.dma_start(slot(n)[:, 0:w], chunks_d[n][:, 0:w]).then_inc(landed_a[n % RING], 16)
                if n == 3:
                    sp.dma_start(ctx_tok, ctx_d).then_inc(tokens_loaded, 16)
                    sp.dma_start(x[:, :, :], x_d).then_inc(tokens_loaded, 16)

            for n in range(RING):
                who, name = first_released(N_FIRST - RING + n)
                sp.wait_ge(who.sem, who.at(name))
                sp.dma_start(slot(n), chunks_d[N_FIRST + n]).then_inc(landed_b[n], 16)
            sp.wait_ge(vec.sem, vec.at("passes"))
            passes = sp.value_load(n_passes[0:1, 0:1], min_val=1, max_val=PASSES_MAX)

            def load(n, first, turn):
                sp.wait_ge(vec_b.sem, vec_b.at(f"split {n - RING}", turn))
                sp.dma_start(slot(n), chunks_d[bass.ds(first + n, 1)].rearrange("a p n -> (a p) n"))\
                    .then_inc(landed_b[n % RING], 16)

            with sp.Fori(0, passes) as p:
                with sp.Fori(0, EXPERTS - 1) as e:
                    for n in range(RING, N_EXPERT + RING):
                        load(n, e * N_EXPERT + N_FIRST, p * EXPERTS + e)
                for n in range(RING, N_EXPERT):
                    load(n, N_FIRST + (EXPERTS - 1) * N_EXPERT, p * EXPERTS + (EXPERTS - 1))
                behind = nc.s_assert_within(
                    (p - passes + 1) * (EXPERTS * N_EXPERT) + (N_FIRST + (EXPERTS - 1) * N_EXPERT),
                    N_FIRST - N_EXPERT, N_FIRST + (EXPERTS - 1) * N_EXPERT,
                    skip_runtime_bounds_check_because="p is below the number of passes, which is at most two")
                for n in range(N_EXPERT, N_EXPERT + RING):
                    load(n, behind, p * EXPERTS + (EXPERTS - 1))

            for layer in range(2):
                for n in range(0 if layer else RING, N_LAYER):
                    who, name = layer_released(n - RING if n >= RING else max(range(n, N_LAYER, RING)))
                    sp.wait_ge(who.sem, who.at(name, layer if n >= RING else layer - 1))
                    w = held(LAYER_ORDER[n])
                    sp.dma_start(slot(n)[:, 0:w], chunks_d[N_FIRST + EXPERTS * N_EXPERT + layer * N_LAYER + n][:, 0:w])\
                        .then_inc(landed_c[n % RING], 16)
            for t in range(TT):
                sp.wait_ge(vec_f.sem, vec_f.at(f"out {t}"))
                sp.dma_start(out[t * P:(t + 1) * P, :], tmp[:, t, :]).then_inc(stored, 16)
            sp.wait_ge(stored, 16 * TT)

        @block.gpsimd
        def _(pool):
            pool.wait_ge(landed_a[4], 16)
            pool.dma_start(bias, bias_d).then_inc(bias_loaded, 16)

            def rsqrt(n, dst, src, w):
                pool.wait_ge(vec.sem, vec.at(f"power {n} wanted"))
                nc.gpsimd.tensor_tensor(dst, src, con("neghalf")[:, 0:w], ALU.pow).then_inc(pol.sem, pol.did(f"power {n}"))

            pool.wait_ge(constants_loaded, 16)
            rsqrt("c", stat[:, 8:14], stat[:, 0:6], 6)
            pool.wait_ge(vec.sem, vec.at("krT"))
            pool.wait_ge(ten.sem, ten.at("scores 15"))
            nc.gpsimd.tensor_copy(kmT[HD:MQ, 4:8, :], krT[HD:MQ, :].unsqueeze(1).broadcast_to([ROPE_D, 4, 2 * SEQ]))\
                .then_inc(pol.sem, pol.did("kmT rope"))
            for n in range(4):
                if n == 0:
                    pool.wait_ge(ten.sem, ten.at("attended"))
                elif n < 3:
                    pool.wait_ge(vec.sem, vec.at(f"norm {n - 1} 1"))
                if n < 3:
                    pool.dma_start(R[:, 0:2 * D], rows_d[n]).then_inc(rows_loaded, 16)
                for t in range(TT):
                    if n < 3:
                        rsqrt(f"norm {n} {t}", stat[:, 40 + t:41 + t], stat[:, 32 + t:33 + t], 1)
                    else:
                        pool.wait_ge(vec_f.sem, vec_f.at(f"power wanted {t}"))
                        nc.gpsimd.tensor_tensor(stat[:, 40 + t:41 + t], stat[:, 32 + t:33 + t], con("neghalf")[:, 0:1],
                                                ALU.pow).then_inc(pol_f.sem, pol_f.did(f"power norm {t}"))
            pool.sem_inc(pol_c.sem, pol_c.per)
            with pool.Fori(0, 2) as l:
                for n, at, w in (("mix 0", 0, 1), ("mix 1", 1, 1), ("v", 2, 2), ("conf", 4, 2), ("ffn 0", 6, 1), ("ffn 1", 7, 1)):
                    pool.wait_ge(vec_c.sem, vec_c.at(f"power {n} wanted", l))
                    nc.gpsimd.tensor_tensor(stat[:, 40 + at:40 + at + w], stat[:, 32 + at:32 + at + w],
                                            con("neghalf")[:, 0:w], ALU.pow).then_inc(pol_c.sem, pol_c.did(f"power {n}"))
            pool.dma_start(gfin, gfin_d).then_inc(gfin_loaded, 16)
            for t in range(TT):
                pool.wait_ge(vec_f.sem, vec_f.at(f"power wanted final {t}"))
                nc.gpsimd.tensor_tensor(stat[:, 40 + t:41 + t], stat[:, 32 + t:33 + t], con("neghalf")[:, 0:1], ALU.pow)\
                    .then_inc(pol_f.sem, pol_f.did(f"power final {t}"))

        @block.tensor
        def _(pe):
            mm, tr = nc.tensor.matmul, nc.tensor.transpose
            csilu = view(stat, 48, KT, 2)

            def landed(chunk):
                n = FIRST_AT[chunk]
                pe.wait_ge(landed_a[n % RING], 16 * (n // RING + 1))
                return slot(n)

            def used(chunk):
                return f"used {FIRST_AT[chunk]}"

            def rows(w):
                return w.rearrange("p (k n) -> p k n", k=KT)

            def wait_all(*whos):
                for who, name in whos:
                    pe.wait_ge(who.sem, who.at(name))

            def mod_chunk(i):
                w = rows(landed(("mod", 0, i)))
                for k in range(KT):
                    last = mm(bank[i][0:2, :], csilu[:, k, :], w[:, k, :], start=k == 0, stop=k == KT - 1)
                last.then_inc(ten.sem, ten.did(used(("mod", 0, i))))

            def mod_columns(i):
                wait_all((sca, f"mod rows {i}"))
                for j in range(4):
                    at = (4 * i + j) * 2
                    last = tr(bank[7][:, at:at + 2], mod_rows[:, (4 * i + j) * P:(4 * i + j + 1) * P], ident[0:2, 0:2])
                last.then_inc(ten.sem, ten.did(f"mod columns {i}"))

            def mod_sums(*which):
                for c in which:
                    pe.wait_ge(vec.sem, vec.at(f"mod sum {c[1]} {c[2]}"))
                    for j in range(4):
                        at = c[1] * 96 + (4 * c[2] + j) * 2
                        last = mm(bank[7][:, at:at + 2], slot(FIRST_AT[c])[:, j * P:(j + 1) * P], ones[:, 0:2], start=True, stop=True)
                    last.then_inc(ten.sem, ten.did(used(c)))

            def feed_forward(wait, parts, at, last_name):
                ten_p, vec_p, sca_p = parts
                for pos, c in enumerate(FFN_ORDER):
                    n = at[("ffn",) + c]
                    for q in range(quarters(c, FT)):
                        m = (4 * pos + q) % Q_FFN
                        wait(vec_p, f"split {n} {q}")
                        if c[0] == "gu":
                            i, (s, j) = c[1], divmod(q, 2)
                            if i >= 2 and j == 0:
                                wait(*((vec_p, f"product {i - 2}") if s else (sca_p, f"silu {i - 2}")))
                            for k in range(KT):
                                if pos == 0 and q == 0 and k % 2 == 0:
                                    wait(vec_p, f"{last_name} input {k // 2}")
                                w = [part[m][:, k * P:(k + 1) * P] for part in (q_hi, q_lo)]
                                last = matmul3(bank[2 * (i % 2) + s][:, j * SEQ:(j + 1) * SEQ], w, (hT_hi[:, k, :], hT_lo[:, k, :]),
                                               k == 0, k == KT - 1)
                        else:
                            f = 4 * c[1] + q
                            wait(vec_p, f"hid {f // 2}")
                            tiles = {FT - 2: [], FT - 1: [(g, t) for t in range(TT) for g in (f - 1, f)]}.get(f, [(f, 0), (f, 1)])
                            for g, t in tiles:
                                w_at = (m - (f - g)) % Q_FFN
                                h = [part[:, g % KEPT, t * P:(t + 1) * P] for part in (hid_hi, hid_lo)]
                                for half in range(2):
                                    w = [part[w_at][:, half * 512:half * 512 + 512] for part in (q_hi, q_lo)]
                                    last = matmul3(bank[4 + 2 * t + half][:, :], h, w, g == 0, g == FT - 1)
                                if f == FT - 1 and t == 0 and g == f:
                                    last.then_inc(ten_p.sem, ten_p.did(f"{last_name} 0"))
                            if f == FT - 2:
                                continue
                        end = pos == len(FFN_ORDER) - 1 and q == quarters(c, FT) - 1
                        last.then_inc(ten_p.sem, ten_p.did(f"multiplied {n} {q}", *[last_name, f"{last_name} 1"] * end))

            pe.wait_ge(sca.sem, sca.at("silu c"))
            for i in range(4):
                mod_chunk(i)
                if i == 1:
                    pe.wait_ge(constants_loaded, 16)
                if i:
                    mod_columns(i - 1)
            mod_columns(3)

            def bank_free(groups, n):
                if n >= 7:
                    who = sca if by_scalar(n - 7) else vec
                    pe.wait_ge(who.sem, who.at(f"got {groups[n - 7]}"))
                return bank[n % 7]

            n = 0
            pe.wait_ge(tokens_loaded, 32)
            pe.wait_ge(vec.sem, vec.at("mod 0 first"))
            for k in range(KT):
                b = bank_free(GROUPS, n)
                for t in range(4):
                    src = ctx_tok[:, t, :] if t < 2 else x[:, t - 2, :]
                    last = tr(b[:, t * P:(t + 1) * P], src[:, k * P:(k + 1) * P], ident)
                last.then_inc(ten.sem, ten.did(f"full {GROUPS[n]}"))
                n += 1
            for k in range(KT):
                who = sca if by_scalar(k) else vec
                pe.wait_ge(who.sem, who.at(f"got {('h', k)}"))
            w = rows(landed(("proj", "c")))
            for t in range(4):
                b = bank_free(GROUPS, n)
                c0 = 256 if t < 2 else 0
                for k in range(KT):
                    last = mm(b[:, c0:416], hT4[:, k, t * P:(t + 1) * P], w[:, k, c0:416], start=k == 0, stop=k == KT - 1)
                last.then_inc(ten.sem, ten.did(f"full {GROUPS[n]}", *[used(("proj", "c"))] * (t == 3)))
                n += 1
                mod_sums(*MODS[0:1] * (t == 3))
            w = rows(landed(("proj", "ka")))
            for i in range(4):
                b = bank_free(GROUPS, n)
                for k in range(KT):
                    last = mm(b[:, :], w[:, k, i * P:(i + 1) * P], hT4[:, k, :], start=k == 0, stop=k == KT - 1)
                last.then_inc(ten.sem, ten.did(f"full {GROUPS[n]}", *[used(("proj", "ka"))] * (i == 3)))
                n += 1
                mod_sums(*MODS[(i + 1) // 2:(i + 3) // 2] * (i % 2))
            w = rows(landed(("proj", "qa")))
            for i in range(2):
                b = bank_free(GROUPS, n)
                for j in range(2):
                    for k in range(KT):
                        last = mm(b[:, j * SEQ:(j + 1) * SEQ], w[:, k, (2 * i + j) * P:(2 * i + j + 1) * P],
                                  hT4[:, k, SEQ:2 * SEQ], start=k == 0, stop=k == KT - 1)
                last.then_inc(ten.sem, ten.did(f"full {GROUPS[n]}", *[used(("proj", "qa"))] * (i == 1)))
                n += 1
            mod_sums(MODS[3])
            w = rows(landed(("proj", "va")))
            for t in range(4):
                b = bank_free(GROUPS, n)
                for k in range(KT):
                    last = mm(b[:, :], hT4[:, k, t * P:(t + 1) * P], w[:, k, :], start=k == 0, stop=k == KT - 1)
                last.then_inc(ten.sem, ten.did(f"full {GROUPS[n]}", *[used(("proj", "va"))] * (t == 3)))
                n += 1
                if t % 2:
                    mod_sums(*MODS[t + 3:t + 5])

            wait_all((vec, "codes normed"), (vec, f"got {('va', 2)}"), (sca, f"got {('va', 3)}"))
            for t in range(TT):
                for j in range(2):
                    last = tr(bank[0][:, j * SEQ + t * P:j * SEQ + (t + 1) * P], c_tok[:, 2 + t, j * P:(j + 1) * P], ident)
            for t in range(4):
                last = tr(bank[1][:, t * P:(t + 1) * P], c_tok[:, t, 256:384], ident)
            for t in range(4):
                last = tr(bank[2][0:MQ, t * P:(t + 1) * P], c_tok[:, t, 416 - MQ:416], ident)
            last.then_inc(ten.sem, ten.did("codes transposed"))
            mod_sums(MODS[PROJ_MODS - 1])
            wait_all((vec, "krT"))
            pe.wait_ge(bias_loaded, 16)

            def scores(u):
                h, t = (u % 16) // 2, u % 2
                b = bank[u % 3]
                if u % 16 >= 3:
                    pe.wait_ge(sca.sem, sca.at(f"exp {u - 3}"))
                if u < 16:
                    s = slice(HD * (h % 2), HD * (h % 2) + HD)
                    mm(b[:, :], qaT[s, h // 2, t * P:(t + 1) * P], kaT[s, h // 2, :], start=True, stop=False)
                    last = mm(b[:, SEQ:], ident, bias[:, t, h, :], start=False, stop=True)
                else:
                    if u == 24:
                        wait_all((pol, "kmT rope"))
                    last = mm(b[:, :], qmT[0:MQ, h, t * P:(t + 1) * P], kmT[0:MQ, h, :], start=True, stop=True)
                last.then_inc(ten.sem, ten.did(f"scores {u}"))

            def transposed(u):
                pe.wait_ge(sca.sem, sca.at(f"exp {u}"))
                if u % 16 >= 2:
                    wait_all((sca, f"probsT {u - 2}"))
                for k in range(4):
                    last = tr(bank[3 + u % 2][:, k * P:(k + 1) * P], probs[:, u % 3, k * P:(k + 1) * P], ident)
                last.then_inc(ten.sem, ten.did(f"probs transposed {u}"))

            def attend(u):
                h = (u % 16) // 2
                v = va if u < 16 else vm
                wait_all((sca, f"probsT {u}"))
                if u % 16 >= 2:
                    wait_all((sca, f"o {u - 2}"))
                for k in range(4):
                    last = mm(bank[5 + u % 2][:, 0:HD], probsT[:, u % 2, k * P:(k + 1) * P], v[:, k, h * HD:(h + 1) * HD],
                              start=k == 0, stop=k == 3)
                last.then_inc(ten.sem, ten.did(f"attended {u}", *["attended"] * (u == 31)))

            def units(first, mods):
                scores(first)
                scores(first + 1)
                transposed(first)
                for u in range(16):
                    if u + 2 < 16:
                        scores(first + u + 2)
                    if u + 1 < 16:
                        transposed(first + u + 1)
                    mod_sums(*mods[3 * (u - 1) // 8 if u else 0:3 * u // 8])
                    attend(first + u)
                mod_sums(*mods[3 * 15 // 8:])

            units(0, MODS[PROJ_MODS:PROJ_MODS + NA_MODS])

            wait_all((sca, "o 15"), (vec, "krT"))
            w = landed(("up",))
            wv = w[:, 1536:2560].rearrange("p (h t d) -> p h t d", h=HEADS, t=2)
            for n, g in enumerate(UP_GROUPS):
                b = bank_free(UP_GROUPS, n)
                if g[0] == "qup":
                    t, half = g[1:]
                    for k in range(2):
                        last = mm(b[:, 0:384], qcT[:, k, t * P:(t + 1) * P], w[:, k * 768 + half * 384:k * 768 + half * 384 + 384],
                                  start=k == 0, stop=k == 1)
                elif g[0] == "v":
                    last = mm(b[:, :], kvcT[:, g[1] * P:(g[1] + 1) * P], wv[:, :, 1, :], start=True, stop=True)
                elif g[0] == "kn":
                    last = mm(b[0:HD, :], wv[:, g[1], 0, :], kvcT, start=True, stop=True)
                else:
                    if g[1] == 0:
                        wait_all((vec, "q rope"))
                    for j in range(2):
                        for t in range(TT):
                            h = 2 * g[1] + j
                            last = tr(b[0:MQ, j * SEQ + t * P:j * SEQ + (t + 1) * P], qm_tok[:, t, h * MQ:(h + 1) * MQ], ident)
                last.then_inc(ten.sem, ten.did(f"full {g}", *[used(("up",))] * (g == ("kn", 7))))
            for g in UP_GROUPS[-7:]:
                n = UP_GROUPS.index(g)
                wait_all((sca if by_scalar(n) else vec, f"got {g}"))
            wait_all((sca, "kmT rope"))
            units(16, MODS[PROJ_MODS + NA_MODS:])

            wait_all((sca, "o 31"), (vec, "mod all"))
            for b in range(4):
                for j in range(2):
                    for t in range(TT):
                        k = 2 * b + j
                        last = tr(bank[b][:, j * SEQ + t * P:j * SEQ + (t + 1) * P], o_tok[:, t, k * P:(k + 1) * P], ident)
                last.then_inc(ten.sem, ten.did(f"o transposed {b}"))
            def gate_rows(n, banks):
                for k in range(KT):
                    wait_all((sca, f"diag {n} {k}"))
                    last = mm(bank[banks[k // 4]][:, (k % 4) * P:(k % 4 + 1) * P], ones, diag[k % 4], start=True, stop=True)
                    last.then_inc(ten.sem, ten.did(f"gate {n} {k}"))

            def transpose_normed(n):
                for t in range(TT):
                    wait_all((vec, f"normed {n} {t}"))
                    for k in range(KT):
                        at = (k % 2) * SEQ + t * P
                        last = tr(bank[k // 2][:, at:at + P], tmp[:, t, k * P:(k + 1) * P], ident)
                        if t == TT - 1 and k % 2:
                            last.then_inc(ten.sem, ten.did(f"x {n} transposed {k // 2}"))

            gate_rows(0, (5, 7))
            w_out = [rows(landed(("out", half))) for half in range(2)]
            for t in range(TT):
                for half in range(2):
                    if t == 0 and half:
                        wait_all((sca, "gate row 0"))
                    for k in range(KT):
                        if t == 0 and half == 0 and k % 2 == 0:
                            wait_all((sca if k % 4 else vec, f"oT {k // 2}"))
                        last = mm(bank[4 + 2 * t + half][:, :], oT[:, k, t * P:(t + 1) * P], w_out[half][:, k, :],
                                  start=k == 0, stop=k == KT - 1)
                    last.then_inc(ten.sem, ten.did(*[f"y 0 {t}"] * half, *[used(("out", half))] * t, *["y 0"] * (t * half)))

            gate_rows(1, (0, 1))
            wait_all((sca, "gate row 1"))
            transpose_normed(0)
            def wait(who, name):
                pe.wait_ge(who.sem, who.at(name))

            feed_forward(wait, (ten, vec, sca), FIRST_AT, "y 1")

            gate_rows(2, (0, 1))
            wait_all((sca, "gate row 2"))
            w = landed(("pool",))
            means = w[:, MEANS_AT:].rearrange("p (g s n) -> p g s n", g=4, s=TT)
            wait_all((vec, "normed 1 0"), (vec, "normed 1 1"))
            for b in range(4):
                for j in range(2):
                    for s in range(TT):
                        k = 2 * b + j
                        last = mm(bank[b][:, j * SEQ:(j + 1) * SEQ], tmp[:, s, k * P:(k + 1) * P], means[:, b, s, :],
                                  start=s == 0, stop=s == TT - 1)
                last.then_inc(ten.sem, ten.did(f"means {b}"))
            for g in range(4):
                wait_all((sca if g % 2 else vec, f"mixT {g}"))
                for t in range(TT):
                    for k in range(2):
                        last = mm(bank[4 + 2 * t + g // 2][:, (g % 2) * 256:(g % 2) * 256 + 256],
                                  mixT[:, 2 * g + k, t * P:(t + 1) * P], w[:, (2 * g + k) * 256:(2 * g + k + 1) * 256],
                                  start=k == 0, stop=k == 1)
            last.then_inc(ten.sem, ten.did("y 2 0", "y 2 1", used(("pool",))))
            gate_rows(3, (0, 1))
            wait_all((sca, "gate row 3"))
            transpose_normed(2)
            wait_all((sca, "hT 2 3"), (vec, "hT 2 2"))
            router = view(cols, COLS["router"][0], KT, EXPERTS)
            for t in range(TT):
                for k in range(KT):
                    last = mm(bank[4][:, t * 8:t * 8 + 8], hT[:, k, t * P:(t + 1) * P], router[:, k, :],
                              start=k == 0, stop=k == KT - 1)
            last.then_inc(ten.sem, ten.did("logits"))
            wait_all((vec, "selected"))
            before = con("before")
            sel = [route[:, 11, 8 * t:8 * t + 8] for t in range(TT)]
            mm(bank[3][:, 0:8], before, sel[0], start=True, stop=True)
            mm(bank[3][:, 8:16], ones, sel[0], start=True, stop=False)
            mm(bank[3][:, 8:16], before, sel[1], start=False, stop=True)
            mm(bank[3][:, 16:24], ones, sel[0], start=True, stop=False)
            mm(bank[3][:, 16:24], ones, sel[1], start=False, stop=True).then_inc(ten.sem, ten.did("places"))

            def gather(b):
                for i in range(4):
                    k = 4 * b + i
                    for t in range(TT):
                        last = mm(bank[6 * b][:, i * P:(i + 1) * P], x[:, t, k * P:(k + 1) * P], pick[:, t, :],
                                  start=t == 0, stop=t == TT - 1)
                return last

            wait_all((vec, "picked"))
            gather(0)
            gather(1).then_inc(ten.sem, ten.did("gathered"))
            wait_all((vec, "passes"), (vec, "xg 1"))
            passes = pe.value_load(n_passes[0:1, 0:1], min_val=1, max_val=PASSES_MAX)
            pe.sem_inc(ten_b.sem, ten_b.per)
            with pe.Fori(0, passes) as p:
                with pe.Fori(0, EXPERTS) as e:
                    turn = p * EXPERTS + e

                    def wait_b(who, name):
                        pe.wait_ge(who.sem, who.at(name, turn))

                    def wait_was(who, name):
                        pe.wait_ge(who.sem, who.was(name, turn))

                    def did(*names):
                        return ten_b.did(*names)

                    def scatter(t):
                        for half in range(2):
                            if t == 1:
                                wait_b(vec_b, f"added {half}")
                            mm(bank[6 + half][:, :], spread[:, t * P:(t + 1) * P], outE[:, half * 512:half * 512 + 512],
                               start=True, stop=True).then_inc(ten_b.sem, did(f"scattered {2 * t + half}"))

                    def transpose_hidden(i):
                        wait_b(vec_b, f"product {i}")
                        if i >= 2:
                            wait_b(vec_b, f"hid {i - 2}")
                        elif i == 1:
                            wait_was(vec_b, "hid 13")
                        else:
                            wait_was(sca_b, "xm 0")
                        for j in range(2):
                            last = tr(bank[i % 2][:, j * P:(j + 1) * P], hid_tok[:, i % 2, j * P:(j + 1) * P], ident)
                        last.then_inc(ten_b.sem, did(f"transposed {i}"))

                    for n, c in enumerate(MOE_ORDER):
                        for q in range(4):
                            m = (4 * n + q) % Q_MOE
                            wait_b(vec_b, f"split {n} {q}")
                            if c[0] == "gu":
                                i = c[1]
                                if q == 0:
                                    if i >= 2:
                                        wait_b(vec_b, f"product {i - 2}")
                                    else:
                                        wait_was(vec_b, f"product {EFT // 2 - 2 + i}")
                                if i == 0 and q % 2 == 0:
                                    wait_was(vec_b, f"xg {q // 2}")
                                for k in (2 * q, 2 * q + 1):
                                    w = [part[m][:, (k % 2) * 512:(k % 2) * 512 + 512] for part in (q_hi, q_lo)]
                                    last = matmul3(bank[2 + i % 2][:, :], (xg_hi[:, k, :], xg_lo[:, k, :]), w, k == 0, k == KT - 1)
                            else:
                                f = 4 * c[1] + q
                                wait_b(vec_b, f"hid {f // 2}")
                                if f == 0:
                                    wait_b(sca_b, "outE")
                                    wait_b(vec_b, "outE")
                                for half in range(2):
                                    w = [part[m][:, half * 512:half * 512 + 512] for part in (q_hi, q_lo)]
                                    last = matmul3(bank[4 + half][:, :], (hidE_hi[:, f % KEPT, :], hidE_lo[:, f % KEPT, :]), w,
                                                   f == 0, f == EFT - 1)
                            last.then_inc(ten_b.sem, did(f"multiplied {n} {q}"))
                            if q == 1 and n and MOE_ORDER[n - 1][0] == "gu" and MOE_ORDER[n - 1][1] < EFT // 2 - 1:
                                transpose_hidden(MOE_ORDER[n - 1][1])
                            if q == 3 and n == 1:
                                wait_b(sca_b, "outE")
                                wait_b(vec_b, "outE")
                                wait_was(vec_b, "xm 1")
                                wait_was(sca_b, "spread")
                                scatter(0)
                            if q == 3 and n == 2:
                                scatter(1)
                            if q == 3 and n == 3:
                                wait_b(vec_b, "added 3")
                                wait_was(vec_b, "pickg")
                                for t in range(TT):
                                    last = tr(bank[7][:, t * P:(t + 1) * P], pickg[:, t, :], ident)
                                last.then_inc(ten_b.sem, did("spread"))
                            if q == 3 and c == ("gu", EFT // 2 - 1):
                                wait_b(vec_b, "picked")
                                wait_b(vec_b, "hid 12")
                                gather(0).then_inc(ten_b.sem, did("gathered 0"))
                                transpose_hidden(EFT // 2 - 1)
                                gather(1).then_inc(ten_b.sem, did("gathered 1"))
            turns = passes * EXPERTS
            pe.wait_ge(vec_b.sem, vec_b.was("xg 1", turns))
            wait_all((sca_f, "outE"), (vec_f, "outE"))
            pe.wait_ge(vec_b.sem, vec_b.was("hid 13", turns))
            pe.wait_ge(sca_b.sem, sca_b.was("spread", turns))
            for t in range(TT):
                for half in range(2):
                    b = bank[(6, 7, 0, 1)[2 * t + half]]
                    mm(b[:, :], spread[:, t * P:(t + 1) * P], outE[:, half * 512:half * 512 + 512], start=True, stop=True)\
                        .then_inc(ten_f.sem, ten_f.did(f"scattered {t} {half}"))
            for i in range(2 * KT):
                wait_all((sca_f, f"diag {i}"))
                mm(bank[2 + i // 4][:, (i % 4) * P:(i % 4 + 1) * P], ones, diag[i % 4], start=True, stop=True)\
                    .then_inc(ten_f.sem, ten_f.did(f"row {i}"))

            for i in range(RING):
                pe.wait_ge(landed_b[i], passes * (16 * EXPERTS * N_EXPERT // RING) + 16)
                pe.sem_inc(landed_c[i], 16)
            pe.wait_ge(vec_f.sem, vec_f.at("x 1"))
            pe.sem_inc(ten_c.sem, ten_c.per)
            with pe.Fori(0, 2) as l:

                def chunk(c):
                    n = LAYER_AT[c]
                    pe.wait_ge(landed_c[n % RING], layer_landed(n, l))
                    return slot(n)

                def done(*names):
                    return ten_c.did(*names)

                def used_c(c):
                    return f"used {LAYER_AT[c]}"

                def wait(who, name):
                    pe.wait_ge(who.sem, who.at(name, l))

                def transpose_scaled(name):
                    for t in range(TT):
                        wait(sca_c, f"{name} scaled {t}")
                        for k in range(KT):
                            at = (k % 2) * SEQ + t * P
                            last = tr(bank[k // 2][:, at:at + P], tmp[:, t, k * P:(k + 1) * P], ident)
                            if t == TT - 1 and k % 2:
                                last.then_inc(ten_c.sem, done(f"{name} transposed {k // 2}"))

                def by_tokens(c, name, first, width):
                    w = chunk(("mix", c))
                    w = w[:, 0:KT * width].rearrange("p (k n) -> p k n", k=KT)
                    for t in range(TT):
                        for k in range(KT):
                            last = mm(bank[first + t][:, 0:width], hT[:, k, t * P:(t + 1) * P], w[:, k, :],
                                      start=k == 0, stop=k == KT - 1)
                        last.then_inc(ten_c.sem, done(f"{name} {t}", *[used_c(("mix", c))] * (t == 1)))

                def by_features(c, name, first):
                    w = rows(chunk(("mix", c)))
                    for i in range(2):
                        for s in range(2):
                            for k in range(KT):
                                last = mm(bank[first + i][:, s * SEQ:(s + 1) * SEQ], w[:, k, s * 256 + i * P:s * 256 + (i + 1) * P],
                                          hT[:, k, :], start=k == 0, stop=k == KT - 1)
                        last.then_inc(ten_c.sem, done(f"{name} {i}", *[used_c(("mix", c))] * (i == 1)))

                pe.wait_ge(vec_c.sem, vec_c.was("x 1", l))
                transpose_scaled("mix")
                wait(vec_c, "mix hT 2")
                wait(sca_c, "mix hT 3")
                by_tokens("qi", "qi", 4, QI_W)
                by_features("dd", "dd", 6)
                wait(vec_c, "qi rope")
                for t in range(TT):
                    for i in range(2):
                        tr(bank[0][:, i * SEQ + t * P:i * SEQ + (t + 1) * P], qir[:, t, i * P:(i + 1) * P], ident)
                for t in range(TT):
                    last = tr(bank[1][:, t * P:(t + 1) * P], qir[:, t, 2 * P:3 * P], ident)
                last.then_inc(ten_c.sem, done("qi transposed"))
                wait(sca_c, "qi got 1")
                by_tokens("qk", "qk", 4, 512)
                wait(sca_c, "qiT")
                for t in range(TT):
                    for i in range(4):
                        s = slice(HD * (i % 2), HD * (i % 2) + HD)
                        last = mm(bank[2 + (i % 2) - 2 * t][:, (i // 2) * SEQ:(i // 2 + 1) * SEQ],
                                  qiT[s, i // 2, t * P:(t + 1) * P], kiT[s, :], start=True, stop=True)
                    last.then_inc(ten_c.sem, done(f"index scores {t}"))
                wait(sca_c, "sig 1")
                wait(vec_c, "yp 1")
                by_tokens("vg", "vg", 6, 512)
                wait(sca_c, "rel 0")
                by_features("ch", "ch", 2)
                wait(sca_c, "qk got 1")
                by_features("bu", "bu", 4)
                wait(vec_c, "qk rope")
                wait(sca_c, "rel 1")
                for i in range(2):
                    for t in range(TT):
                        tr(bank[0][:, i * SEQ + t * P:i * SEQ + (t + 1) * P], qkr[:, t, i * P:(i + 1) * P], ident)
                        last = tr(bank[1][:, i * SEQ + t * P:i * SEQ + (t + 1) * P], qkr[:, t, 256 + i * P:256 + (i + 1) * P], ident)
                last.then_inc(ten_c.sem, done("qk transposed"))
                wait(vec_c, "vn")
                wait(sca_c, "vg got 1")
                for h in range(4):
                    for t in range(TT):
                        s = slice(HD * (h % 2), HD * (h % 2) + HD)
                        last = mm(bank[6 + h // 2][s, t * P:(t + 1) * P], vn[:, t, h * HD:(h + 1) * HD], wsm[:, h, :],
                                  start=True, stop=True)
                last.then_inc(ten_c.sem, done("gated"))
                wait(vec_c, "conv 1")
                wait(sca_c, "ch got 1")
                for t in range(TT):
                    for i in range(2):
                        last = tr(bank[2][:, t * SEQ + i * P:t * SEQ + (i + 1) * P], conv[:, i, t * P:(t + 1) * P], ident)
                last.then_inc(ten_c.sem, done("conv transposed"))

                wait(vec_c, "kT")
                wait(sca_c, "qT")

                def scores_c(u):
                    h, t = u // 2, u % 2
                    if u == 2:
                        wait(vec_c, "ynorm 1")
                    if u >= 3:
                        wait(vec_c, f"masked {u - 3}")
                    s = slice(HD * (h % 2), HD * (h % 2) + HD)
                    mm(bank[u % 3][:, 0:SEQ], qT[s, h // 2, t * P:(t + 1) * P], kT[s, h // 2, :], start=True, stop=True)\
                        .then_inc(ten_c.sem, done(f"scores {u}"))

                def transposed_c(u):
                    wait(sca_c, f"exp {u}")
                    if u >= 2:
                        wait(sca_c, f"probsT {u - 2}")
                    for k in range(TT):
                        last = tr(bank[4 + u % 2][:, k * P:(k + 1) * P], probs2[:, u % 3, k * P:(k + 1) * P], ident)
                    last.then_inc(ten_c.sem, done(f"probs transposed {u}"))

                def attend_c(u):
                    h = u // 2
                    wait(sca_c, f"probsT {u}")
                    if u >= 2:
                        wait(vec_c, f"o {u - 2}")
                    for k in range(TT):
                        last = mm(bank[6 + u % 2][:, 0:HD], probsT2[:, u % 2, k * P:(k + 1) * P],
                                  vg_tok[:, k, h * HD:(h + 1) * HD], start=k == 0, stop=k == 1)
                    last.then_inc(ten_c.sem, done(f"attended {u}"))

                scores_c(0)
                scores_c(1)
                wait(vec_c, "y_b 1")
                wait(sca_c, "bu got 1")
                transposed_c(0)
                for u in range(8):
                    if u == 3:
                        wait(vec_c, "ynorm 1")
                        for t in range(TT):
                            for i in range(2):
                                last = tr(bank[3][:, i * SEQ + t * P:i * SEQ + (t + 1) * P], ynorm[:, t, i * P:(i + 1) * P], ident)
                        last.then_inc(ten_c.sem, done("ynorm transposed"))
                    if u + 2 < 8:
                        scores_c(u + 2)
                    if u + 1 < 8:
                        transposed_c(u + 1)
                    attend_c(u)
                wait(vec_c, "o 7")
                for i in range(2):
                    for t in range(TT):
                        last = tr(bank[0][:, i * SEQ + t * P:i * SEQ + (t + 1) * P], o_c[:, t, i * P:(i + 1) * P], ident)
                last.then_inc(ten_c.sem, done("o transposed"))
                w_out = [rows(chunk(("out", half))) for half in range(2)]
                for t in range(TT):
                    for half in range(2):
                        for k in range(KT):
                            if t == 0 and half == 0 and k in (4, 6):
                                wait(*((vec_c, "y_c") if k == 4 else (sca_c, "y_d 1")))
                            last = mm(bank[4 + 2 * t + half][:, :], catT[:, k, t * P:(t + 1) * P], w_out[half][:, k, :],
                                      start=k == 0, stop=k == KT - 1)
                        last.then_inc(ten_c.sem, done(*[f"y 0 {t}"] * half, *[used_c(("out", half))] * t))
                transpose_scaled("ffn")
                feed_forward(wait, (ten_c, vec_c, sca_c), LAYER_AT, "y 1")

        def gate_col(n, k):
            layer, part = n // 2, n % 2
            return mod[:, layer, 16 + 24 * part + k, 0:1]

        @block.vector
        def _(dve):
            v = nc.vector

            def hold():
                dve.wait_ge(vec.sem, vec.last())

            def after(*whos):
                for who, name in whos:
                    dve.wait_ge(who.sem, who.at(name))

            def sign(ins, *names):
                ins.then_inc(vec.sem, vec.did(*names))

            dve.wait_ge(columns_loaded, 16)
            dve.wait_ge(constants_loaded, 16)
            after((ten, "mod columns 3"))
            modb = [cols[:, COLS[f"modb{i}"][0]:COLS[f"modb{i}"][0] + 48] for i in range(2)]

            def mod_out(layer, j0, j1, plus_one, *names):
                n = j1 - j0
                src = bank[7][:, layer * 96 + 2 * j0:layer * 96 + 2 * j1].rearrange("p (j c) -> p j c", c=2)
                v.tensor_tensor(mod[:, layer, j0:j1, :], src, modb[layer][:, j0:j1].unsqueeze(2).broadcast_to([P, n, 2]), ALU.add)\
                    .then_inc(vec.sem, vec.did())
                hold()
                for i, j in enumerate(plus_one):
                    v.tensor_scalar(mod[:, layer, j:j + 8, :], mod[:, layer, j:j + 8, :], 1.0, None, ALU.add)\
                        .then_inc(vec.sem, vec.did(*names * (i == len(plus_one) - 1)))

            mod_out(0, 0, 16, [8], "mod 0 first")
            hold()

            def got(groups, n):
                after((ten, f"full {groups[n]}"))
                return bank[n % 7], f"got {groups[n]}"

            def mod_step(s):
                c, k = MODS[s // KT], s % KT
                n = FIRST_AT[c]
                w = slot(n).rearrange("p (k n) -> p k n", k=KT)
                ck = stat[:, 48 + 2 * k:49 + 2 * k]
                if k == 0:
                    dve.wait_ge(landed_a[n % RING], 16 * (n // RING + 1))
                    v.tensor_scalar(w[:, 0, :], w[:, 0, :], ck, None, ALU.mult).then_inc(vec.sem, vec.did(f"mod step {s}"))
                else:
                    after((vec, f"mod step {s - 1}"))
                    v.scalar_tensor_tensor(w[:, 0, :], w[:, k, :], ck, w[:, 0, :], ALU.mult, ALU.add)\
                        .then_inc(vec.sem, vec.did(f"mod step {s}", *[f"mod sum {c[1]} {c[2]}"] * (k == KT - 1)))

            msin, mcos = con("msin", 2, 2, 8), con("mcos", 2, 32)

            def norm_codes():
                after((sca, f"got {('c', 1)}"), (sca, f"got {('c', 3)}"))
                hold()
                parts = [(2, 0, 256), (3, 0, 256)] + [(t, 256, 384) for t in range(4)]
                for i, (t, a, b) in enumerate(parts):
                    v.tensor_tensor_reduce(out=probs[:, 0, 0:b - a], in0=c_tok[:, t, a:b], in1=c_tok[:, t, a:b], scale=1.0,
                                           scalar=0.0, op0=ALU.mult, op1=ALU.add, accum_out=stat[:, 16 + i:17 + i])\
                        .then_inc(vec.sem, vec.did())
                    hold()
                v.tensor_scalar(stat[:, 0:2], stat[:, 16:18], 1.0 / 256, RMS_EPS, ALU.mult, ALU.add).then_inc(vec.sem, vec.did())
                v.tensor_scalar(stat[:, 2:6], stat[:, 18:22], 1.0 / 128, RMS_EPS, ALU.mult, ALU.add)\
                    .then_inc(vec.sem, vec.did("power c wanted"))
                kr = c_tok[:, 2:4, 384:416]
                kr5 = kr.rearrange("p t (a s f) -> p t a s f", a=2, s=2)
                ra = rope_a[:, 0:64].rearrange("p (t n) -> p t n", t=2)
                ra5 = ra.rearrange("p t (a s f) -> p t a s f", a=2, s=2)
                rb = [rope_b[:, 32 * i:32 * i + 32].rearrange("p (t a f) -> p t a f", t=2, a=2) for i in range(2)]
                v.tensor_tensor(ra, kr, mcos, ALU.mult).then_inc(vec.sem, vec.did())
                v.tensor_tensor(rb[0], kr5[:, :, :, 1, :], msin, ALU.mult).then_inc(vec.sem, vec.did())
                v.tensor_tensor(rb[1], kr5[:, :, :, 0, :], msin, ALU.mult).then_inc(vec.sem, vec.did())
                hold()
                v.tensor_tensor(kr5[:, :, :, 0, :], ra5[:, :, :, 0, :], rb[0], ALU.subtract).then_inc(vec.sem, vec.did())
                v.tensor_tensor(kr5[:, :, :, 1, :], ra5[:, :, :, 1, :], rb[1], ALU.add).then_inc(vec.sem, vec.did())
                after((pol, "power c"))
                for i, (t, a, b) in enumerate(parts):
                    v.tensor_scalar(c_tok[:, t, a:b], c_tok[:, t, a:b], stat[:, 8 + i:9 + i], None, ALU.mult)\
                        .then_inc(vec.sem, vec.did(*["codes normed"] * (i == 5)))

            MODS_BEHIND = {8: (0,), 10: (1,), 12: (2,), 14: (3,), 16: (4, 5), 18: (6,), 20: (7, 8)}
            for n, g in enumerate(GROUPS):
                if by_scalar(n):
                    continue
                b, name = got(GROUPS, n)
                if g[0] == "h":
                    k = g[1]
                    for c in range(2):
                        v.tensor_scalar(hT4[:, k, (1 - c) * SEQ:(2 - c) * SEQ], b[:, (1 - c) * SEQ:(2 - c) * SEQ],
                                        mod[:, 0, 8 + k, c:c + 1], mod[:, 0, k, c:c + 1], ALU.mult, ALU.add)\
                            .then_inc(vec.sem, vec.did(*[name] * c))
                elif g[0] == "c":
                    t, c0 = g[1], 256 if g[1] < 2 else 0
                    v.tensor_copy(c_tok[:, t, c0:], b[:, c0:416]).then_inc(vec.sem, vec.did(name))
                elif g[0] == "ka":
                    v.tensor_copy(kaT[:, g[1], :], b[:, :]).then_inc(vec.sem, vec.did(name))
                elif g[0] == "qa":
                    v.tensor_scalar(qaT[:, 2 * g[1]:2 * g[1] + 2, :], b[:, :].rearrange("p (j n) -> p j n", j=2),
                                    NA_SCALE, None, ALU.mult).then_inc(vec.sem, vec.did(name))
                else:
                    v.tensor_copy(va[:, g[1], :], b[:, :]).then_inc(vec.sem, vec.did(name))
                if n == 12:
                    norm_codes()
                for c in MODS_BEHIND.get(n, ()):
                    for k in range(KT):
                        mod_step(c * KT + k)

            after((ten, "codes transposed"))
            for j in range(2):
                v.tensor_scalar(qcT[:, j, :], bank[0][:, j * SEQ:(j + 1) * SEQ], col("qn", j), None, ALU.mult)\
                    .then_inc(vec.sem, vec.did())
            v.tensor_scalar(kvcT, bank[1][:, :], col("kvn"), None, ALU.mult).then_inc(vec.sem, vec.did())
            v.tensor_copy(krT[HD:MQ, :], bank[2][HD:MQ, :]).then_inc(vec.sem, vec.did("krT"))

            def peak(u):
                after((ten, f"scores {u}"))
                v.tensor_reduce(nmax[:, u:u + 1], bank[u % 3][:, :], axis=AX_X, op=ALU.max, negate=True)\
                    .then_inc(vec.sem, vec.did(f"nmax {u}"))

            def inverse_sum(u):
                after((sca, f"exp {u}"))
                v.reciprocal(rinv[:, u:u + 1], rsum[:, u:u + 1]).then_inc(vec.sem, vec.did(f"inverse {u}"))

            def units(first, mods_at, mods):
                def mod_part(i):
                    if i < mods * KT:
                        mod_step(mods_at * KT + i)

                peak(first)
                peak(first + 1)
                for u in range(16):
                    if u + 2 < 16:
                        peak(first + u + 2)
                    mod_part(3 * u)
                    mod_part(3 * u + 1)
                    inverse_sum(first + u)
                    mod_part(3 * u + 2)

            units(0, PROJ_MODS, NA_MODS)
            for n, g in enumerate(UP_GROUPS):
                if not by_scalar(n):
                    b, name = got(UP_GROUPS, n)
                    if g[0] == "qup":
                        v.tensor_scalar(qm_tok[:, g[1], g[2] * 384:g[2] * 384 + 384], b[:, 0:384], MLA_SCALE, None, ALU.mult)\
                            .then_inc(vec.sem, vec.did(name))
                    elif g[0] == "v":
                        v.tensor_copy(vm[:, g[1], :], b[:, :]).then_inc(vec.sem, vec.did(name))
                    elif g[0] == "kn":
                        v.tensor_copy(kmT[0:HD, g[1], :], b[0:HD, :]).then_inc(vec.sem, vec.did(name))
                    else:
                        v.tensor_copy(qmT[0:MQ, 2 * g[1]:2 * g[1] + 2, :], b[0:MQ, :].rearrange("p (j n) -> p j n", j=2))\
                            .then_inc(vec.sem, vec.did(name))
                if g == ("qup", 1, 1):
                    after((sca, f"got {('qup', 0, 1)}"), (sca, f"got {('qup', 1, 1)}"))
                    for t in range(TT):
                        q = qm_tok[:, t, :].rearrange("p (h c) -> p h c", h=HEADS)[:, :, HD:MQ]
                        q5 = q.rearrange("p h (a s f) -> p h a s f", a=2, s=2)
                        ra = rope_a.rearrange("p (h n) -> p h n", h=HEADS)
                        ra5 = ra.rearrange("p h (a s f) -> p h a s f", a=2, s=2)
                        rb = [rope_b[:, 128 * i:128 * i + 128].rearrange("p (h a f) -> p h a f", h=HEADS, a=2) for i in range(2)]
                        hold()
                        v.tensor_tensor(ra, q, mcos[:, t, :].unsqueeze(1).broadcast_to([P, HEADS, ROPE_D]), ALU.mult)\
                            .then_inc(vec.sem, vec.did())
                        s = msin[:, t, :, :].unsqueeze(1).broadcast_to([P, HEADS, 2, 8])
                        v.tensor_tensor(rb[0], q5[:, :, :, 1, :], s, ALU.mult).then_inc(vec.sem, vec.did())
                        v.tensor_tensor(rb[1], q5[:, :, :, 0, :], s, ALU.mult).then_inc(vec.sem, vec.did())
                        hold()
                        v.tensor_tensor(q5[:, :, :, 0, :], ra5[:, :, :, 0, :], rb[0], ALU.subtract).then_inc(vec.sem, vec.did())
                        v.tensor_tensor(q5[:, :, :, 1, :], ra5[:, :, :, 1, :], rb[1], ALU.add)\
                            .then_inc(vec.sem, vec.did(*["q rope"] * (t == 1)))
            units(16, PROJ_MODS + NA_MODS, len(MODS) - PROJ_MODS - NA_MODS)
            after((ten, f"used {FIRST_AT[('mod', 1, 11)]}"))
            mod_out(0, 16, 48, [32])
            mod_out(1, 0, 48, [8, 32], "mod all")
            hold()
            for n, (layer, at) in enumerate(((0, 32), (1, 8), (1, 32))):
                gain, bias_col = [cols[:, COLS[c][0] + 8 * n:COLS[c][0] + 8 * n + 8] for c in ("lng", "lnb")]
                v.tensor_tensor(fold[:, n, 0, :], gain, mod[:, layer, at:at + 8, 0], ALU.mult).then_inc(vec.sem, vec.did())
                v.tensor_tensor(fold[:, n, 1, :], bias_col, mod[:, layer, at:at + 8, 0], ALU.mult).then_inc(vec.sem, vec.did())
            hold()
            for n, (layer, at) in enumerate(((0, 24), (1, 0), (1, 24))):
                v.tensor_tensor(fold[:, n, 1, :], fold[:, n, 1, :], mod[:, layer, at:at + 8, 0], ALU.add).then_inc(vec.sem, vec.did())
            v.tensor_tensor(mod[:, 1, 16:24, 0], mod[:, 1, 16:24, 0], cols[:, COLS["pscale"][0]:COLS["pscale"][0] + 8], ALU.mult)\
                .then_inc(vec.sem, vec.did("mod folded"))

            for b in range(0, 4, 2):
                after((ten, f"o transposed {b}"))
                v.tensor_copy(oT[:, 2 * b:2 * b + 2, :], bank[b][:, :].rearrange("p (j n) -> p j n", j=2))\
                    .then_inc(vec.sem, vec.did(f"oT {b}"))

            def layer_norm(n, y, seq, powered, ready):
                def own():
                    dve.wait_ge(seq.sem, seq.last())

                bn = view(stat, 64, TT, 2, 6)
                mv = view(stat, 88, TT, 2)

                def gated(t):
                    for half in range(2):
                        c = slice(half * 512, half * 512 + 512)
                        v.tensor_tensor(tmp[:, t, c], y(t, half), gate_row[n % 2][:, c], ALU.mult).then_inc(seq.sem, seq.did())

                def moments(t):
                    own()
                    v.scalar_tensor_tensor(x[:, t, :], x[:, t, :], ALPHA, tmp[:, t, :], ALU.mult, ALU.add)\
                        .then_inc(seq.sem, seq.did())
                    own()
                    for half in range(2):
                        v.bn_stats(bn[:, t, half, :], x[:, t, half * 512:half * 512 + 512]).then_inc(seq.sem, seq.did())
                    own()
                    v.bn_aggr(mv[:, t, :], bn[:, t, :, :].rearrange("p a b -> p (a b)")).then_inc(seq.sem, seq.did())
                    own()
                    v.tensor_scalar(stat[:, 32 + t:33 + t], mv[:, t, 1:2], LN_EPS, None, ALU.add)\
                        .then_inc(seq.sem, seq.did(powered[0].format(t=t)))

                def normed(t):
                    who = powered[2]
                    dve.wait_ge(who.sem, who.at(powered[1].format(t=t)))
                    v.tensor_scalar(tmp[:, t, :], x[:, t, :], mv[:, t, 0:1], stat[:, 40 + t:41 + t], ALU.subtract, ALU.mult)\
                        .then_inc(seq.sem, seq.did(f"normed {n} {t}"))

                for t in range(TT):
                    ready(t)
                    gated(t)
                    if t:
                        normed(t - 1)
                    moments(t)
                normed(TT - 1)

            def gain_and_bias(n, seq, rows, t, step, *names):
                if step == 0:
                    if rows:
                        dve.wait_ge(rows_loaded, 16 * rows)
                    else:
                        dve.wait_ge(sca_f.sem, sca_f.at("rows"))
                    dve.wait_ge(seq.sem, seq.at(f"normed {n} {t}"))
                    v.tensor_tensor(x[:, t, :], tmp[:, t, :], ln_g, ALU.mult).then_inc(seq.sem, seq.did(f"gained {n} {t}"))
                else:
                    dve.wait_ge(seq.sem, seq.at(f"gained {n} {t}"))
                    v.tensor_tensor(x[:, t, :], x[:, t, :], ln_b, ALU.add).then_inc(seq.sem, seq.did(*names))

            def first_norm(n):
                after((sca, f"gate row {n}"))
                layer_norm(n, lambda t, half: bank[4 + 2 * t + half][:, :], vec,
                           (f"power norm {n} {{t}} wanted", f"power norm {n} {{t}}", pol),
                           lambda t: after((ten, f"y {n} {t}")))

            def first_update(n, i):
                t, step = divmod(i, 2)
                gain_and_bias(n, vec, n + 1, t, step, f"norm {n} {t}")

            def wait_a(who, name):
                dve.wait_ge(who.sem, who.at(name))

            def low_quarter(wait, parts, at, pos, q):
                sca_p, vec_p = parts[2], parts[1]
                n, m = at[("ffn",) + FFN_ORDER[pos]], (4 * pos + q) % Q_FFN
                wait(sca_p, f"high {n} {q}")
                end = q == quarters(FFN_ORDER[pos], FT) - 1
                v.tensor_tensor(q_lo[m], slot(n)[:, q * QW:(q + 1) * QW], q_hi[m].bitcast(F32), ALU.subtract)\
                    .then_inc(vec_p.sem, vec_p.did(f"split {n} {q}", *[f"split {n}"] * end))

            def input_parts(wait, parts, last_name, source_done, scaled):
                ten_p, vec_p, sca_p = parts
                for b in range(0, 4, 2):
                    wait(ten_p, f"{source_done} transposed {b}")
                    for j in range(2):
                        scaled(hm[:, 2 * b + j, :], bank[b][:, j * SEQ:(j + 1) * SEQ], 2 * b + j)\
                            .then_inc(vec_p.sem, vec_p.did(*[f"{last_name} scaled {b}"] * j))
                for b in range(4):
                    wait(sca_p, f"{last_name} high {b}")
                    v.tensor_tensor(hT_lo[:, 2 * b:2 * b + 2, :], hm[:, 2 * b:2 * b + 2, :],
                                    hT_hi[:, 2 * b:2 * b + 2, :].bitcast(F32), ALU.subtract)\
                        .then_inc(vec_p.sem, vec_p.did(f"{last_name} input {b}"))

            def feed_forward(wait, parts, at, update=None):
                ten_p, vec_p, sca_p = parts
                for pos, c in enumerate(FFN_ORDER):
                    before = FFN_ORDER[pos - 1] if pos else ("d", 0)
                    for q in range(quarters(c, FT)):
                        if 4 * pos + q >= 2:
                            low_quarter(wait, parts, at, pos, q)
                        if update and 2 <= 4 * pos + q < 6:
                            update(4 * pos + q - 2)
                        if before[0] == "gu":
                            i = before[1]
                            pair = lambda a: a.rearrange("p (j n) -> p j n", j=2)
                            if q == 1:
                                wait(ten_p, f"multiplied {at[('ffn',) + before]} 3")
                                wait(sca_p, f"silu {i}")
                                v.tensor_tensor(silu[:, i % 2, :], silu[:, i % 2, :], bank[2 * (i % 2) + 1][:, :], ALU.mult)\
                                    .then_inc(vec_p.sem, vec_p.did(f"product {i}"))
                            if q == 2:
                                wait(sca_p, f"hidden high {i}")
                                f = 2 * i % KEPT
                                v.tensor_tensor(hid_lo[:, f:f + 2, :], pair(silu[:, i % 2, :]),
                                                hid_hi[:, f:f + 2, :].bitcast(F32), ALU.subtract).then_inc(vec_p.sem, vec_p.did(f"hid {i}"))

            first_norm(0)
            first_parts = (ten, vec, sca)
            low_quarter(wait_a, first_parts, FIRST_AT, 0, 0)
            low_quarter(wait_a, first_parts, FIRST_AT, 0, 1)
            input_parts(wait_a, first_parts, "y 1", "x 0",
                        lambda dst, src, k: v.tensor_scalar(dst, src, fold[:, 0, 0, k:k + 1], fold[:, 0, 1, k:k + 1],
                                                            ALU.mult, ALU.add))
            feed_forward(wait_a, first_parts, FIRST_AT, lambda i: first_update(0, i))
            first_norm(1)
            for b in range(0, 4, 2):
                after((ten, f"means {b}"))
                for j in range(2):
                    k = 2 * b + j
                    v.tensor_scalar(mixT[:, k, :], bank[b][:, j * SEQ:(j + 1) * SEQ], fold[:, 1, 0, k:k + 1], None, ALU.mult)\
                        .then_inc(vec.sem, vec.did(*[f"mixT {b}"] * j))
            for i in range(4):
                first_update(1, i)
            first_norm(2)
            first_update(2, 0)
            for b in range(0, 4, 2):
                after((ten, f"x 2 transposed {b}"))
                for j in range(2):
                    k = 2 * b + j
                    v.tensor_scalar(hT[:, k, :], bank[b][:, j * SEQ:(j + 1) * SEQ], fold[:, 2, 0, k:k + 1],
                                    fold[:, 2, 1, k:k + 1], ALU.mult, ALU.add)\
                        .then_inc(vec.sem, vec.did(*[f"hT 2 {b}"] * j))
            for i in range(1, 4):
                first_update(2, i)

            def r(i):
                return route[:, i, :].rearrange("p (t e) -> p t e", t=TT)

            def over(m):
                return m.unsqueeze(2).broadcast_to([P, TT, EXPERTS])

            rev = con("rev").unsqueeze(1).broadcast_to([P, TT, EXPERTS])
            m = [stat[:, 96 + 2 * i:98 + 2 * i] for i in range(8)]

            def step(ins, *names):
                ins.then_inc(vec.sem, vec.did(*names))
                hold()

            v.memset(acc, 0.0).then_inc(vec.sem, vec.did())
            v.memset(spread, 0.0).then_inc(vec.sem, vec.did())
            after((ten, "logits"))
            step(v.tensor_copy(route[:, 0, :], bank[4][:, 0:16]))
            src = 0
            for i in range(2):
                step(v.tensor_reduce(m[i], r(src), axis=AX_X, op=ALU.max))
                step(v.tensor_tensor(r(1), r(src), over(m[i]), ALU.is_equal))
                step(v.tensor_tensor(r(1), r(1), rev, ALU.mult))
                step(v.tensor_reduce(m[2], r(1), axis=AX_X, op=ALU.max))
                step(v.tensor_tensor(r(2 + i), rev, over(m[2]), ALU.is_equal))
                if i == 0:
                    step(v.scalar_tensor_tensor(route[:, 4, :], route[:, 2, :], -3e38, route[:, 0, :], ALU.mult, ALU.add))
                    src = 4
            step(v.tensor_tensor(m[3], m[1], m[0], ALU.subtract), "gate exponents")
            after((sca, "gate exponentials"))
            step(v.tensor_scalar(m[5], m[4], 1.0, None, ALU.add))
            step(v.reciprocal(m[6], m[5]))
            step(v.tensor_tensor(m[7], m[4], m[6], ALU.mult))
            step(v.tensor_tensor(r(5), r(2), over(m[6]), ALU.mult))
            step(v.tensor_tensor(r(6), r(3), over(m[7]), ALU.mult))
            step(v.tensor_tensor(gates[:, :, 0:EXPERTS], r(5), r(6), ALU.add))
            step(v.tensor_tensor(r(11), r(2), r(3), ALU.add), "selected")
            for half in range(2):
                v.memset(bank[4 + half][:, :], 0.0).then_inc(vec.sem, vec.did())
            step(v.tensor_scalar(r(7), r(11), -1e6, 1e6, ALU.mult, ALU.add))
            after((ten, "places"))
            spots = bank[3]
            step(v.tensor_tensor(place[:, :, 0:EXPERTS], spots[:, 0:16].rearrange("p (t e) -> p t e", t=TT), r(7), ALU.add))

            def pick_tokens(column, own, sem_of, did):
                v.tensor_copy(now[:, 0, :].unsqueeze(2), place[:, :, column]).then_inc(sem_of, did())
                v.tensor_copy(now[:, 1, :].unsqueeze(2), gates[:, :, column]).then_inc(sem_of, did())
                own()
                v.tensor_scalar(place[:, :, column], place[:, :, column], -float(SLOTS), None, ALU.add).then_inc(sem_of, did())
                for t in range(TT):
                    v.tensor_scalar(pick[:, t, :], con("iota"), now[:, 0, t:t + 1], None, ALU.is_equal)\
                        .then_inc(sem_of, did(*["picked"] * t))
                for t in range(TT):
                    v.tensor_scalar(pickg[:, t, :], con("iota"), now[:, 0, t:t + 1], now[:, 1, t:t + 1],
                                    ALU.is_equal, ALU.mult).then_inc(sem_of, did(*["pickg"] * t))

            pick_tokens(slice(0, 1), hold, vec.sem, vec.did)
            step(v.tensor_reduce(m[0][:, 0:1], spots[:, 16:24], axis=AX_X, op=ALU.max))
            step(v.tensor_scalar(n_passes[:, :], m[0][:, 0:1], float(SLOTS), 1.0, ALU.is_gt, ALU.add), "passes")
            v.tensor_copy(place[:, :, EXPERTS:], place[:, :, 0:1]).then_inc(vec.sem, vec.did())
            v.tensor_copy(gates[:, :, EXPERTS:], gates[:, :, 0:1]).then_inc(vec.sem, vec.did())

            def low_gathered(half):
                return v.tensor_tensor(xg_lo[:, 4 * half:4 * half + 4, :], xm[:, 4 * half:4 * half + 4, :],
                                       xg_hi[:, 4 * half:4 * half + 4, :].bitcast(F32), ALU.subtract)

            def modulate_gathered(k):
                return v.tensor_scalar(xm[:, k, :], bank[6][:, (k - 4) * P:(k - 3) * P], mod[:, 1, 32 + k, 0:1],
                                       mod[:, 1, 24 + k, 0:1], ALU.mult, ALU.add)

            after((ten, "gathered"))
            for k in range(4, KT):
                modulate_gathered(k).then_inc(vec.sem, vec.did(*["xm 1"] * (k == KT - 1)))
            after((sca, "xg high 0"))
            low_gathered(0).then_inc(vec.sem, vec.did("xg 0"))
            after((sca, "xg high 1"))
            low_gathered(1).then_inc(vec.sem, vec.did("xg 1"))
            hold()

            passes = dve.value_load(n_passes[0:1, 0:1], min_val=1, max_val=PASSES_MAX)
            dve.sem_inc(vec_b.sem, vec_b.per)
            with dve.Fori(0, passes) as p:
                with dve.Fori(0, EXPERTS) as e:
                    turn = p * EXPERTS + e

                    def own():
                        dve.wait_ge(vec_b.sem, vec_b.last(turn))

                    def wait_b(who, name):
                        dve.wait_ge(who.sem, who.at(name, turn))

                    def sign_b(ins, *names):
                        ins.then_inc(vec_b.sem, vec_b.did(*names))

                    def low_hidden(i):
                        wait_b(sca_b, f"hidden high {i}")
                        f = 2 * i % KEPT
                        sign_b(v.tensor_tensor(hidE_lo[:, f:f + 2, :],
                                               bank[i % 2][:, 0:256].rearrange("p (j n) -> p j n", j=2),
                                               hidE_hi[:, f:f + 2, :].bitcast(F32), ALU.subtract), f"hid {i}")

                    for n, c in enumerate(MOE_ORDER):
                        before = [MOE_ORDER[n - back] if n >= back else ("d", 0) for back in (1, 2)]
                        for q in range(4):
                            m = (4 * n + q) % Q_MOE
                            wait_b(sca_b, f"high {n} {q}")
                            sign_b(v.tensor_tensor(q_lo[m], slot(n)[:, q * QW:(q + 1) * QW], q_hi[m].bitcast(F32), ALU.subtract),
                                   f"split {n} {q}", *[f"split {n}"] * (q == 3))
                            if before[0][0] == "gu" and q == 2:
                                i = before[0][1]
                                wait_b(sca_b, f"silu {i}")
                                if i >= 2:
                                    wait_b(ten_b, f"transposed {i - 2}")
                                sign_b(v.tensor_tensor(hid_tok[:, i % 2, :], siluE[:, i % 2, :], bank[2 + i % 2][:, 256:512],
                                                       ALU.mult), f"product {i}")
                            if before[1][0] == "gu" and q == 1:
                                low_hidden(before[1][1])
                            if n == 0 and q == 3:
                                wait_b(ten_b, "multiplied 0 0")
                                sign_b(v.tensor_copy(outE[:, 512:D], bank[5][:, :]), "outE")
                            if n in (2, 3) and q == 3:
                                for i in (2 * n - 4, 2 * n - 3):
                                    wait_b(ten_b, f"scattered {i}")
                                    a = acc[:, i // 2, (i % 2) * 512:(i % 2) * 512 + 512]
                                    sign_b(v.tensor_tensor(a, a, bank[6 + i % 2][:, :], ALU.add), f"added {i}")
                            if n == 8 and q == 3:
                                wait_b(ten_b, "spread")
                                pick_tokens(bass.ds(e + 1, 1), own, vec_b.sem, vec_b.did)
                    low_hidden(EFT // 2 - 1)
                    wait_b(ten_b, "gathered 1")
                    for k in range(4, KT):
                        sign_b(modulate_gathered(k), *["xm 1"] * (k == KT - 1))
                    for half in range(2):
                        wait_b(sca_b, f"xg high {half}")
                        sign_b(low_gathered(half), f"xg {half}")

            turns = passes * EXPERTS
            dve.wait_ge(ten_b.sem, ten_b.was("multiplied 20 3", turns))
            dve.wait_ge(vec_b.sem, vec_b.was("xg 1", turns))
            v.tensor_copy(outE[:, 512:D], bank[5][:, :]).then_inc(vec_f.sem, vec_f.did("outE"))

            def add_scattered(t):
                for half in range(2):
                    dve.wait_ge(ten_f.sem, ten_f.at(f"scattered {t} {half}"))
                    a = acc[:, t, half * 512:half * 512 + 512]
                    v.tensor_tensor(a, a, bank[(6, 7, 0, 1)[2 * t + half]][:, :], ALU.add).then_inc(vec_f.sem, vec_f.did())
                dve.wait_ge(vec_f.sem, vec_f.last())

            layer_norm(3, lambda t, half: acc[:, t, half * 512:half * 512 + 512], vec_f,
                       ("power wanted {t}", "power norm {t}", pol_f), add_scattered)
            for t in range(TT):
                for step in range(2):
                    gain_and_bias(3, vec_f, 0, t, step, f"x {t}")

            dve.sem_inc(vec_c.sem, vec_c.per)
            with dve.Fori(0, 2) as l:

                def own():
                    dve.wait_ge(vec_c.sem, vec_c.last(l))

                def wait(who, name):
                    dve.wait_ge(who.sem, who.at(name, l))

                def alone():
                    dve.sem_inc(wait_carrier, 1)

                def did(*names):
                    return vec_c.did(*names)

                S = vec_c.sem
                dve.wait_ge(landed_c[0], layer_landed(0, l))
                dve.wait_ge(sca_c.sem, sca_c.was("y 1 scaled 3", l))
                dve.wait_ge(ten_c.sem, ten_c.was("gated", l))
                first = slot(0)
                v.tensor_copy(par, first[:, PAR_AT:PAR_AT + N_PAR]).then_inc(S, did("par"))
                v.tensor_tensor(wsm, first[:, WS_AT:WS_AT + 4 * P].rearrange("p (h t) -> p h t", h=4),
                                con("tri").unsqueeze(1).broadcast_to([P, 4, P]), ALU.mult).then_inc(S, did())

                def power(name, at, src, scale, eps, w=2):
                    dst = stat[:, 32 + at:32 + at + w]
                    if scale is None:
                        v.tensor_scalar(dst, src, eps, None, ALU.add).then_inc(S, did(f"power {name} wanted"))
                    else:
                        v.tensor_scalar(dst, src, scale, eps, ALU.mult, ALU.add).then_inc(S, did(f"power {name} wanted"))

                def rms_power(name, at, squares):
                    for t in range(TT):
                        wait(sca_c, f"{name} squares {t}")
                        power(f"{name} {t}", at + t, stat[:, squares + t:squares + t + 1], 1.0 / D, RMS_EPS, 1)

                def scaled_out(name, gain):
                    for b in range(0, 4, 2):
                        wait(ten_c, f"{name} transposed {b}")
                        for j in range(2):
                            v.tensor_scalar(hT[:, 2 * b + j, :], bank[b][:, j * SEQ:(j + 1) * SEQ], pr(gain, 2 * b + j), None,
                                            ALU.mult).then_inc(S, did(*[f"{name} hT {b}"] * j))

                rms_power("mix", 0, 16)
                own()
                scaled_out("mix", "gmix")

                def rotate(dst, src, t, heads):
                    s4 = src.rearrange("p (h s f) -> p h s f", h=heads, s=2)
                    d4 = dst.rearrange("p (h s f) -> p h s f", h=heads, s=2)
                    a4 = rt_a[:, 0:heads * HD].rearrange("p (h s f) -> p h s f", h=heads, s=2)
                    a3 = rt_a[:, 0:heads * HD].rearrange("p (g f) -> p g f", f=32)
                    b = [rt_b[:, 256 * i:256 * i + 32 * heads].rearrange("p (h f) -> p h f", h=heads) for i in range(2)]
                    cos, sin = con("dcos", 2, 32)[:, t, :], con("dsin", 2, 32)[:, t, :]
                    v.tensor_tensor(a3, src.rearrange("p (g f) -> p g f", f=32),
                                    cos.unsqueeze(1).broadcast_to([P, 2 * heads, 32]), ALU.mult).then_inc(S, did())
                    for i in range(2):
                        v.tensor_tensor(b[i], s4[:, :, 1 - i, :], sin.unsqueeze(1).broadcast_to([P, heads, 32]), ALU.mult)\
                            .then_inc(S, did())
                    own()
                    v.tensor_tensor(d4[:, :, 0, :], a4[:, :, 0, :], b[0], ALU.subtract).then_inc(S, did())
                    v.tensor_tensor(d4[:, :, 1, :], a4[:, :, 1, :], b[1], ALU.add).then_inc(S, did())
                    own()

                wi = view(stat, 20, TT, 4)
                for t in range(TT):
                    wait(sca_c, f"qi got {t}")
                    v.tensor_scalar(wi[:, t, :], qi_tok[:, t, 320:324], 0.5 * NA_SCALE, None, ALU.mult).then_inc(S, did())
                    rotate(qir[:, t, 0:320], qi_tok[:, t, 0:320], t, 5)
                    v.tensor_copy(qir[:, t, 320:384], qir[:, t, 256:320]).then_inc(S, did(*["qi rope"] * t))
                v.memset(yp[:, :, 0:TAPS_C - 1], 0.0).then_inc(S, did())
                for i in range(2):
                    wait(sca_c, f"sig {i}")
                    v.tensor_tensor(yp[:, i, TAPS_C - 1:], bank[6 + i][:, 0:SEQ], sig[:, i, :], ALU.mult)\
                        .then_inc(S, did(f"yp {i}"))

                def conv_taps(first, end):
                    for tap in range(first, end):
                        for i in range(2):
                            w = pr("wcf", TAPS_C * i + tap)
                            if tap > first:
                                dve.wait_ge(S, vec_c.last_but(1, l))
                            elif i == 0:
                                own()
                            if tap == 0:
                                v.tensor_scalar(conv[:, i, :], yp[:, i, 0:SEQ], w, pr("bcf", i), ALU.mult, ALU.add).then_inc(S, did())
                            else:
                                v.scalar_tensor_tensor(conv[:, i, :], yp[:, i, tap:tap + SEQ], w, conv[:, i, :], ALU.mult, ALU.add)\
                                    .then_inc(S, did(*[f"conv {i}"] * (tap == TAPS_C - 1)))

                conv_taps(0, TAPS_EARLY)
                top = [stat[:, 104:112], stat[:, 112:120]]
                wait(sca_c, "rel 0")
                wait(sca_c, "rel 1")

                def tiles(step):
                    for t in range(TT):
                        dve.wait_ge(S, vec_c.last_but(1, l))
                        step(t, left[:, t, :]).then_inc(S, did())

                own()
                tiles(lambda t, s: v.tensor_scalar(s, rel[:, t, 0, :], wi[:, t, 0:1], None, ALU.mult))
                for i in range(1, 4):
                    tiles(lambda t, s: v.scalar_tensor_tensor(s, rel[:, t, i, :], wi[:, t, i:i + 1], s, ALU.mult, ALU.add))
                tiles(lambda t, s: v.tensor_tensor(s, s, con("causal", 2, SEQ)[:, t, :], ALU.add))
                for _ in range(SEQ // 4 // 8):
                    for t in range(TT):
                        dve.wait_ge(S, vec_c.last_but(1, l))
                        alone()
                        v.max(top[t], left[:, t, :]).then_inc(S, did())
                    for t in range(TT):
                        dve.wait_ge(S, vec_c.last_but(1, l))
                        alone()
                        v.match_replace(out=left[:, t, :], in_to_replace=top[t], in_values=left[:, t, :], imm_value=-3e38)\
                            .then_inc(S, did())
                tiles(lambda t, s: v.tensor_scalar(mask[:, t, :], s, -2e38, NEG, ALU.is_gt, ALU.mult))
                tiles(lambda t, s: v.tensor_tensor(mask[:, t, :], mask[:, t, :], con("causal", 2, SEQ)[:, t, :], ALU.add))
                own()
                for t in range(TT):
                    rotate(qkr[:, t, :], qk_tok[:, t, :], t, 8)
                v.memset(chp[:, :, 0:TAPS_A - 1], 0.0).then_inc(S, did("qk rope"))
                conv_taps(TAPS_EARLY, TAPS_C)
                for i in range(2):
                    wait(sca_c, f"ch got {i}")
                    v.tensor_tensor(chp[:, i, TAPS_A - 1:], ac[:, i, :], ah[:, i, :], ALU.mult).then_inc(S, did())
                wait(sca_c, "vg got 1")
                bn, mv = view(stat, 64, TT, 6), view(stat, 88, TT, 2)
                for t in range(TT):
                    v.bn_stats(bn[:, t, :], vg_tok[:, t, 256:512]).then_inc(S, did())
                own()
                alone()
                for t in range(TT):
                    v.bn_aggr(mv[:, t, :], bn[:, t, :]).then_inc(S, did())
                own()
                power("v", 2, mv[:, :, 1], None, LN_EPS)
                ya = rt_a.rearrange("p (i n) -> p i n", i=2)
                for tap in range(TAPS_A):
                    own()
                    for i in range(2):
                        w = pr("wca", 3 * i + tap)
                        if tap == 0:
                            v.tensor_scalar(ya[:, i, :], chp[:, i, 0:SEQ], w, None, ALU.mult).then_inc(S, did())
                        else:
                            v.scalar_tensor_tensor(ya[:, i, :], chp[:, i, tap:tap + SEQ], w, ya[:, i, :], ALU.mult, ALU.add)\
                                .then_inc(S, did())
                wait(pol_c, "power v")
                for t in range(TT):
                    v.tensor_scalar(vn[:, t, :], vg_tok[:, t, 256:512], mv[:, t, 0:1], stat[:, 42 + t:43 + t],
                                    ALU.subtract, ALU.mult).then_inc(S, did())
                own()
                for name, op in (("gg", ALU.mult), ("gb", ALU.add)):
                    v.tensor_tensor(vn, vn, pr(name, 0, 256).unsqueeze(1).broadcast_to([P, TT, 256]), op)\
                        .then_inc(S, did(*["vn"] * (name == "gb")))
                    own()
                wait(ten_c, "qk transposed")
                v.tensor_copy(kT, bank[1][:, :].rearrange("p (i n) -> p i n", i=2)).then_inc(S, did("kT"))
                for i in range(2):
                    wait(sca_c, f"bu got {i}")
                    v.tensor_tensor(catT[:, i, :], ya[:, i, :], bu[:, i, 0:SEQ], ALU.mult).then_inc(S, did())
                wait(ten_c, "gated")
                for i in range(2):
                    v.tensor_tensor(mixed[:, i, :].rearrange("p (t n) -> p t n", t=TT),
                                    bank[6 + i][:, 0:SEQ].rearrange("p (t n) -> p t n", t=TT),
                                    pr("bs", P * i, P).unsqueeze(1).broadcast_to([P, TT, P]), ALU.add).then_inc(S, did())
                own()
                for i in range(2):
                    v.tensor_tensor(catT[:, 2 + i, :], mixed[:, i, :], bu[:, i, SEQ:2 * SEQ], ALU.mult).then_inc(S, did(f"y_b {i}"))
                def peak_c(u):
                    wait(ten_c, f"scores {u}")
                    if u >= 3:
                        wait(sca_c, f"exp {u - 3}")
                    alone()
                    v.tensor_tensor_reduce(out=ms[:, u % 3, :], in0=bank[u % 3][:, 0:SEQ], in1=mask[:, u % 2, :], scale=1.0,
                                           scalar=-3e38, op0=ALU.add, op1=ALU.max, accum_out=rinv[:, 8 + u:9 + u])\
                        .then_inc(S, did(f"masked {u}"))
                    own()
                    v.tensor_scalar(nmax[:, u:u + 1], rinv[:, 8 + u:9 + u], -1.0, None, ALU.mult).then_inc(S, did(f"nmax {u}"))

                wait(ten_c, "conv transposed")
                for t in range(TT):
                    v.bn_stats(bn[:, t, :], bank[2][:, t * SEQ:(t + 1) * SEQ]).then_inc(S, did())
                own()
                alone()
                for t in range(TT):
                    v.bn_aggr(mv[:, t, :], bn[:, t, :]).then_inc(S, did())
                own()
                power("conf", 4, mv[:, :, 1], None, LN_EPS)
                peak_c(0)
                peak_c(1)
                wait(pol_c, "power conf")
                for t in range(TT):
                    v.tensor_scalar(ynorm[:, t, :], bank[2][:, t * SEQ:(t + 1) * SEQ], mv[:, t, 0:1], stat[:, 44 + t:45 + t],
                                    ALU.subtract, ALU.mult).then_inc(S, did(f"ynorm {t}"))

                def o_c_out(u):
                    wait(sca_c, f"exp {u}")
                    v.reciprocal(rinv[:, u:u + 1], rsum[:, u:u + 1]).then_inc(S, did())
                    wait(ten_c, f"attended {u}")
                    own()
                    v.tensor_scalar(o_c[:, u % 2, (u // 2) * HD:(u // 2 + 1) * HD], bank[6 + u % 2][:, 0:HD], rinv[:, u:u + 1],
                                    None, ALU.mult).then_inc(S, did(f"o {u}"))

                for u in range(8):
                    if u + 2 < 8:
                        peak_c(u + 2)
                    o_c_out(u)
                wait(ten_c, "o transposed")
                v.tensor_copy(catT[:, 4:6, :], bank[0][:, :].rearrange("p (i n) -> p i n", i=2)).then_inc(S, did("y_c"))

                def residual(name):
                    for t in range(TT):
                        wait(ten_c, f"{name.replace('x', 'y')} {t}")
                        for half in range(2):
                            a = x[:, t, half * 512:half * 512 + 512]
                            v.tensor_tensor(a, a, bank[4 + 2 * t + half][:, :], ALU.add)\
                                .then_inc(S, did(*[f"{name} {t}"] * half, *[name] * (t == 1 and half == 1)))

                residual("x 0")
                layer_parts = (ten_c, vec_c, sca_c)
                low_quarter(wait, layer_parts, LAYER_AT, 0, 0)
                rms_power("ffn", 6, 18)
                low_quarter(wait, layer_parts, LAYER_AT, 0, 1)
                input_parts(wait, layer_parts, "y 1", "ffn",
                            lambda dst, src, k: v.tensor_scalar(dst, src, pr("gffn", k), None, ALU.mult))
                feed_forward(wait, layer_parts, LAYER_AT)
                residual("x 1")

            dve.wait_ge(vec_c.sem, vec_c.at("x 1", 1))
            for t in range(TT):
                dve.wait_ge(sca_f.sem, sca_f.at(f"squares {t}"))
                v.tensor_scalar(stat[:, 32 + t:33 + t], stat[:, 16 + t:17 + t], 1.0 / D, RMS_EPS, ALU.mult, ALU.add)\
                    .then_inc(vec_f.sem, vec_f.did(f"power wanted final {t}"))
            dve.wait_ge(gfin_loaded, 16)
            for t in range(TT):
                dve.wait_ge(pol_f.sem, pol_f.at(f"power final {t}"))
                v.scalar_tensor_tensor(tmp[:, t, :], x[:, t, :], stat[:, 40 + t:41 + t], gfin, ALU.mult, ALU.mult)\
                    .then_inc(vec_f.sem, vec_f.did(f"out {t}"))

        @block.scalar
        def _(act):
            a = nc.scalar
            act.dma_start(cols[:, :], cols_d).then_inc(columns_loaded, 16)
            act.dma_start(const[:, :], const_d).then_inc(constants_loaded, 16)

            def after(*whos):
                for who, name in whos:
                    act.wait_ge(who.sem, who.at(name))

            act.wait_ge(columns_loaded, 16)
            a.activation(stat[:, 48:64], cols[:, COLS["c"][0]:COLS["c"][0] + 16], ACT.Silu).then_inc(sca.sem, sca.did("silu c"))

            def copy(dst, src, **kw):
                return a.activation(dst, src, ACT.Copy, **kw)

            for i in range(4):
                after((ten, f"used {FIRST_AT[('mod', 0, i)]}"))
                copy(mod_rows[:, i * 512:(i + 1) * 512], bank[i][0:2, :]).then_inc(sca.sem, sca.did(f"mod rows {i}"))
            after((vec, "mod 0 first"))
            for n, g in enumerate(GROUPS):
                if not by_scalar(n):
                    continue
                after((ten, f"full {g}"))
                b, name = bank[n % 7], f"got {g}"
                if g[0] == "h":
                    k = g[1]
                    for c in range(2):
                        a.activation(hT4[:, k, (1 - c) * SEQ:(2 - c) * SEQ], b[:, (1 - c) * SEQ:(2 - c) * SEQ], ACT.Identity,
                                     scale=mod[:, 0, 8 + k, c:c + 1], bias=mod[:, 0, k, c:c + 1])\
                            .then_inc(sca.sem, sca.did(*[name] * c))
                elif g[0] == "c":
                    t, c0 = g[1], 256 if g[1] < 2 else 0
                    copy(c_tok[:, t, c0:], b[:, c0:416]).then_inc(sca.sem, sca.did(name))
                elif g[0] == "ka":
                    copy(kaT[:, g[1], :], b[:, :]).then_inc(sca.sem, sca.did(name))
                elif g[0] == "qa":
                    copy(qaT[:, 2 * g[1]:2 * g[1] + 2, :], b[:, :].rearrange("p (j n) -> p j n", j=2), scale=NA_SCALE)\
                        .then_inc(sca.sem, sca.did(name))
                else:
                    copy(va[:, g[1], :], b[:, :]).then_inc(sca.sem, sca.did(name))

            def exp(u):
                after((vec, f"nmax {u}"))
                if u >= 3:
                    after((ten, f"probs transposed {u - 3}"))
                a.activation(probs[:, u % 3, :], bank[u % 3][:, :], ACT.Exp, bias=nmax[:, u:u + 1],
                             accum_out=rsum[:, u:u + 1]).then_inc(sca.sem, sca.did(f"exp {u}"))

            def probs_out(u):
                after((ten, f"probs transposed {u}"))
                if u >= 2:
                    after((ten, f"attended {u - 2}"))
                copy(probsT[:, u % 2, :], bank[3 + u % 2][:, :]).then_inc(sca.sem, sca.did(f"probsT {u}"))

            def o_out(u):
                h, t = (u % 16) // 2, u % 2
                after((vec, f"inverse {u}"))
                after((ten, f"attended {u}"))
                at = h * HD + (u // 16) * 512
                copy(o_tok[:, t, at:at + HD], bank[5 + u % 2][:, 0:HD], scale=rinv[:, u:u + 1]).then_inc(sca.sem, sca.did(f"o {u}"))

            def units(first):
                exp(first)
                exp(first + 1)
                probs_out(first)
                for u in range(first, first + 16):
                    if u > first:
                        o_out(u - 1)
                    if u + 1 < first + 16:
                        probs_out(u + 1)
                    if u + 2 < first + 16:
                        exp(u + 2)
                o_out(first + 15)

            units(0)
            after((vec, "krT"))
            copy(kmT[HD:MQ, 0:4, :], krT[HD:MQ, :].unsqueeze(1).broadcast_to([ROPE_D, 4, 2 * SEQ]))\
                .then_inc(sca.sem, sca.did("kmT rope"))
            for n, g in enumerate(UP_GROUPS):
                if not by_scalar(n):
                    continue
                after((ten, f"full {g}"))
                b, name = bank[n % 7], f"got {g}"
                if g[0] == "qup":
                    copy(qm_tok[:, g[1], g[2] * 384:g[2] * 384 + 384], b[:, 0:384], scale=MLA_SCALE).then_inc(sca.sem, sca.did(name))
                elif g[0] == "v":
                    copy(vm[:, g[1], :], b[:, :]).then_inc(sca.sem, sca.did(name))
                elif g[0] == "kn":
                    copy(kmT[0:HD, g[1], :], b[0:HD, :]).then_inc(sca.sem, sca.did(name))
                else:
                    copy(qmT[0:MQ, 2 * g[1]:2 * g[1] + 2, :], b[0:MQ, :].rearrange("p (j n) -> p j n", j=2))\
                        .then_inc(sca.sem, sca.did(name))
            units(16)
            for b in range(1, 4, 2):
                after((ten, f"o transposed {b}"))
                copy(oT[:, 2 * b:2 * b + 2, :], bank[b][:, :].rearrange("p (j n) -> p j n", j=2)).then_inc(sca.sem, sca.did(f"oT {b}"))

            def gate_row_out(n, banks):
                layer, part = n // 2, n % 2
                for k in range(KT):
                    if n or k >= 4:
                        before = f"gate {n} {k - 4}" if k >= 4 else f"gate {n - 1} {k + 4}"
                        after((ten, before))
                    copy(diag[k % 4], ident, scale=mod[:, layer, 16 + 24 * part + k, 0:1])\
                        .then_inc(sca.sem, sca.did(f"diag {n} {k}"))
                for half in range(2):
                    after((ten, f"gate {n} {4 * half + 3}"))
                    copy(gate_row[n % 2][:, half * 512:half * 512 + 512], bank[banks[half]][:, :])\
                        .then_inc(sca.sem, sca.did(*[f"gate row {n}"] * half))

            after((vec, "mod folded"))
            gate_row_out(0, (5, 7))
            after((ten, "y 0"))
            gate_row_out(1, (0, 1))
            def wait_a(who, name):
                act.wait_ge(who.sem, who.at(name))

            def land_a(n):
                act.wait_ge(landed_a[n % RING], 16 * (n // RING + 1))

            def high_quarter(wait, land, parts, at, pos, q):
                ten_p, vec_p, sca_p = parts
                n, m = at[("ffn",) + FFN_ORDER[pos]], 4 * pos + q
                if q == 0:
                    land(n)
                if m >= Q_FFN:
                    old = m - Q_FFN
                    wait(ten_p, f"multiplied {at[('ffn',) + FFN_ORDER[old // 4]]} {old % 4}")
                copy(q_hi[m % Q_FFN], slot(n)[:, q * QW:(q + 1) * QW])\
                    .then_inc(sca_p.sem, sca_p.did(f"high {n} {q}"))

            def input_parts(wait, parts, last_name, source_done, scaled):
                ten_p, vec_p, sca_p = parts
                for b in range(4):
                    if b % 2 == 0:
                        wait(ten_p, f"{source_done} transposed {b + 1}")
                        for j in range(2):
                            scaled(hm[:, 2 * b + 2 + j, :], bank[b + 1][:, j * SEQ:(j + 1) * SEQ], 2 * b + 2 + j)\
                                .then_inc(sca_p.sem, sca_p.did(*[f"{last_name} scaled {b + 1}"] * j))
                        wait(vec_p, f"{last_name} scaled {b}")
                    else:
                        wait(sca_p, f"{last_name} scaled {b}")
                    copy(hT_hi[:, 2 * b:2 * b + 2, :], hm[:, 2 * b:2 * b + 2, :])\
                        .then_inc(sca_p.sem, sca_p.did(f"{last_name} high {b}"))

            def feed_forward(wait, land, parts, at):
                ten_p, vec_p, sca_p = parts
                for pos, c in enumerate(FFN_ORDER):
                    before = FFN_ORDER[pos - 1] if pos else ("d", 0)
                    for q in range(quarters(c, FT)):
                        if 4 * pos + q >= 2:
                            high_quarter(wait, land, parts, at, pos, q)
                        if before[0] == "gu" and q == 2:
                            i = before[1]
                            wait(vec_p, f"product {i}")
                            f = 2 * i % KEPT
                            copy(hid_hi[:, f:f + 2, :], silu[:, i % 2, :].rearrange("p (j n) -> p j n", j=2))\
                                .then_inc(sca_p.sem, sca_p.did(f"hidden high {i}"))
                        if c[0] == "gu" and q == 3:
                            i = c[1]
                            wait(ten_p, f"multiplied {at[('ffn',) + c]} 1")
                            if i >= 2:
                                wait(vec_p, f"hid {i - 2}")
                            a.activation(silu[:, i % 2, :], bank[2 * (i % 2)][:, :], ACT.Silu)\
                                .then_inc(sca_p.sem, sca_p.did(f"silu {i}"))

            first_parts = (ten, vec, sca)
            wait_a(ten, "y 0")
            high_quarter(wait_a, land_a, first_parts, FIRST_AT, 0, 0)
            high_quarter(wait_a, land_a, first_parts, FIRST_AT, 0, 1)
            input_parts(wait_a, first_parts, "y 1", "x 0",
                        lambda dst, src, k: a.activation(dst, src, ACT.Identity, scale=fold[:, 0, 0, k:k + 1],
                                                         bias=fold[:, 0, 1, k:k + 1]))
            feed_forward(wait_a, land_a, first_parts, FIRST_AT)
            gate_row_out(2, (0, 1))
            for b in range(1, 4, 2):
                after((ten, f"means {b}"))
                for j in range(2):
                    k = 2 * b + j
                    copy(mixT[:, k, :], bank[b][:, j * SEQ:(j + 1) * SEQ], scale=fold[:, 1, 0, k:k + 1])\
                        .then_inc(sca.sem, sca.did(*[f"mixT {b}"] * j))
            gate_row_out(3, (0, 1))
            for b in range(1, 4, 2):
                after((ten, f"x 2 transposed {b}"))
                for j in range(2):
                    k = 2 * b + j
                    a.activation(hT[:, k, :], bank[b][:, j * SEQ:(j + 1) * SEQ], ACT.Identity, scale=fold[:, 2, 0, k:k + 1],
                                 bias=fold[:, 2, 1, k:k + 1]).then_inc(sca.sem, sca.did(*[f"hT 2 {b}"] * j))
            after((vec, "gate exponents"))
            a.activation(stat[:, 104:106], stat[:, 102:104], ACT.Exp).then_inc(sca.sem, sca.did("gate exponentials"))

            def modulate_gathered(k):
                return a.activation(xm[:, k, :], bank[0][:, k * P:(k + 1) * P], ACT.Identity, scale=mod[:, 1, 32 + k, 0:1],
                                    bias=mod[:, 1, 24 + k, 0:1])

            def high_gathered(half):
                return copy(xg_hi[:, 4 * half:4 * half + 4, :], xm[:, 4 * half:4 * half + 4, :])

            after((ten, "gathered"))
            for k in range(4):
                modulate_gathered(k).then_inc(sca.sem, sca.did(*["xm 0"] * (k == 3)))
            after((sca, "xm 0"))
            high_gathered(0).then_inc(sca.sem, sca.did("xg high 0"))
            after((vec, "xm 1"))
            high_gathered(1).then_inc(sca.sem, sca.did("xg high 1"))

            after((vec, "xg 1"))
            passes = act.value_load(n_passes[0:1, 0:1], min_val=1, max_val=PASSES_MAX)
            act.sem_inc(sca_b.sem, sca_b.per)
            with act.Fori(0, passes) as p:
                with act.Fori(0, EXPERTS) as e:
                    turn = p * EXPERTS + e

                    def wait_b(who, name):
                        act.wait_ge(who.sem, who.at(name, turn))

                    def sign_b(ins, *names):
                        ins.then_inc(sca_b.sem, sca_b.did(*names))

                    def high_hidden(i):
                        wait_b(ten_b, f"transposed {i}")
                        f = 2 * i % KEPT
                        sign_b(copy(hidE_hi[:, f:f + 2, :], bank[i % 2][:, 0:256].rearrange("p (j n) -> p j n", j=2)),
                               f"hidden high {i}")

                    for n, c in enumerate(MOE_ORDER):
                        before = [MOE_ORDER[n - back] if n >= back else ("d", 0) for back in (1, 2)]
                        for q in range(4):
                            m = 4 * n + q
                            if q == 0:
                                act.wait_ge(landed_b[n % RING], turn * (16 * N_EXPERT // RING) + 16 * (n // RING + 1))
                            old = m - Q_MOE
                            if old >= 0:
                                wait_b(ten_b, f"multiplied {old // 4} {old % 4}")
                            else:
                                old += 4 * N_EXPERT
                                act.wait_ge(ten_b.sem, ten_b.was(f"multiplied {old // 4} {old % 4}", turn))
                            sign_b(copy(q_hi[m % Q_MOE], slot(n)[:, q * QW:(q + 1) * QW]), f"high {n} {q}")
                            if before[0][0] == "gu" and q == 2:
                                i = before[0][1]
                                wait_b(ten_b, f"multiplied {n - 1} 3")
                                if i >= 2:
                                    wait_b(vec_b, f"product {i - 2}")
                                else:
                                    act.wait_ge(vec_b.sem, vec_b.was(f"product {EFT // 2 - 2 + i}", turn))
                                sign_b(a.activation(siluE[:, i % 2, :], bank[2 + i % 2][:, 0:256], ACT.Silu), f"silu {i}")
                            if before[1][0] == "gu" and q == 1:
                                high_hidden(before[1][1])
                            if n == 0 and q == 3:
                                act.wait_ge(vec_b.sem, vec_b.was("xg 1", turn))
                                sign_b(copy(outE[:, 0:512], bank[4][:, :]), "outE")
                            if n == 4 and q == 3:
                                wait_b(ten_b, "spread")
                                sign_b(copy(spread, bank[7][:, 0:SEQ]), "spread")
                    wait_b(ten_b, "gathered 0")
                    for k in range(4):
                        sign_b(modulate_gathered(k), *["xm 0"] * (k == 3))
                    high_hidden(EFT // 2 - 1)
                    wait_b(sca_b, "xm 0")
                    sign_b(high_gathered(0), "xg high 0")
                    wait_b(vec_b, "xm 1")
                    sign_b(high_gathered(1), "xg high 1")
            turns = passes * EXPERTS
            act.wait_ge(ten_b.sem, ten_b.was("multiplied 20 3", turns))
            act.wait_ge(vec_b.sem, vec_b.was("xg 1", turns))
            copy(outE[:, 0:512], bank[4][:, :]).then_inc(sca_f.sem, sca_f.did("outE"))
            for i in range(2 * KT):
                if i >= 4:
                    after((ten_f, f"row {i - 4}"))
                c, k = divmod(i, KT)
                at = COLS[("lng", "lnb")[c]][0] + 3 * KT + k
                copy(diag[i % 4], ident, scale=cols[:, at:at + 1]).then_inc(sca_f.sem, sca_f.did(f"diag {i}"))
                if i >= 4 and i % 4 == 0:
                    after((ten_f, f"row {i - 1}"))
                    copy(R[:, (i // 4 - 1) * 512:(i // 4) * 512], bank[1 + i // 4][:, :]).then_inc(sca_f.sem, sca_f.did())
            after((ten_f, f"row {2 * KT - 1}"))
            copy(R[:, 1536:2048], bank[5][:, :]).then_inc(sca_f.sem, sca_f.did("rows"))

            act.sem_inc(sca_c.sem, sca_c.per)
            act.wait_ge(vec_f.sem, vec_f.at("x 1"))
            with act.Fori(0, 2) as l:
                S = sca_c.sem

                def wait(who, name):
                    act.wait_ge(who.sem, who.at(name, l))

                def did(*names):
                    return sca_c.did(*names)

                def scale_x(name, at, power):
                    for t in range(TT):
                        if name == "ffn":
                            wait(vec_c, f"x 0 {t}")
                        else:
                            act.wait_ge(vec_c.sem, vec_c.was(f"x 1 {t}", l))
                        a.activation(junk, x[:, t, :], ACT.Square, accum_out=stat[:, at + t:at + t + 1])\
                            .then_inc(S, did(f"{name} squares {t}"))
                        act.wait_ge(S, sca_c.last(l))
                    for t in range(TT):
                        wait(pol_c, f"power {name} {t}")
                        a.activation(tmp[:, t, :], x[:, t, :], ACT.Copy, scale=stat[:, power + t:power + t + 1])\
                            .then_inc(S, did(f"{name} scaled {t}"))

                def scaled_out(name, gain):
                    for b in range(1, 4, 2):
                        wait(ten_c, f"{name} transposed {b}")
                        for j in range(2):
                            a.activation(hT[:, 2 * b + j, :], bank[b][:, j * SEQ:(j + 1) * SEQ], ACT.Copy,
                                         scale=pr(gain, 2 * b + j)).then_inc(S, did(*[f"{name} hT {b}"] * j))

                scale_x("mix", 16, 40)
                wait(vec_c, "par")
                scaled_out("mix", "gmix")
                for t in range(TT):
                    wait(ten_c, f"qi {t}")
                    copy(qi_tok[:, t, :], bank[4 + t][:, 0:QI_W]).then_inc(S, did(f"qi got {t}"))
                for i in range(2):
                    wait(ten_c, f"dd {i}")
                    a.activation(sig[:, i, :], bank[6 + i][:, SEQ:2 * SEQ], ACT.Sigmoid).then_inc(S, did(f"sig {i}"))
                wait(ten_c, "qi transposed")
                copy(qiT, bank[0][:, :].rearrange("p (i n) -> p i n", i=2)).then_inc(S, did())
                copy(kiT, bank[1][:, 0:SEQ]).then_inc(S, did("qiT"))
                for t in range(TT):
                    wait(ten_c, f"qk {t}")
                    copy(qk_tok[:, t, :], bank[4 + t][:, :]).then_inc(S, did(f"qk got {t}"))
                for t in range(TT):
                    wait(ten_c, f"index scores {t}")
                    for i in range(2):
                        a.activation(rel[:, t, i:4:2, :], bank[2 + i - 2 * t][:, :].rearrange("p (i n) -> p i n", i=2), ACT.Relu)\
                            .then_inc(S, did(*[f"rel {t}"] * i))
                for t in range(TT):
                    wait(ten_c, f"vg {t}")
                    copy(vg_tok[:, t, :], bank[6 + t][:, :]).then_inc(S, did(f"vg got {t}"))
                for i in range(2):
                    wait(ten_c, f"ch {i}")
                    copy(ac[:, i, :], bank[2 + i][:, 0:SEQ]).then_inc(S, did())
                    copy(ah[:, i, :], bank[2 + i][:, SEQ:2 * SEQ]).then_inc(S, did(f"ch got {i}"))
                for i in range(2):
                    wait(ten_c, f"bu {i}")
                    copy(bu[:, i, :], bank[4 + i][:, :]).then_inc(S, did(f"bu got {i}"))
                wait(ten_c, "qk transposed")
                copy(qT, bank[0][:, :].rearrange("p (i n) -> p i n", i=2), scale=NA_SCALE).then_inc(S, did("qT"))

                def exp_c(u):
                    wait(vec_c, f"nmax {u}")
                    if u >= 3:
                        wait(ten_c, f"probs transposed {u - 3}")
                    a.activation(probs2[:, u % 3, :], ms[:, u % 3, :], ACT.Exp, bias=nmax[:, u:u + 1],
                                 accum_out=rsum[:, u:u + 1]).then_inc(S, did(f"exp {u}"))

                def probs_out_c(u):
                    wait(ten_c, f"probs transposed {u}")
                    if u >= 2:
                        wait(ten_c, f"attended {u - 2}")
                    copy(probsT2[:, u % 2, :], bank[4 + u % 2][:, 0:SEQ]).then_inc(S, did(f"probsT {u}"))

                exp_c(0)
                exp_c(1)
                probs_out_c(0)
                for u in range(8):
                    if u + 1 < 8:
                        probs_out_c(u + 1)
                    if u + 2 < 8:
                        exp_c(u + 2)
                wait(ten_c, "ynorm transposed")
                for i in range(2):
                    a.activation(catT[:, 6 + i, :], bank[3][:, i * SEQ:(i + 1) * SEQ], ACT.Silu, scale=pr("clg", i),
                                 bias=pr("clb", i)).then_inc(S, did(f"y_d {i}"))

                def land_c(n):
                    act.wait_ge(landed_c[n % RING], layer_landed(n, l))

                layer_parts = (ten_c, vec_c, sca_c)
                wait(vec_c, "y_c")
                high_quarter(wait, land_c, layer_parts, LAYER_AT, 0, 0)
                high_quarter(wait, land_c, layer_parts, LAYER_AT, 0, 1)
                scale_x("ffn", 18, 46)
                input_parts(wait, layer_parts, "y 1", "ffn",
                            lambda dst, src, k: a.activation(dst, src, ACT.Copy, scale=pr("gffn", k)))
                feed_forward(wait, land_c, layer_parts, LAYER_AT)
            for t in range(TT):
                act.wait_ge(vec_c.sem, vec_c.at(f"x 1 {t}", 1))
                a.activation(junk, x[:, t, :], ACT.Square, accum_out=stat[:, 16 + t:17 + t])\
                    .then_inc(sca_f.sem, sca_f.did(f"squares {t}"))
                act.wait_ge(sca_f.sem, sca_f.last())


def host_constants():
    f = np.float32
    c = np.zeros((P, N_CONST), f)

    def put(name, a):
        at, w = CONST[name]
        c[:, at:at + w] = np.asarray(a, f).reshape(P, w)

    i = np.arange(P)
    put("ident", np.eye(P))
    put("ones", np.ones((P, P)))
    put("before", i[:, None] < i[None, :])
    put("tri", i[:, None] <= i[None, :])
    put("iota", np.broadcast_to(i, (P, P)))
    tok = (np.arange(TT)[None, :] * P + i[:, None])
    put("causal", np.where(np.arange(SEQ)[None, None, :] <= tok[:, :, None], 0.0, NEG))
    inv = (1.0 / (np.float32(10000.0) ** (np.arange(8, dtype=f) / f(8)))).astype(f)
    ang = np.stack([(tok // 64).astype(f)[:, :, None] * inv, (tok % 64).astype(f)[:, :, None] * inv], 2).astype(f)
    put("mcos", np.stack([np.cos(ang)] * 2, 3))
    put("msin", np.sin(ang))
    inv = (np.float32(10000.0) ** (-np.arange(0, HD, 2, dtype=f) / f(HD))).astype(f)
    ang = (tok.astype(f)[:, :, None] * inv).astype(f)
    put("dcos", np.cos(ang))
    put("dsin", np.sin(ang))
    put("rev", np.broadcast_to(np.arange(8, 0, -1), (P, 8)))
    put("neghalf", np.full((P, 8), -0.5))
    t = np.arange(SEQ)
    means = np.zeros((len(WINDOWS), SEQ, SEQ), f)
    for g, w in enumerate(WINDOWS):
        lo, hi = np.clip(t - w // 2, 0, SEQ), np.clip(t + w // 2, 0, SEQ)
        inside = (t[:, None] >= lo[None, :]) & (t[:, None] < hi[None, :])
        means[g] = inside / (hi - lo).astype(f) - np.eye(SEQ, dtype=f)
    return c, means.reshape(len(WINDOWS), TT, P, SEQ).transpose(2, 0, 1, 3)


def by_rows(w):
    return w.reshape(-1, P, w.shape[1]).transpose(1, 0, 2)


def column(a):
    return np.asarray(a).reshape(-1, P).T


def ffn_chunks(order, wg, wu, wd, by_tiles):
    g, u, d = by_rows(wg), by_rows(wu), by_rows(wd)
    for kind, i in order:
        if kind == "gu":
            both = np.stack([g[:, :, 256 * i:256 * i + 256], u[:, :, 256 * i:256 * i + 256]], 2)
            yield both.reshape(P, KT, 4, P).transpose(0, 2, 1, 3) if by_tiles else both
        else:
            yield d[:, 4 * i:4 * i + 4]


def host_layout(a, means):
    chunks = np.zeros((N_CHUNKS, P, CW), np.float32)
    count = [0]

    def push(*parts):
        at = 0
        for part in parts:
            part = np.asarray(part).reshape(P, -1)
            chunks[count[0], :, at:at + part.shape[1]] = part
            at += part.shape[1]
        count[0] += 1

    w_in = by_rows(a["attn_w_in"][0])
    w_out = by_rows(a["attn_w_out"][0])
    proj = {"qa": slice(0, 512), "ka": slice(512, 1024), "va": slice(1024, 1536), "c": slice(1536, NC_COLS)}
    ffn = ffn_chunks(FFN_ORDER, a["ffn_w_gate"][0], a["ffn_w_up"][0], a["ffn_w_down"][0], True)
    for c in FIRST_ORDER:
        if c[0] == "mod":
            push(by_rows(a["mod_w"][c[1]][:, 512 * c[2]:512 * c[2] + 512]))
        elif c[0] == "proj":
            w = w_in[:, :, proj[c[1]]]
            push(np.pad(w, ((0, 0), (0, 0), (0, 512 - w.shape[2]))))
        elif c[0] == "up":
            push(by_rows(a["mla_w_q_up"][0]), a["mla_w_kv_up"][0])
        elif c[0] == "out":
            push(w_out[:, :, 512 * c[1]:512 * c[1] + 512])
        elif c[0] == "ffn":
            push(next(ffn))
        else:
            push(a["pool_w"][0].reshape(4, 2, P, 256).transpose(2, 0, 1, 3), means)
    for e in range(EXPERTS):
        for part in ffn_chunks(MOE_ORDER, a["moe_w_gate"][0, e], a["moe_w_up"][0, e], a["moe_w_down"][0, e], False):
            push(part)
    for l in range(2):
        w = by_rows(a["w_in_2"][l])
        w_out = by_rows(a["w_out_2"][l])
        ffn = ffn_chunks(FFN_ORDER, a["w_gate_2"][l], a["w_up_2"][l], a["w_down_2"][l], True)
        spread = lambda v: np.broadcast_to(np.asarray(v).reshape(1, -1), (P, 256))
        taps = lambda v: np.asarray(v).T.reshape(2, P, -1).transpose(1, 0, 2)
        b_s = np.repeat(a["b_s_2"][l].reshape(2, 2, 1, P), HD, axis=2).reshape(2, P, P).transpose(1, 0, 2)
        mix = {
            "qi": (w[:, :, 2048:2048 + QI_W], a["w_s_2"][l].transpose(2, 0, 1), column(a["g_mix_2"][l]), column(a["g_ffn_2"][l]),
                   taps(a["w_conv_a_2"][l]), taps(a["w_conf_2"][l]), column(a["b_conf_2"][l]), column(a["conf_ln_g_2"][l]),
                   column(a["conf_ln_b_2"][l]), spread(a["gmlp_ln_g_2"][l]), spread(a["gmlp_ln_b_2"][l]), b_s),
            "dd": (w[:, :, 2372:2884],),
            "qk": (w[:, :, 1280:1792],),
            "vg": (np.concatenate([w[:, :, 1792:2048], w[:, :, 1024:1280]], 2),),
            "ch": (w[:, :, 256:768],),
            "bu": (np.concatenate([w[:, :, 0:256], w[:, :, 768:1024]], 2),),
        }
        for c in LAYER_ORDER:
            if c[0] == "mix":
                push(*mix[c[1]])
            elif c[0] == "out":
                push(w_out[:, :, 512 * c[1]:512 * c[1] + 512])
            else:
                push(next(ffn))
    assert count[0] == N_CHUNKS

    cols = np.zeros((P, N_COLS), np.float32)

    def put(name, v):
        at, w = COLS[name]
        cols[:, at:at + w] = np.asarray(v).reshape(P, w)

    put("modb0", column(a["mod_b"][0]))
    put("modb1", column(a["mod_b"][1]))
    put("c", np.stack([column(a["c"][0]), column(a["c_ctx"])], 2))
    put("qn", column(a["mla_q_norm"][0]))
    put("kvn", column(a["mla_kv_norm"][0]))
    put("pscale", column(a["pool_scale"][0]))
    norms = [(f"ln{i % 2 + 1}", i // 2) for i in range(4)]
    put("lng", np.concatenate([column(a[name + "_g"][layer]) for name, layer in norms], 1))
    put("lnb", np.concatenate([column(a[name + "_b"][layer]) for name, layer in norms], 1))
    put("router", by_rows(a["moe_router"][0]))

    rb = a["na_rel_bias"][0]
    pos = np.arange(SEQ)
    row, colm = pos // 64, pos % 64
    start = np.clip(colm - 8, 0, 64 - 16)
    near = (colm[None, :] >= start[:, None]) & (colm[None, :] < start[:, None] + 16)
    drow = row[None, :] - row[:, None] + 7
    dcol = np.where(near, colm[None, :] - colm[:, None] + 15, 0)
    bias = np.where(near[None], rb[:, drow, dcol], np.float32(NEG)).astype(np.float32)
    bias = bias.reshape(HEADS, TT, P, SEQ).transpose(2, 1, 0, 3)
    rows = np.stack([np.concatenate([a[f"ln{i % 2 + 1}_g"][i // 2], a[f"ln{i % 2 + 1}_b"][i // 2]]) for i in range(3)])
    rows = np.broadcast_to(rows[:, None, :], (3, P, 2 * D))
    gfin = np.broadcast_to(a["g_final_2"][None, :], (P, D))
    tokens = lambda v: v.reshape(TT, P, D).transpose(1, 0, 2)
    return chunks, tokens(a["x"][0]), tokens(a["ctx"][0]), cols, bias, rows, gfin


def kernel(**inputs):
    from concourse import bacc
    from concourse.bass_utils import run_bass_kernel_spmd

    arrays = {name: np.asarray(value) for name, value in inputs.items()}
    const, means = host_constants()
    chunks, x, ctx, cols, bias, rows, gfin = host_layout(arrays, means)
    sent = {"chunks": chunks, "x_in": x, "ctx_in": ctx, "cols_in": cols, "const_in": const, "bias_in": bias,
            "rows_in": rows, "gfin_in": gfin}
    sent = {name: np.ascontiguousarray(value) for name, value in sent.items()}

    def program(books):
        nc = bacc.Bacc("TRN2", target_bir_lowering=False, num_devices=1)
        ins = [nc.dram_tensor(name, value.shape, F32, kind="ExternalInput").ap() for name, value in sent.items()]
        out = nc.dram_tensor("out", (SEQ, D), F32, kind="ExternalOutput").ap()
        build(nc, ins, out, books)
        return nc

    books = {}
    program(books)
    for book in books.values():
        book["complete"] = True
    nc = program(books)
    result = run_bass_kernel_spmd(nc, [sent], core_ids=[0])
    return result.results[0]["out"].reshape(1, SEQ, D)
```
